# Optimizing a Trainium2 kernel written in Bass

```python
import numpy as np
import jax, jax.numpy as jnp
from jax import lax
import math

D_MODEL = 1024
BATCH = 1
SEQ = 256
DEPTH = 2

D_MIX = D_MODEL
D_FF = 2816
NSA_HEADS = 8
NSA_KV_GROUPS = 2
NSA_HEAD_DIM = 64
NSA_GROUP_SIZE = NSA_HEADS // NSA_KV_GROUPS
NSA_OUT = NSA_HEADS * NSA_HEAD_DIM
NSA_KV_DIM = NSA_KV_GROUPS * NSA_HEAD_DIM
CMP_BLOCK = 32
CMP_STRIDE = 16
SLC_BLOCK = 64
SLC_TOPK = 8
WINDOW = 512
Q_BLOCK = 128
POOL_WINDOWS = (2, 4, 8, 16)
POOL_GROUPS = 4
POOL_GROUP_DIM = 64
POOL_DIM = POOL_GROUPS * POOL_GROUP_DIM
GLA_HEADS = 4
GLA_KEY_DIM = 32
GLA_VAL_DIM = 64
GLA_GATE_RANK = 16
GLA_TAU = 16.0
GLA_CHUNK = 64
GLA_QK = GLA_HEADS * GLA_KEY_DIM
GLA_OUT = GLA_HEADS * GLA_VAL_DIM
IN_SPLITS = (NSA_OUT, NSA_KV_DIM, NSA_KV_DIM, NSA_KV_DIM, NSA_KV_DIM, NSA_KV_DIM, NSA_KV_DIM,
             3 * NSA_HEADS, POOL_DIM, GLA_QK, GLA_QK, GLA_OUT, GLA_GATE_RANK, GLA_OUT)
D_IN = NSA_OUT + 6 * NSA_KV_DIM + 3 * NSA_HEADS + POOL_DIM + 2 * GLA_QK + 2 * GLA_OUT + GLA_GATE_RANK
ALPHA = (2.0 * DEPTH) ** 0.25
BETA = (8.0 * DEPTH) ** -0.25
LN_EPS = 1e-5
RMS_EPS = 1e-6


def layer_norm(x, g, b):
    xf = x.astype(jnp.float32)
    mu = jnp.mean(xf, axis=-1, keepdims=True)
    var = jnp.mean(jnp.square(xf - mu), axis=-1, keepdims=True)
    y = (xf - mu) * lax.rsqrt(var + LN_EPS)
    return (y * g + b).astype(x.dtype)

def swiglu(x, wg, wu, wd):
    return (jax.nn.silu(x @ wg) * (x @ wu)) @ wd

def masked_softmax(s, mask):
    s = jnp.where(mask, s.astype(jnp.float32), -jnp.inf)
    m = jnp.max(s, axis=-1, keepdims=True)
    m = jnp.where(jnp.isfinite(m), m, 0.0)
    e = jnp.exp(s - m)
    d = jnp.sum(e, axis=-1, keepdims=True)
    return e / jnp.where(d > 0, d, 1.0)

def compress_tokens(z, pe, w1, w2):
    B, S, G, D = z.shape
    chunks = z.reshape(B, S // CMP_STRIDE, CMP_STRIDE, G, D)
    blocks = jnp.concatenate([chunks[:, :-1], chunks[:, 1:]], axis=2)
    blocks = blocks + pe[None, None, :, None, :]
    flat = jnp.transpose(blocks, (0, 1, 3, 2, 4)).reshape(B, -1, G, CMP_BLOCK * D)
    return jax.nn.gelu(flat @ w1) @ w2

def nsa_mixer(q, kc_raw, vc_raw, ks, vs, kw, vw, gates, pe_k, w1_k, w2_k, pe_v, w1_v, w2_v):
    B, S = q.shape[:2]
    G, R, HD = NSA_KV_GROUPS, NSA_GROUP_SIZE, NSA_HEAD_DIM
    q = q.reshape(B, S, G, R, HD) * (HD ** -0.5)
    kc = compress_tokens(kc_raw, pe_k, w1_k, w2_k)
    vc = compress_tokens(vc_raw, pe_v, w1_v, w2_v)
    n_cmp = kc.shape[1]
    cmp_end = jnp.arange(n_cmp) * CMP_STRIDE + CMP_BLOCK - 1
    n_slc = S // SLC_BLOCK
    topk = min(SLC_TOPK, n_slc)
    c_start = jnp.arange(n_cmp)[:, None] * CMP_STRIDE
    s_start = jnp.arange(n_slc)[None, :] * SLC_BLOCK
    overlap = ((c_start <= s_start + SLC_BLOCK - 1) & (c_start + CMP_BLOCK - 1 >= s_start)).astype(jnp.float32)
    ks_blk = jnp.transpose(ks.reshape(B, n_slc, SLC_BLOCK, G, HD), (0, 3, 1, 2, 4))
    vs_blk = jnp.transpose(vs.reshape(B, n_slc, SLC_BLOCK, G, HD), (0, 3, 1, 2, 4))
    pad = ((0, 0), (WINDOW, 0), (0, 0), (0, 0))
    kw_pad = jnp.pad(kw, pad)
    vw_pad = jnp.pad(vw, pad)
    n_qb = S // Q_BLOCK
    q_blocks = jnp.swapaxes(q.reshape(B, n_qb, Q_BLOCK, G, R, HD), 0, 1)
    g_blocks = jnp.swapaxes(gates.reshape(B, n_qb, Q_BLOCK, G, R, 3), 0, 1)
    blk_ids = jnp.arange(n_slc)
    gather = jax.vmap(jax.vmap(lambda kb, ix: kb[ix]))

    def one_block(args):
        qi, qb, gb = args
        t = qi * Q_BLOCK + jnp.arange(Q_BLOCK)
        s_c = jnp.einsum('bqgrd,bngd->bgrqn', qb, kc)
        p_c = masked_softmax(s_c, cmp_end[None, :] <= t[:, None])
        o_c = jnp.einsum('bgrqn,bngd->bqgrd', p_c.astype(vc.dtype), vc)
        imp = jnp.einsum('bgrqn,nm->bgqm', p_c, overlap)
        cur = (t // SLC_BLOCK)[:, None]
        forced = (blk_ids == 0) | (blk_ids == cur) | (blk_ids == cur - 1)
        future = blk_ids[None, :] * SLC_BLOCK > t[:, None]
        imp = jnp.where(forced, jnp.inf, jnp.where(future, -jnp.inf, imp))
        _, sel = lax.top_k(imp, topk)
        k_sel = gather(ks_blk, sel).reshape(B, G, Q_BLOCK, topk * SLC_BLOCK, HD)
        v_sel = gather(vs_blk, sel).reshape(B, G, Q_BLOCK, topk * SLC_BLOCK, HD)
        kpos = (sel[..., None] * SLC_BLOCK + jnp.arange(SLC_BLOCK)).reshape(B, G, Q_BLOCK, topk * SLC_BLOCK)
        s_s = jnp.einsum('bqgrd,bgqkd->bgrqk', qb, k_sel)
        p_s = masked_softmax(s_s, (kpos <= t[:, None])[:, :, None])
        o_s = jnp.einsum('bgrqk,bgqkd->bqgrd', p_s.astype(v_sel.dtype), v_sel)
        start = qi * Q_BLOCK
        k_win = lax.dynamic_slice_in_dim(kw_pad, start, Q_BLOCK + WINDOW, axis=1)
        v_win = lax.dynamic_slice_in_dim(vw_pad, start, Q_BLOCK + WINDOW, axis=1)
        kp = start - WINDOW + jnp.arange(Q_BLOCK + WINDOW)
        mask_w = (kp[None, :] <= t[:, None]) & (kp[None, :] > t[:, None] - WINDOW) & (kp[None, :] >= 0)
        s_w = jnp.einsum('bqgrd,bkgd->bgrqk', qb, k_win)
        p_w = masked_softmax(s_w, mask_w)
        o_w = jnp.einsum('bgrqk,bkgd->bqgrd', p_w.astype(v_win.dtype), v_win)
        o = gb[..., 0:1] * o_c + gb[..., 1:2] * o_s + gb[..., 2:3] * o_w
        return o.reshape(B, Q_BLOCK, G * R * HD)

    out = lax.map(one_block, (jnp.arange(n_qb), q_blocks, g_blocks))
    return jnp.swapaxes(out, 0, 1).reshape(B, S, NSA_OUT)

def pool_mixer(u, pool_w, pool_scale):
    B, S, _ = u.shape
    uf = u.astype(jnp.float32).reshape(B, S, POOL_GROUPS, POOL_GROUP_DIM)
    c = jnp.pad(jnp.cumsum(uf, axis=1), ((0, 0), (1, 0), (0, 0), (0, 0)))
    t = jnp.arange(S)
    means = []
    for gi, w in enumerate(POOL_WINDOWS):
        cg = c[:, :, gi]
        lower = jnp.pad(cg, ((0, 0), (w, 0), (0, 0)))[:, 1:S + 1]
        cnt = jnp.minimum(w, t + 1).astype(jnp.float32)[None, :, None]
        means.append((cg[:, 1:] - lower) / cnt)
    pooled = (jnp.stack(means, axis=2) - uf).astype(u.dtype)
    y = jnp.einsum('bsgc,gcd->bsgd', pooled, pool_w).reshape(B, S, POOL_DIM)
    return y * pool_scale

def gla_mixer(q, k, v, a_lr, r, wa2, ba, norm_g):
    B, S = q.shape[:2]
    H, DK, DV, C = GLA_HEADS, GLA_KEY_DIM, GLA_VAL_DIM, GLA_CHUNK
    nc = S // C
    log_a = jax.nn.log_sigmoid((a_lr @ wa2 + ba).astype(jnp.float32)) / GLA_TAU
    qf = q.astype(jnp.float32).reshape(B, nc, C, H, DK) * (DK ** -0.5)
    kf = k.astype(jnp.float32).reshape(B, nc, C, H, DK)
    vf = v.astype(jnp.float32).reshape(B, nc, C, H, DV)
    b = jnp.cumsum(log_a.reshape(B, nc, C, H, DK), axis=2)
    b_last = b[:, :, -1:]
    q_t = qf * jnp.exp(b)
    k_t = kf * jnp.exp(-b)
    causal = jnp.tril(jnp.ones((C, C), dtype=bool))
    A = jnp.where(causal, jnp.einsum('bnihk,bnjhk->bnhij', q_t, k_t), 0.0)
    o_intra = jnp.einsum('bnhij,bnjhv->bnihv', A, vf)
    dS = jnp.einsum('bnjhk,bnjhv->nbhkv', kf * jnp.exp(b_last - b), vf)
    decay = jnp.swapaxes(jnp.exp(b_last[:, :, 0]), 0, 1)

    def step(state, inp):
        d, ds = inp
        return d[..., None] * state + ds, state

    _, s_in = lax.scan(step, jnp.zeros((B, H, DK, DV), jnp.float32), (decay, dS))
    o_inter = jnp.einsum('bnihk,nbhkv->bnihv', q_t, s_in)
    o = (o_intra + o_inter).reshape(B, S, H, DV)
    o = o * lax.rsqrt(jnp.mean(jnp.square(o), axis=-1, keepdims=True) + RMS_EPS)
    o = o.reshape(B, S, GLA_OUT) * norm_g
    return (o * jax.nn.silu(r.astype(jnp.float32))).astype(q.dtype)

def token_mix(x, w_in, w_out, cmp_pe, cmp_w1, cmp_w2, pool_w, pool_scale, gla_wa2, gla_ba, gla_norm_g):
    B, S, _ = x.shape
    h = x @ w_in
    split_pts = np.cumsum(IN_SPLITS)[:-1].tolist()
    (nq, kc, vc, ks, vs, kw, vw, gl, u, gq, gk, gv, ga, gr) = jnp.split(h, split_pts, axis=-1)
    kv = lambda z: z.reshape(B, S, NSA_KV_GROUPS, NSA_HEAD_DIM)
    gates = jax.nn.sigmoid(gl).reshape(B, S, NSA_HEADS, 3)
    o_a = nsa_mixer(nq, kv(kc), kv(vc), kv(ks), kv(vs), kv(kw), kv(vw), gates,
                    cmp_pe[0], cmp_w1[0], cmp_w2[0], cmp_pe[1], cmp_w1[1], cmp_w2[1])
    o_b = pool_mixer(u, pool_w, pool_scale)
    o_c = gla_mixer(gq, gk, gv, ga, gr, gla_wa2, gla_ba, gla_norm_g)
    return jnp.concatenate([o_a, o_b, o_c], axis=-1) @ w_out

def first_inputs(seed: int = 0) -> dict:
    key = jax.random.key(seed)
    ks = jax.random.split(key, 16)
    nrm = lambda k, shape, s: jax.random.normal(k, shape, jnp.float32) * s
    L = DEPTH
    return {
        "x": nrm(ks[0], (BATCH, SEQ, D_MODEL), 1.0),
        "ln_g": 1.0 + nrm(ks[1], (L, 3, D_MODEL), 0.05),
        "ln_b": nrm(ks[2], (L, 3, D_MODEL), 0.01),
        "ffn_wg": nrm(ks[3], (L, 2, D_MODEL, D_FF), D_MODEL ** -0.5),
        "ffn_wu": nrm(ks[4], (L, 2, D_MODEL, D_FF), D_MODEL ** -0.5),
        "ffn_wd": nrm(ks[5], (L, 2, D_FF, D_MODEL), BETA * D_FF ** -0.5),
        "w_in": nrm(ks[6], (L, D_MODEL, D_IN), D_MODEL ** -0.5),
        "w_out": nrm(ks[7], (L, D_MIX, D_MODEL), BETA * D_MIX ** -0.5),
        "cmp_pe": nrm(ks[8], (L, 2, CMP_BLOCK, NSA_HEAD_DIM), 0.1),
        "cmp_w1": nrm(ks[9], (L, 2, CMP_BLOCK * NSA_HEAD_DIM, NSA_HEAD_DIM), (CMP_BLOCK * NSA_HEAD_DIM) ** -0.5),
        "cmp_w2": nrm(ks[10], (L, 2, NSA_HEAD_DIM, NSA_HEAD_DIM), NSA_HEAD_DIM ** -0.5),
        "pool_w": nrm(ks[11], (L, POOL_GROUPS, POOL_GROUP_DIM, POOL_GROUP_DIM), POOL_GROUP_DIM ** -0.5),
        "pool_scale": 1.0 + nrm(ks[12], (L, POOL_DIM), 0.1),
        "gla_wa2": nrm(ks[13], (L, GLA_GATE_RANK, GLA_QK), GLA_GATE_RANK ** -0.5),
        "gla_ba": nrm(ks[14], (L, GLA_QK), 0.1),
        "gla_norm_g": 1.0 + nrm(ks[15], (L, GLA_OUT), 0.05),
    }

def first_block(x, ln_g, ln_b, ffn_wg, ffn_wu, ffn_wd, w_in, w_out, cmp_pe, cmp_w1, cmp_w2,
              pool_w, pool_scale, gla_wa2, gla_ba, gla_norm_g):
    for l in range(DEPTH):
        x = layer_norm(ALPHA * x + 0.5 * swiglu(x, ffn_wg[l, 0], ffn_wu[l, 0], ffn_wd[l, 0]), ln_g[l, 0], ln_b[l, 0])
        m = token_mix(x, w_in[l], w_out[l], cmp_pe[l], cmp_w1[l], cmp_w2[l], pool_w[l], pool_scale[l],
                      gla_wa2[l], gla_ba[l], gla_norm_g[l])
        x = layer_norm(ALPHA * x + m, ln_g[l, 1], ln_b[l, 1])
        x = layer_norm(ALPHA * x + 0.5 * swiglu(x, ffn_wg[l, 1], ffn_wu[l, 1], ffn_wd[l, 1]), ln_g[l, 2], ln_b[l, 2])
    return x


DEPTH_2 = 4

CHUNK = 64
N_MIXERS = 3
D_FF_2 = 4 * D_MODEL
NORM_EPS = 1e-6
GDN_HEADS = 8
GDN_DK = D_MODEL // GDN_HEADS
GDN_DV = D_MODEL // GDN_HEADS
GDN_CONV = 4
GDN_QKV = GDN_HEADS * (2 * GDN_DK + GDN_DV)
GDN_IN = GDN_QKV + GDN_HEADS * GDN_DV + 2 * GDN_HEADS
MLSTM_HEADS = 8
MLSTM_DV = D_MODEL // MLSTM_HEADS
MLSTM_DK = MLSTM_DV // 2
GATE_CAP = 15.0
MLSTM_IN = MLSTM_HEADS * (2 * MLSTM_DK + 2 * MLSTM_DV) + 2 * MLSTM_HEADS
DIFF_HEADS = 8
DIFF_D = D_MODEL // (2 * DIFF_HEADS)
ROPE_THETA = 500000.0
ROT_DIMS = DIFF_D // 4
N_GDN = (DEPTH_2 + 2) // 3
N_MLSTM = (DEPTH_2 + 1) // 3
N_DIFF = DEPTH_2 // 3


def rms_norm(x, g):
    xf = x.astype(jnp.float32)
    y = xf * lax.rsqrt(jnp.mean(xf * xf, axis=-1, keepdims=True) + NORM_EPS)
    return (y * g.astype(jnp.float32)).astype(x.dtype)

def l2_norm(x):
    xf = x.astype(jnp.float32)
    return xf * lax.rsqrt(jnp.sum(xf * xf, axis=-1, keepdims=True) + NORM_EPS)

def soft_cap(x):
    return GATE_CAP * jnp.tanh(x / GATE_CAP)

def to_chunks(x):
    b, t, h = x.shape[:3]
    x = x.reshape((b, t // CHUNK, CHUNK, h) + x.shape[3:])
    return jnp.swapaxes(jnp.moveaxis(x, 1, 0), 2, 3)

def from_chunks(x):
    n, b, h, c, d = x.shape
    return jnp.moveaxis(jnp.swapaxes(x, 2, 3), 0, 1).reshape(b, n * c, h, d)

def causal_conv(x, w):
    width, t = w.shape[0], x.shape[1]
    xp = jnp.pad(x, ((0, 0), (width - 1, 0), (0, 0)))
    return sum(xp[:, j:j + t] * w[j] for j in range(width))

def partial_rope(x, cos, sin):
    shp = (1, x.shape[1]) + (1,) * (x.ndim - 3) + (ROT_DIMS // 2,)
    c, s = cos.reshape(shp), sin.reshape(shp)
    x1, x2, rest = x[..., :ROT_DIMS // 2], x[..., ROT_DIMS // 2:ROT_DIMS], x[..., ROT_DIMS:]
    return jnp.concatenate([x1 * c - x2 * s, x1 * s + x2 * c, rest], axis=-1)

def gated_delta_rule(q, k, v, g, beta):
    dk, dv = q.shape[-1], v.shape[-1]
    qc = to_chunks(q * dk ** -0.5)
    kc = to_chunks(k)
    vc = to_chunks(v.astype(jnp.float32))
    gc = jnp.cumsum(to_chunks(g.astype(jnp.float32)), axis=-1)
    bc = to_chunks(beta.astype(jnp.float32))
    tril = jnp.tril(jnp.ones((CHUNK, CHUNK), bool))
    strict = jnp.tril(jnp.ones((CHUNK, CHUNK), bool), -1)
    diff = gc[..., :, None] - gc[..., None, :]
    decay = jnp.where(tril, jnp.exp(jnp.where(tril, diff, 0.0)), 0.0)
    kb = kc * bc[..., None]
    a_mat = jnp.where(strict, jnp.einsum('nbhid,nbhjd->nbhij', kb, kc) * decay, 0.0)
    t_mat = a_mat + jnp.eye(CHUNK, dtype=jnp.float32)
    rhs = jnp.concatenate([vc * bc[..., None], kb * jnp.exp(gc)[..., None]], axis=-1)
    sol = lax.linalg.triangular_solve(t_mat, rhs, left_side=True, lower=True, unit_diagonal=True)
    value, kcd = sol[..., :dv], sol[..., dv:]
    attn = jnp.einsum('nbhid,nbhjd->nbhij', qc, kc) * decay
    q_inter = qc * jnp.exp(gc)[..., None]
    g_last = gc[..., -1]
    k_state = kc * jnp.exp(g_last[..., None] - gc)[..., None]

    def step(s_st, xs):
        qi, kcd_i, val_i, attn_i, kst_i, gl_i = xs
        v_new = val_i - jnp.einsum('bhck,bhkv->bhcv', kcd_i, s_st)
        o = jnp.einsum('bhck,bhkv->bhcv', qi, s_st) + jnp.einsum('bhcs,bhsv->bhcv', attn_i, v_new)
        s_st = s_st * jnp.exp(gl_i)[..., None, None] + jnp.einsum('bhck,bhcv->bhkv', kst_i, v_new)
        return s_st, o

    s0 = jnp.zeros(qc.shape[1:3] + (dk, dv), jnp.float32)
    _, o = lax.scan(step, s0, (q_inter, kcd, value, attn, k_state, g_last))
    return from_chunks(o)

def gdn_mixer(h, w_in, conv_w, a_log, dt_bias, norm_g, w_out):
    b, t, _ = h.shape
    proj = h @ w_in
    qkv = jax.nn.silu(causal_conv(proj[..., :GDN_QKV], conv_w))
    z = proj[..., GDN_QKV:GDN_QKV + GDN_HEADS * GDN_DV].reshape(b, t, GDN_HEADS, GDN_DV)
    a = proj[..., GDN_QKV + GDN_HEADS * GDN_DV:GDN_IN - GDN_HEADS]
    bt = proj[..., GDN_IN - GDN_HEADS:]
    hk = GDN_HEADS * GDN_DK
    q = l2_norm(qkv[..., :hk].reshape(b, t, GDN_HEADS, GDN_DK))
    k = l2_norm(qkv[..., hk:2 * hk].reshape(b, t, GDN_HEADS, GDN_DK))
    v = qkv[..., 2 * hk:].reshape(b, t, GDN_HEADS, GDN_DV)
    g = -jnp.exp(a_log.astype(jnp.float32)) * jax.nn.softplus((a + dt_bias).astype(jnp.float32))
    beta = jax.nn.sigmoid(bt.astype(jnp.float32))
    o = gated_delta_rule(q, k, v, g, beta)
    o = rms_norm(o, norm_g) * jax.nn.silu(z.astype(jnp.float32))
    return o.reshape(b, t, GDN_HEADS * GDN_DV).astype(h.dtype) @ w_out

def mlstm_chunkwise(q, k, v, i_pre, f_pre):
    dk, dv = q.shape[-1], v.shape[-1]
    qc = to_chunks(q.astype(jnp.float32) * dk ** -0.5)
    kc = to_chunks(k.astype(jnp.float32))
    vc = to_chunks(v.astype(jnp.float32))
    lfc = to_chunks(jax.nn.log_sigmoid(f_pre.astype(jnp.float32)))
    ic = to_chunks(i_pre.astype(jnp.float32))
    tril = jnp.tril(jnp.ones((CHUNK, CHUNK), bool))

    def step(carry, xs):
        c_st, n_st, m_st = carry
        q_, k_, v_, lf, ig = xs
        bcum = jnp.cumsum(lf, axis=-1)
        g = bcum[..., -1]
        dlog = jnp.where(tril, bcum[..., :, None] - bcum[..., None, :] + ig[..., None, :], -jnp.inf)
        m_inter = bcum + m_st[..., None]
        m_out = jnp.maximum(m_inter, jnp.max(dlog, axis=-1))
        w_inter = jnp.exp(m_inter - m_out)
        s = jnp.einsum('bhtd,bhsd->bhts', q_, k_) * jnp.exp(dlog - m_out[..., None])
        num = w_inter[..., None] * jnp.einsum('bhtd,bhde->bhte', q_, c_st) + jnp.einsum('bhts,bhse->bhte', s, v_)
        den = w_inter * jnp.einsum('bhtd,bhd->bht', q_, n_st) + jnp.sum(s, axis=-1)
        h_ = num / jnp.maximum(jnp.abs(den), jnp.exp(-m_out))[..., None]
        a = g[..., None] - bcum + ig
        m_new = jnp.maximum(g + m_st, jnp.max(a, axis=-1))
        w_old = jnp.exp(g + m_st - m_new)
        kw = k_ * jnp.exp(a - m_new[..., None])[..., None]
        c_new = w_old[..., None, None] * c_st + jnp.einsum('bhsd,bhse->bhde', kw, v_)
        n_new = w_old[..., None] * n_st + jnp.sum(kw, axis=-2)
        return (c_new, n_new, m_new), h_

    bh = qc.shape[1:3]
    init = (jnp.zeros(bh + (dk, dv), jnp.float32), jnp.zeros(bh + (dk,), jnp.float32),
            jnp.zeros(bh, jnp.float32))
    _, hs = lax.scan(step, init, (qc, kc, vc, lfc, ic))
    return from_chunks(hs)

def mlstm_mixer(h, w_in, gate_b, norm_g, w_out):
    b, t, _ = h.shape
    proj = h @ w_in
    hk, hv = MLSTM_HEADS * MLSTM_DK, MLSTM_HEADS * MLSTM_DV
    q = proj[..., :hk].reshape(b, t, MLSTM_HEADS, MLSTM_DK)
    k = proj[..., hk:2 * hk].reshape(b, t, MLSTM_HEADS, MLSTM_DK)
    v = proj[..., 2 * hk:2 * hk + hv].reshape(b, t, MLSTM_HEADS, MLSTM_DV)
    o_gate = proj[..., 2 * hk + hv:2 * hk + 2 * hv]
    i_pre = soft_cap(proj[..., MLSTM_IN - 2 * MLSTM_HEADS:MLSTM_IN - MLSTM_HEADS] + gate_b[0])
    f_pre = soft_cap(proj[..., MLSTM_IN - MLSTM_HEADS:] + gate_b[1])
    hc = mlstm_chunkwise(q, k, v, i_pre, f_pre)
    hn = rms_norm(hc, norm_g.reshape(MLSTM_HEADS, MLSTM_DV)).reshape(b, t, hv)
    return (jax.nn.sigmoid(o_gate.astype(jnp.float32)) * hn).astype(h.dtype) @ w_out

def diff_attention(q, k, v, lam):
    b, t, h, _, d = q.shape
    nq = t // Q_BLOCK
    qf = jnp.moveaxis((q.astype(jnp.float32) * d ** -0.5).reshape(b, nq, Q_BLOCK, h, 2, d), 1, 0)
    kf, vf = k.astype(jnp.float32), v.astype(jnp.float32)
    key_chunk = jnp.arange(t) // CHUNK

    def one_block(args):
        qb, idx = args
        q_chunk = (idx * Q_BLOCK + jnp.arange(Q_BLOCK)) // CHUNK
        s = jnp.einsum('bqhcd,bkhcd->bhcqk', qb, kf)
        mask = key_chunk[None, :] <= q_chunk[:, None]
        p = jax.nn.softmax(jnp.where(mask, s, -jnp.inf), axis=-1)
        attn = p[:, :, 0] - lam * p[:, :, 1]
        return jnp.einsum('bhqk,bkhe->bqhe', attn, vf)

    o = lax.map(one_block, (qf, jnp.arange(nq)))
    return jnp.moveaxis(o, 0, 1).reshape(b, t, h, 2 * d)

def diff_mixer(h, w_in, lam_p, norm_g, w_out, lambda_init, cos, sin):
    b, t, _ = h.shape
    proj = h @ w_in
    hq = DIFF_HEADS * 2 * DIFF_D
    q = partial_rope(proj[..., :hq].reshape(b, t, DIFF_HEADS, 2, DIFF_D), cos, sin)
    k = partial_rope(proj[..., hq:2 * hq].reshape(b, t, DIFF_HEADS, 2, DIFF_D), cos, sin)
    v = proj[..., 2 * hq:].reshape(b, t, DIFF_HEADS, 2 * DIFF_D)
    lp = lam_p.astype(jnp.float32)
    lam = jnp.exp(jnp.sum(lp[0] * lp[1])) - jnp.exp(jnp.sum(lp[2] * lp[3])) + lambda_init
    o = diff_attention(q, k, v, lam)
    o = rms_norm(o, norm_g) * (1.0 - lambda_init)
    return o.reshape(b, t, hq).astype(h.dtype) @ w_out

def sq_relu_mlp(h, w1, w2):
    return jnp.square(jax.nn.relu(h @ w1)) @ w2

def second_inputs(seed: int = 0) -> dict:
    key = jax.random.key(seed)
    ks = jax.random.split(key, 18)
    nrm = lambda k, shape, scale: jax.random.normal(k, shape, jnp.float32) * scale
    return {
        "x": nrm(ks[0], (BATCH, SEQ, D_MODEL), 1.0),
        "norm_g": 1.0 + nrm(ks[1], (DEPTH_2, 4, D_MODEL), 0.05),
        "mlp_w1": nrm(ks[2], (DEPTH_2, D_MODEL, D_FF_2), D_MODEL ** -0.5),
        "mlp_w2": nrm(ks[3], (DEPTH_2, D_FF_2, D_MODEL), D_FF_2 ** -0.5),
        "gdn_w_in": nrm(ks[4], (N_GDN, D_MODEL, GDN_IN), D_MODEL ** -0.5),
        "gdn_conv": nrm(ks[5], (N_GDN, GDN_CONV, GDN_QKV), GDN_CONV ** -0.5),
        "gdn_a_log": jnp.log(jax.random.uniform(ks[6], (N_GDN, GDN_HEADS), jnp.float32, 1.0, 16.0)),
        "gdn_dt_bias": -4.0 + nrm(ks[7], (N_GDN, GDN_HEADS), 0.5),
        "gdn_norm_g": 1.0 + nrm(ks[8], (N_GDN, GDN_DV), 0.05),
        "gdn_w_out": nrm(ks[9], (N_GDN, GDN_HEADS * GDN_DV, D_MODEL), (GDN_HEADS * GDN_DV) ** -0.5),
        "mlstm_w_in": nrm(ks[10], (N_MLSTM, D_MODEL, MLSTM_IN), D_MODEL ** -0.5),
        "mlstm_gate_b": jnp.array([[-1.0], [3.0]], jnp.float32) + nrm(ks[11], (N_MLSTM, 2, MLSTM_HEADS), 0.1),
        "mlstm_norm_g": 1.0 + nrm(ks[12], (N_MLSTM, MLSTM_HEADS * MLSTM_DV), 0.05),
        "mlstm_w_out": nrm(ks[13], (N_MLSTM, MLSTM_HEADS * MLSTM_DV, D_MODEL), (MLSTM_HEADS * MLSTM_DV) ** -0.5),
        "diff_w_in": nrm(ks[14], (N_DIFF, D_MODEL, 3 * DIFF_HEADS * 2 * DIFF_D), D_MODEL ** -0.5),
        "diff_lambda": nrm(ks[15], (N_DIFF, 4, DIFF_D), 0.1),
        "diff_norm_g": 1.0 + nrm(ks[16], (N_DIFF, 2 * DIFF_D), 0.05),
        "diff_w_out": nrm(ks[17], (N_DIFF, DIFF_HEADS * 2 * DIFF_D, D_MODEL), (DIFF_HEADS * 2 * DIFF_D) ** -0.5),
    }

def second_block(x, norm_g, mlp_w1, mlp_w2, gdn_w_in, gdn_conv, gdn_a_log, gdn_dt_bias, gdn_norm_g,
              gdn_w_out, mlstm_w_in, mlstm_gate_b, mlstm_norm_g, mlstm_w_out, diff_w_in,
              diff_lambda, diff_norm_g, diff_w_out):
    t = x.shape[1]
    inv_freq = ROPE_THETA ** (-jnp.arange(0, ROT_DIMS, 2, dtype=jnp.float32) / ROT_DIMS)
    ang = jnp.arange(t, dtype=jnp.float32)[:, None] * inv_freq[None, :]
    cos, sin = jnp.cos(ang).astype(x.dtype), jnp.sin(ang).astype(x.dtype)
    for i in range(DEPTH_2):
        kind, j = i % N_MIXERS, i // N_MIXERS
        h = rms_norm(x, norm_g[i, 0])
        if kind == 0:
            m = gdn_mixer(h, gdn_w_in[j], gdn_conv[j], gdn_a_log[j], gdn_dt_bias[j], gdn_norm_g[j], gdn_w_out[j])
        elif kind == 1:
            m = mlstm_mixer(h, mlstm_w_in[j], mlstm_gate_b[j], mlstm_norm_g[j], mlstm_w_out[j])
        else:
            lambda_init = 0.8 - 0.6 * math.exp(-0.3 * i)
            m = diff_mixer(h, diff_w_in[j], diff_lambda[j], diff_norm_g[j], diff_w_out[j], lambda_init, cos, sin)
        x = x + rms_norm(m, norm_g[i, 1])
        h = rms_norm(x, norm_g[i, 2])
        x = x + rms_norm(sq_relu_mlp(h, mlp_w1[i], mlp_w2[i]), norm_g[i, 3])
    return x


def setup_inputs(seed=0):
    out = dict(first_inputs(seed))
    for name, value in second_inputs(seed + 1).items():
        if name != "x":
            out[name + "_2"] = value
    return out


def reference(
    x, ln_g, ln_b, ffn_wg, ffn_wu, ffn_wd, w_in, w_out, cmp_pe, cmp_w1, cmp_w2, pool_w,
    pool_scale, gla_wa2, gla_ba, gla_norm_g, norm_g_2, mlp_w1_2, mlp_w2_2, gdn_w_in_2,
    gdn_conv_2, gdn_a_log_2, gdn_dt_bias_2, gdn_norm_g_2, gdn_w_out_2, mlstm_w_in_2,
    mlstm_gate_b_2, mlstm_norm_g_2, mlstm_w_out_2, diff_w_in_2, diff_lambda_2, diff_norm_g_2,
    diff_w_out_2,
):
    x = first_block(
        x, ln_g, ln_b, ffn_wg, ffn_wu, ffn_wd, w_in, w_out, cmp_pe, cmp_w1, cmp_w2, pool_w,
        pool_scale, gla_wa2, gla_ba, gla_norm_g,
    )
    return second_block(
        x, norm_g_2, mlp_w1_2, mlp_w2_2, gdn_w_in_2, gdn_conv_2, gdn_a_log_2, gdn_dt_bias_2,
        gdn_norm_g_2, gdn_w_out_2, mlstm_w_in_2, mlstm_gate_b_2, mlstm_norm_g_2, mlstm_w_out_2,
        diff_w_in_2, diff_lambda_2, diff_norm_g_2, diff_w_out_2,
    )


_drawn_inputs = setup_inputs


def setup_inputs(seed=0):
    import zlib

    import numpy as np

    out = dict(_drawn_inputs(seed))
    spreads = {}
    factors = {'gla_ba': 4.08, 'gla_norm_g': 3.192}
    for name, (base, spread) in spreads.items():
        noise = np.random.default_rng([zlib.crc32(name.encode()), seed]).standard_normal(out[name].shape)
        drawn = base * np.exp(spread * noise) if base else spread * noise
        out[name] = __import__('jax').numpy.asarray(drawn.astype(out[name].dtype))
    for name, factor in factors.items():
        out[name] = (out[name] * factor).astype(out[name].dtype)
    return out
```

```python
from contextlib import ExitStack
import math

import concourse.bass as bass
from concourse import mybir

F32 = mybir.dt.float32
F32R = mybir.dt.float32r
BF16 = mybir.dt.bfloat16
ALU = mybir.AluOpType
ACT = mybir.ActivationFunctionType
AX = mybir.AxisListType

P = 128
D = 1024
KT = D // P
SEQ = 256
TT = SEQ // P
DEPTH = 2
D_FF = 2816
ALPHA = (2.0 * DEPTH) ** 0.25
LN_EPS = 1e-5
RMS_EPS = 1e-6
DEPTH_2 = 4
D_FF_2 = 4096
CHUNK = 64
NEG = -1.0e30

CW = 256
RAW = 3
SPLIT = 3
BODY = 6
assert BODY % RAW == 0 and BODY % SPLIT == 0

FF_STEPS = D_FF // CW
MLP_STEPS = D_FF_2 // CW

NSA_Q, NSA_KC, NSA_VC, NSA_KS, NSA_VS, NSA_KW, NSA_VW = 0, 512, 640, 768, 896, 1024, 1152
NSA_GATE, POOL_U, GLA_Q, GLA_K, GLA_V, GLA_A, GLA_R = 1280, 1304, 1560, 1688, 1816, 2072, 2088
GDN_QKV, GDN_Z, GDN_AB = 3072, 1024, 16


class Signal:

    def __init__(self, ctx, nc, name, per):
        self.sem, self.per = ctx.enter_context(nc.semaphore(name)), per

    def count(self, turn, k):
        assert 0 <= k < self.per
        return turn * self.per + k + 1


class Chain:

    def __init__(self, eng, sem):
        self.eng, self.sem, self.n = eng, sem, 0

    def mark(self, ins):
        self.n += 1
        ins.then_inc(self.sem, 1)
        return self.n

    def wait(self, n=None):
        self.eng.wait_ge(self.sem, self.n if n is None else n)

    def link(self, ins):
        self.mark(ins)
        self.wait()


def column_pieces(w, pieces):
    out, at = [], 0
    for c0, n in pieces:
        out.append(("cols", at, n, w[:, c0:c0 + n].rearrange("(k p) c -> p k c", p=P)))
        at += n
    return out


def row_pieces(w, r0):
    return [("rows", 0, 2, w[r0:r0 + 2 * P, :].rearrange("(r p) c -> p r c", p=P))]


def mixed_row_pieces(w, r0):
    out = []
    for r in range(2):
        f = r0 // P + r
        for g in range(2):
            out.append(("half", g, r, w[g * 256 + f * 64:g * 256 + f * 64 + 64, :]))
    return out


def weight_plan(w):
    plan, start = [], {}
    for l in range(DEPTH):
        for j in range(2):
            if j == 1:
                start["mix", l] = len(plan)
                wi = w["w_in"][l]
                for f0 in (0, 128):
                    plan.append(column_pieces(wi, [(NSA_Q + f0, 64), (NSA_Q + f0 + 256, 64),
                                                   (NSA_Q + f0 + 64, 64), (NSA_Q + f0 + 320, 64)]))
                for c0 in (NSA_KC, NSA_VC):
                    plan.append(column_pieces(wi, [(c0, 64), (c0, 64), (c0 + 64, 64), (c0 + 64, 64)]))
                plan.append(column_pieces(wi, [(NSA_KS, P), (NSA_KW, P)]))
                plan.append(column_pieces(wi, [(NSA_VS, P), (NSA_VW, P)]))
                plan.append(column_pieces(wi, [(POOL_U, 256)]))
                plan.append(column_pieces(wi, [(GLA_Q, 256)]))
                plan.append(column_pieces(wi, [(GLA_K, P), (NSA_GATE, 24), (GLA_A, 16)]))
                plan.append(column_pieces(wi, [(GLA_V, 256)]))
                plan.append(column_pieces(wi, [(GLA_R, 256)]))
                start["mix_out", l] = len(plan)
                wo = w["w_out"][l]
                plan += [mixed_row_pieces(wo, 0), mixed_row_pieces(wo, 256), row_pieces(wo, 512), row_pieces(wo, 768)]
            start["ffn", l, j] = len(plan)
            wg, wu, wd = w["ffn_wg"][l, j], w["ffn_wu"][l, j], w["ffn_wd"][l, j]
            for i in range(FF_STEPS):
                plan.append(column_pieces(wg, [(i * CW, CW)]))
                plan.append(column_pieces(wu, [(i * CW, CW)]))
                if i:
                    plan.append(row_pieces(wd, (i - 1) * CW))
            plan.append(row_pieces(wd, (FF_STEPS - 1) * CW))
    for i in range(DEPTH_2):
        start["in", i] = len(plan)
        if i % 3 == 0:
            wi, wo = w["gdn_w_in_2"][i // 3], w["gdn_w_out_2"][i // 3]
            plan.append(column_pieces(wi, [(GDN_QKV + GDN_Z, GDN_AB)]))
            plan += [column_pieces(wi, [(c, CW)]) for c in range(0, GDN_QKV + GDN_Z, CW)]
        elif i % 3 == 1:
            wi, wo = w["mlstm_w_in_2"][0], w["mlstm_w_out_2"][0]
            plan.append(column_pieces(wi, [(3072, 16)]))
            plan += [column_pieces(wi, [(c, CW)]) for c in range(0, 3072, CW)]
        else:
            wi, wo = w["diff_w_in_2"][0], w["diff_w_out_2"][0]
            plan += [column_pieces(wi, [(c, CW)]) for c in range(0, 3072, CW)]
        start["out", i] = len(plan)
        plan += [row_pieces(wo, r) for r in range(0, D, CW)]
        start["mlp", i] = len(plan)
        w1, w2 = w["mlp_w1_2"][i], w["mlp_w2_2"][i]
        for s in range(MLP_STEPS):
            plan.append(column_pieces(w1, [(s * CW, CW)]))
            if s:
                plan.append(row_pieces(w2, (s - 1) * CW))
        plan.append(row_pieces(w2, (MLP_STEPS - 1) * CW))
    return plan, start



POOL_WINDOWS = (2, 4, 8, 16)
N_CMP, CMP_STRIDE, CMP_BLOCK = 15, 16, 32
LEVELS = 6
ROT = 16
ROPE_THETA = 500000.0

CONST_AT = {}
_at = 0
for _name, _n in (("ident", P), ("upto", P), ("after", P), ("causal", 3 * P), ("cmp_mask", 2 * N_CMP), ("has_cmp", 2)):
    CONST_AT[_name] = (_at, _at + _n)
    _at += _n
N_CONST = _at


def shape_constants():
    import numpy as np

    s = np.arange(P)[:, None]
    t = np.arange(P)[None, :]
    same = (s // CHUNK) == (t // CHUNK)
    c = np.zeros((P, N_CONST), np.float32)

    def put(name, a):
        c[:, slice(*CONST_AT[name])] = a

    put("ident", s == t)
    put("upto", (s <= t) & same)
    put("after", (s > t) & same)
    tri = np.where(t <= s, 0.0, NEG)
    put("causal", np.concatenate([tri, np.zeros((P, P)), tri], 1))
    token = np.arange(SEQ).reshape(TT, P).T
    ends = np.arange(N_CMP) * CMP_STRIDE + CMP_BLOCK - 1
    put("cmp_mask", np.where(ends[None, None, :] <= token[:, :, None], 0.0, NEG).reshape(P, -1))
    put("has_cmp", token >= CMP_BLOCK - 1)

    pool = np.zeros((SEQ, len(POOL_WINDOWS), SEQ), np.float64)
    for g, width in enumerate(POOL_WINDOWS):
        for target in range(SEQ):
            lo = max(0, target - width + 1)
            pool[lo:target + 1, g, target] = 1.0 / (target + 1 - lo)
            pool[target, g, target] -= 1.0
    pool = np.concatenate([pool[:P], pool[P:, :, P:]], 2).reshape(P, -1)

    levels = np.zeros((P, LEVELS, P), np.float32)
    for v in range(LEVELS):
        b = 1 << v
        levels[:, v, :] = (s // (2 * b) == t // (2 * b)) & (s // b % 2 == 1) & (t // b % 2 == 0)
    heads = ((np.arange(P) // 32)[:, None] == (np.arange(256) // 64)[None, :])

    inv = ROPE_THETA ** (-np.arange(0, ROT, 2, dtype=np.float32) / ROT)
    angle = np.arange(SEQ, dtype=np.float32)[:, None] * inv.astype(np.float32)[None, :]
    rope = np.stack([np.cos(angle), np.sin(angle)], 1).reshape(TT, P, 2 * (ROT // 2)).transpose(1, 0, 2)
    hidden = np.where(t // CHUNK <= s // CHUNK, 0.0, NEG)
    return {
        "const_main": c,
        "const_pool": pool.astype(np.float32),
        "const_levels": levels.reshape(P, -1),
        "const_heads": heads.astype(np.float32),
        "const_rope": np.ascontiguousarray(rope.reshape(P, -1), np.float32),
        "const_tri": (s <= t).astype(np.float32),
        "const_chunks": np.concatenate([hidden, np.zeros((P, P)), hidden], 1).astype(np.float32),
    }


def two_block_model(nc, w, out):
    plan, start = weight_plan(w)
    n_chunks = len(plan)
    landed, total = [], [0] * RAW
    for n, pieces in enumerate(plan):
        total[n % RAW] += 16 * len(pieces)
        landed.append(total[n % RAW])

    ctx = ExitStack()
    ctx.enter_context(nc.allow_non_contiguous_dma(reason="small transposed parameters"))

    def sb(name, shape, dt=F32):
        return ctx.enter_context(nc.sbuf_tensor(name, shape, dt))

    def signal(name, per):
        return Signal(ctx, nc, name, per)

    def semaphore(name):
        return ctx.enter_context(nc.semaphore(name))

    raw = sb("raw", [P, RAW, KT * CW])
    w_hi = sb("w_hi", [P, SPLIT, KT * CW], F32R)
    w_lo = sb("w_lo", [P, SPLIT, KT * CW], F32R)
    x = sb("x", [P, TT, D])
    aT_hi = sb("aT_hi", [P, KT, SEQ], F32R)
    aT_lo = sb("aT_lo", [P, KT, SEQ], F32R)
    h_hi = sb("h_hi", [P, 3, 512], F32R)
    h_lo = sb("h_lo", [P, 3, 512], F32R)
    gb = sb("gb", [P, 2, D])
    NW = 10
    ws = [sb(f"ws{k}", [P, 2048]) for k in range(NW)]
    consts = sb("consts", [P, N_CONST])
    zrow = sb("zrow", [1, 512], BF16)
    ones = sb("ones", [P, 1])
    small = sb("small", [P, 640])
    ps = ctx.enter_context(nc.psum_tensor("ps", [P, 8, 512], F32))

    c_at = {name: slice(a, b) for name, (a, b) in CONST_AT.items()}
    ident = consts[:, c_at["ident"]]

    raw_landed = [semaphore(f"raw_landed{s}") for s in range(RAW)]
    hi_ready = semaphore("hi_ready")
    lo_ready = semaphore("lo_ready")
    weights_used = semaphore("weights_used")
    x_landed = semaphore("x_landed")
    consts_landed = semaphore("consts_landed")
    zrow_set = semaphore("zrow_set")
    opened = semaphore("accumulators_opened")
    out_stored = semaphore("out_stored")
    gain_landed = semaphore("gain_landed")
    gate_act = semaphore("gate_activated")
    hid_made = semaphore("hidden_made")
    hid_hi = semaphore("hidden_hi_ready")
    hid_lo = semaphore("hidden_lo_ready")
    ln_var = signal("ln_variance", TT)
    ln_rstd = signal("ln_rstd", TT)
    y_bank = signal("y_bank_summed", 3)
    ln_done = signal("ln_done", TT)
    turned = signal("turned_by_pe", 2 * TT)
    aT_hi_set = signal("aT_hi_set", 2 * TT)
    aT_lo_set = signal("aT_lo_set", 2 * TT)
    act_chain = semaphore("act_chain")
    dve_chain = semaphore("dve_chain")
    pool_chain = semaphore("pool_chain")
    pe_chain = semaphore("pe_chain")

    hid_before, seen = {}, 0
    for l in range(DEPTH):
        for j in range(2):
            hid_before["ffn", l, j] = seen
            seen += FF_STEPS
    for i in range(DEPTH_2):
        hid_before["mlp", i] = seen
        seen += MLP_STEPS

    PER_TURN = 16 * BODY // RAW


    def slot_view(t, n, piece):
        kind, at, size = piece[:3]
        if kind == "cols":
            return t[:, n % RAW, :].rearrange("p (k c) -> p k c", c=CW)[:, :, at:at + size]
        return t[:, n % RAW, :].rearrange("p (r c) -> p r c", c=D)

    def used_part(t, n):
        pieces = plan[n]
        if pieces[0][0] != "cols":
            return t[:, n % RAW, :]
        width = sum(p[2] for p in pieces)
        if width == CW:
            return t[:, n % RAW, :]
        return t[:, n % RAW, :].rearrange("p (k c) -> p k c", c=CW)[:, :, 0:width]

    def load_chunk(sp, n):
        if n >= RAW:
            sp.wait_ge(lo_ready, n - RAW + 1)
        for piece in plan[n]:
            if piece[0] == "half":
                _, g, r, src = piece
                dst = raw[64 * g:64 * g + 64, n % RAW, r * D:(r + 1) * D]
            else:
                dst, src = slot_view(raw, n, piece), piece[3]
            sp.dma_start(dst, src).then_inc(raw_landed[n % RAW], 16)

    def split_high(act, n, turn=0):
        if n >= n_chunks:
            return
        act.wait_ge(raw_landed[n % RAW], landed[n] + PER_TURN * turn)
        if n >= SPLIT:
            act.wait_ge(weights_used, n - SPLIT + 1 + BODY * turn)
        nc.scalar.copy(used_part(w_hi, n), used_part(raw, n)).then_inc(hi_ready, 1)

    def split_low(dve, n, turn=0):
        if n >= n_chunks:
            return
        dve.wait_ge(hi_ready, n + 1 + BODY * turn)
        nc.vector.tensor_tensor(used_part(w_lo, n), used_part(raw, n), used_part(w_hi, n).bitcast(F32),
                                ALU.subtract).then_inc(lo_ready, 1)

    def product(pe, dst, l_hi, l_lo, r_hi, r_lo, start, stop):
        nc.tensor.matmul(dst, l_hi, r_hi, start=start, stop=False)
        nc.tensor.matmul(dst, l_hi, r_lo, start=False, stop=False)
        return nc.tensor.matmul(dst, l_lo, r_hi, start=False, stop=stop)

    def cols_slot(t, n):
        return t[:, n % SPLIT, :].rearrange("p (k c) -> p k c", c=CW)

    def features_product(pe, n, bank, turn=0, tiles=2, xpass=None):
        pe.wait_ge(lo_ready, n + 1 + BODY * turn)
        hi, lo = cols_slot(w_hi, n), cols_slot(w_lo, n)
        for ft in range(tiles):
            for k in range(KT):
                if xpass is not None and ft == 0 and k % 4 == 0:
                    pe.wait_ge(aT_lo_set.sem, aT_lo_set.count(xpass, 2 + k // 4))
                last = product(pe, ps[:, bank, ft * SEQ:(ft + 1) * SEQ], hi[:, k, ft * P:(ft + 1) * P],
                               lo[:, k, ft * P:(ft + 1) * P], aT_hi[:, k, :], aT_lo[:, k, :], k == 0, k == KT - 1)
        last.then_inc(weights_used, 1)

    def tokens_product(pe, n, bank, width=CW):
        pe.wait_ge(lo_ready, n + 1)
        hi, lo = cols_slot(w_hi, n), cols_slot(w_lo, n)
        for t in range(TT):
            for k in range(KT):
                last = product(pe, ps[:, bank, t * CW:t * CW + width], aT_hi[:, k, t * P:(t + 1) * P],
                               aT_lo[:, k, t * P:(t + 1) * P], hi[:, k, 0:width], lo[:, k, 0:width], k == 0, k == KT - 1)
        last.then_inc(weights_used, 1)

    def open_accumulators(pe):
        for b in range(4):
            last = nc.tensor.matmul(ps[:, b, :], zrow[0:1, 0:P], zrow[0:1, :], start=True, stop=False)
        return last

    def last_rows(pe, chunks, turn):
        for b in range(4):
            t, c = b // 2, slice(b % 2 * 512, b % 2 * 512 + 512)
            for q, (n, l_hi, l_lo, wait) in enumerate(chunks):
                if b == 0:
                    wait()
                    pe.wait_ge(lo_ready, n + 1)
                hi = w_hi[:, n % SPLIT, :].rearrange("p (r c) -> p r c", c=D)
                lo = w_lo[:, n % SPLIT, :].rearrange("p (r c) -> p r c", c=D)
                for r in range(2):
                    s = slice(r * SEQ + t * P, r * SEQ + (t + 1) * P)
                    last = product(pe, ps[:, b, :], l_hi[:, s], l_lo[:, s], hi[:, r, c], lo[:, r, c], False, q == 1 and r == 1)
                if b == 3:
                    last.then_inc(weights_used, 1)
            if b < 3:
                last.then_inc(y_bank.sem, 1)

    def wait_y(eng, turn, b, n_last):
        if b < 3:
            eng.wait_ge(y_bank.sem, y_bank.count(turn, b))
        else:
            eng.wait_ge(weights_used, n_last + 1)

    def rows_product(pe, n, l_hi, l_lo, turn=0):
        pe.wait_ge(lo_ready, n + 1 + BODY * turn)
        hi = w_hi[:, n % SPLIT, :].rearrange("p (r c) -> p r c", c=D)
        lo = w_lo[:, n % SPLIT, :].rearrange("p (r c) -> p r c", c=D)
        for t in range(TT):
            for half in range(2):
                c = slice(half * 512, half * 512 + 512)
                for r in range(2):
                    s = slice(r * SEQ + t * P, r * SEQ + (t + 1) * P)
                    last = product(pe, ps[:, 2 * t + half, :], l_hi[:, s], l_lo[:, s], hi[:, r, c], lo[:, r, c],
                                   False, False)
        last.then_inc(weights_used, 1)

    def y_tile(t):
        return ps[:, 2 * t:2 * t + 2, :].rearrange("p b c -> p (b c)")


    def ffn_tensor(pe, l, j, xpass):
        n0, hid0 = start["ffn", l, j], hid_before["ffn", l, j]
        open_accumulators(pe)
        features_product(pe, n0, 4, xpass=xpass)
        features_product(pe, n0 + 1, 5)

        def step(b, it, rows=True):
            n, i = n0 + 2 + 3 * b, 1 + b
            features_product(pe, n, 4 + 2 * (i % 2), turn=it)
            features_product(pe, n + 1, 5 + 2 * (i % 2), turn=it)
            if rows:
                pe.wait_ge(hid_lo, hid0 + i + 2 * it)
                rows_product(pe, n + 2, h_hi[:, (i - 1) % 2, :], h_lo[:, (i - 1) % 2, :], turn=it)

        turns = (FF_STEPS - 1) // 2 - 1
        with pe.Fori(0, turns) as it:
            step(0, it)
            step(1, it)
        step(2 * turns, 0)
        step(2 * turns + 1, 0, rows=False)
        last_rows(pe, [(n, h_hi[:, i % 2, :], h_lo[:, i % 2, :], lambda i=i: pe.wait_ge(hid_lo, hid0 + i + 1))
                       for n, i in ((n0 + 3 * FF_STEPS - 2, FF_STEPS - 2), (n0 + 3 * FF_STEPS - 1, FF_STEPS - 1))],
                  3 * l + 2 * j)

    def ffn_scalar(act, l, j):
        n0, hid0 = start["ffn", l, j], hid_before["ffn", l, j]
        gate = [ws[0][:, 0:512], ws[0][:, 512:1024]]

        def silu(n, i, turn=0, steps=0):
            act.wait_ge(weights_used, n + 1 + BODY * turn)
            if i + steps >= 2 or steps:
                act.wait_ge(hid_made, hid0 + i - 1 + 2 * turn)
            nc.scalar.activation(gate[i % 2], ps[:, 4 + 2 * (i % 2), :], ACT.Silu).then_inc(gate_act, 1)

        split_high(act, n0 + 3)
        silu(n0, 0)
        split_high(act, n0 + 4)

        def two_steps(n_first, i_first, turn=0, final=False):
            for b in range(2):
                n, i = n_first + 3 * b, i_first + b
                split_high(act, n + 3, turn)
                silu(n, i, turn, steps=1)
                split_high(act, n + 4, turn)
                if not (final and b == 1):
                    split_high(act, n + 5, turn)

        turns = (FF_STEPS - 1) // 2 - 1
        with act.Fori(0, turns) as it:
            two_steps(n0 + 2, 1, it)
        two_steps(n0 + 2 + BODY * turns, 1 + 2 * turns, final=True)

    def hidden_vector(dve, n, hid, buf, bank, gate, turn=0, step=0, war=True):
        dve.wait_ge(gate_act, hid + 1 + step * turn)
        if n is not None:
            dve.wait_ge(weights_used, n + 1 + BODY * turn)
        up = ps[:, bank, :] if bank is not None else gate
        h = ws[1][:, 512 * buf:512 * buf + 512]
        nc.vector.tensor_tensor(h, gate, up, ALU.mult).then_inc(hid_made, 1)
        dve.wait_ge(hid_made, hid + 1 + step * turn)
        nc.vector.tensor_copy(h_hi[:, buf, :], h).then_inc(hid_hi, 1)
        dve.wait_ge(hid_hi, hid + 1 + step * turn)
        nc.vector.tensor_tensor(h_lo[:, buf, :], h, h_hi[:, buf, :].bitcast(F32), ALU.subtract).then_inc(hid_lo, 1)

    def ffn_vector(dve, l, j):
        n0, hid0 = start["ffn", l, j], hid_before["ffn", l, j]
        gate = [ws[0][:, 0:512], ws[0][:, 512:1024]]
        split_low(dve, n0 + 3)
        hidden_vector(dve, n0 + 1, hid0, 0, 5, gate[0])
        split_low(dve, n0 + 4)

        def two_steps(n_first, i_first, turn=0, final=False):
            for b in range(2):
                n, i = n_first + 3 * b, i_first + b
                split_low(dve, n + 3, turn)
                hidden_vector(dve, n + 1, hid0 + i, i % 2, 5 + 2 * (i % 2), gate[i % 2], turn, step=2)
                split_low(dve, n + 4, turn)
                if not (final and b == 1):
                    split_low(dve, n + 5, turn)

        turns = (FF_STEPS - 1) // 2 - 1
        with dve.Fori(0, turns) as it:
            two_steps(n0 + 2, 1, it)
        two_steps(n0 + 2 + BODY * turns, 1 + 2 * turns, final=True)

    def ffn_sync(sp, l, j):
        n0 = start["ffn", l, j]
        wg, wu, wd = w["ffn_wg"][l, j], w["ffn_wu"][l, j], w["ffn_wd"][l, j]
        wdr = wd.rearrange("(s r p) c -> p s r c", p=P, r=2)
        load_chunk(sp, n0)
        load_chunk(sp, n0 + 1)
        with sp.Fori(0, (FF_STEPS - 1) // 2) as it:
            for b in range(2):
                n = n0 + 2 + 3 * b
                for q, m in ((0, wg), (1, wu)):
                    wait_slot(sp, n + q, it)
                    src = m[:, bass.ds((1 + b) * CW + it * (2 * CW), CW)].rearrange("(k p) c -> p k c", p=P)
                    sp.dma_start(slot_view(raw, n + q, plan[n + q][0]), src).then_inc(raw_landed[(n + q) % RAW], 16)
                wait_slot(sp, n + 2, it)
                src = wd[bass.ds(b * CW + it * (2 * CW), CW), :].rearrange("(r p) c -> p r c", p=P)
                sp.dma_start(slot_view(raw, n + 2, plan[n + 2][0]), src).then_inc(raw_landed[(n + 2) % RAW], 16)
        load_chunk(sp, n0 + 3 * FF_STEPS - 1)

    def wait_slot(sp, n, turn):
        sp.wait_ge(lo_ready, n - RAW + 1 + BODY * turn)


    def mlp_tensor(pe, i, xpass):
        n0, hid0 = start["mlp", i], hid_before["mlp", i]
        open_accumulators(pe)
        features_product(pe, n0, 4, xpass=xpass)

        def step(b, it, rows=True):
            n, s = n0 + 1 + 2 * b, 1 + b
            features_product(pe, n, 4 + s % 3, turn=it)
            if rows:
                pe.wait_ge(hid_lo, hid0 + s + 3 * it)
                rows_product(pe, n + 1, h_hi[:, (s - 1) % 3, :], h_lo[:, (s - 1) % 3, :], turn=it)

        turns = (MLP_STEPS - 1) // 3 - 1
        with pe.Fori(0, turns) as it:
            for b in range(3):
                step(b, it)
        for b in range(3):
            step(3 * turns + b, 0, rows=b < 2)
        last_rows(pe, [(n, h_hi[:, s % 3, :], h_lo[:, s % 3, :], lambda s=s: pe.wait_ge(hid_lo, hid0 + s + 1))
                       for n, s in ((n0 + 2 * MLP_STEPS - 2, MLP_STEPS - 2), (n0 + 2 * MLP_STEPS - 1, MLP_STEPS - 1))],
                  3 * DEPTH + 2 * i + 1)

    def mlp_scalar(act, i):
        n0, hid0 = start["mlp", i], hid_before["mlp", i]
        gate = [ws[0][:, 512 * k:512 * k + 512] for k in range(3)]

        def relu(n, s, turn=0, loop=False):
            act.wait_ge(weights_used, n + 1 + BODY * turn)
            if loop:
                act.wait_ge(hid_made, hid0 + s - 2 + 3 * turn if s >= 2 else hid0 + 3 * turn)
            nc.scalar.activation(gate[s % 3], ps[:, 4 + s % 3, :], ACT.Relu).then_inc(gate_act, 1)

        split_high(act, n0 + 3)
        relu(n0, 0)

        def three_steps(n_first, s_first, turn=0, final=False):
            for b in range(3):
                n, s = n_first + 2 * b, s_first + b
                split_high(act, n + 3, turn)
                relu(n, s, turn, loop=True)
                if not (final and b == 2):
                    split_high(act, n + 4, turn)

        turns = (MLP_STEPS - 1) // 3 - 1
        with act.Fori(0, turns) as it:
            three_steps(n0 + 1, 1, it)
        three_steps(n0 + 1 + BODY * turns, 1 + 3 * turns, final=True)

    def mlp_vector(dve, i):
        n0, hid0 = start["mlp", i], hid_before["mlp", i]
        gate = [ws[0][:, 512 * k:512 * k + 512] for k in range(3)]
        split_low(dve, n0 + 3)
        hidden_vector(dve, None, hid0, 0, None, gate[0])

        def three_steps(n_first, s_first, turn=0, final=False):
            for b in range(3):
                n, s = n_first + 2 * b, s_first + b
                split_low(dve, n + 3, turn)
                hidden_vector(dve, None, hid0 + s, s % 3, None, gate[s % 3], turn, step=3)
                if not (final and b == 2):
                    split_low(dve, n + 4, turn)

        turns = (MLP_STEPS - 1) // 3 - 1
        with dve.Fori(0, turns) as it:
            three_steps(n0 + 1, 1, it)
        three_steps(n0 + 1 + BODY * turns, 1 + 3 * turns, final=True)

    def mlp_sync(sp, i):
        n0 = start["mlp", i]
        w1, w2 = w["mlp_w1_2"][i], w["mlp_w2_2"][i]
        load_chunk(sp, n0)
        with sp.Fori(0, (MLP_STEPS - 1) // 3) as it:
            for b in range(3):
                n = n0 + 1 + 2 * b
                wait_slot(sp, n, it)
                src = w1[:, bass.ds((1 + b) * CW + it * (3 * CW), CW)].rearrange("(k p) c -> p k c", p=P)
                sp.dma_start(slot_view(raw, n, plan[n][0]), src).then_inc(raw_landed[n % RAW], 16)
                wait_slot(sp, n + 1, it)
                src = w2[bass.ds(b * CW + it * (3 * CW), CW), :].rearrange("(r p) c -> p r c", p=P)
                sp.dma_start(slot_view(raw, n + 1, plan[n + 1][0]), src).then_inc(raw_landed[(n + 1) % RAW], 16)
        load_chunk(sp, n0 + 2 * MLP_STEPS - 1)


    def turn_tensor(pe, xpass, src, ready, scaled=False):
        for t in range(TT):
            ready(pe, t)
            for half in range(2):
                for q in range(4):
                    k = 4 * half + q
                    o, tile = ps[:, 4 + 2 * t + half, q * P:(q + 1) * P], src[:, t, k * P:(k + 1) * P]
                    if scaled:
                        last = nc.tensor.matmul(o, tile, diag[:, t, :], start=True, stop=True)
                    else:
                        last = nc.tensor.transpose(o, tile, ident)
                last.then_inc(turned.sem, 1)

    def turn_scalar(act, xpass):
        for t in range(TT):
            for half in range(2):
                act.wait_ge(turned.sem, turned.count(xpass, 2 * t + half))
                nc.scalar.copy(aT_hi[:, 4 * half:4 * half + 4, t * P:(t + 1) * P],
                               ps[:, 4 + 2 * t + half, :].rearrange("p (q c) -> p q c", c=P)).then_inc(aT_hi_set.sem, 1)

    def turn_vector(dve, xpass):
        for t in range(TT):
            for half in range(2):
                dve.wait_ge(aT_hi_set.sem, aT_hi_set.count(xpass, 2 * t + half))
                s = (slice(None), slice(4 * half, 4 * half + 4), slice(t * P, (t + 1) * P))
                nc.vector.tensor_tensor(aT_lo[s], ps[:, 4 + 2 * t + half, :].rearrange("p (q c) -> p q c", c=P),
                                        aT_hi[s].bitcast(F32), ALU.subtract).then_inc(aT_lo_set.sem, 1)

    def wait_turned(pe, xpass):
        pe.wait_ge(aT_lo_set.sem, aT_lo_set.count(xpass, 2 * TT - 1))


    Z = ws[2].rearrange("p (t c) -> p t c", c=D)
    stats = small[:, 0:24].rearrange("p (t a b) -> p t a b", a=2, b=6)
    mv = small[:, 24:28].rearrange("p (t a) -> p t a", a=2)
    ve = small[:, 28:30]
    rstd = small[:, 30:32]
    mhalf = small[:, 34:66]
    eps_d = small[:, 32:33]

    def norm_vector(dve, q, scale, n_last):
        ch = Chain(dve, dve_chain)
        ch.n = dve_steps[0]
        for t in range(TT):
            wait_y(dve, q, 2 * t + 1, n_last)
            ch.link(nc.vector.scalar_tensor_tensor(out=Z[:, t, :], in0=y_tile(t), scalar=scale / ALPHA, in1=x[:, t, :],
                                                   op0=ALU.mult, op1=ALU.add))
            for a in range(2):
                m = ch.mark(nc.vector.bn_stats(stats[:, t, a, :], Z[:, t, 512 * a:512 * a + 512]))
            ch.wait(m)
            ch.link(nc.vector.bn_aggr(mv[:, t, :], stats[:, t, :, :].rearrange("p a b -> p (a b)")))
            nc.vector.tensor_scalar(ve[:, t:t + 1], mv[:, t, 1:2], LN_EPS / ALPHA ** 2, None, ALU.add).then_inc(ln_var.sem, 1)
            if t == 0:
                dve.wait_ge(gain_landed, gain_count("ln", q))
            ch.link(nc.vector.scalar_tensor_tensor(out=Z[:, t, :], in0=Z[:, t, :], scalar=mv[:, t, 0:1], in1=gb[:, 0, :],
                                                   op0=ALU.subtract, op1=ALU.mult))
            dve.wait_ge(ln_rstd.sem, ln_rstd.count(q, t))
            nc.vector.scalar_tensor_tensor(out=x[:, t, :], in0=Z[:, t, :], scalar=rstd[:, t:t + 1], in1=gb[:, 1, :],
                                           op0=ALU.mult, op1=ALU.add).then_inc(ln_done.sem, 1)
        dve_steps[0] = ch.n

    def norm_pool(pool, q):
        l, j = q // 3, q % 3
        if q:
            pool.wait_ge(ln_done.sem, ln_done.count(q - 1, TT - 1))
        if q == 3 * DEPTH - 1:
            load_pre_gain(pool, 0)
        pool.dma_start(gb[:, 0, :], w["ln_g"][l, j:j + 1, :].to_broadcast([P, D])).then_inc(gain_landed, 16)
        pool.dma_start(gb[:, 1, :], w["ln_b"][l, j:j + 1, :].to_broadcast([P, D])).then_inc(gain_landed, 16)
        for t in range(TT):
            pool.wait_ge(ln_var.sem, ln_var.count(q, t))
            nc.gpsimd.tensor_tensor(rstd[:, t:t + 1], ve[:, t:t + 1], mhalf[:, 0:1], ALU.pow).then_inc(ln_rstd.sem, 1)

    def gain_count(kind, q):
        return 32 * (q + 1) if kind == "ln" else 32 * 3 * DEPTH + 16 * (q + 1)

    def norm_done(q):
        return lambda pe, t: pe.wait_ge(ln_done.sem, ln_done.count(q, t))


    def cols(k, a, b, rows=slice(0, P)):
        return ws[k][rows, a:b]

    qT = cols(0, 0, 1024).rearrange("p (f s) -> p f s", s=SEQ)
    kT = cols(0, 1024, 1536).rearrange("p (b s) -> p b s", s=SEQ)
    gqT, gkT = cols(0, 1536, 1792), cols(0, 1792, 2048)
    pooledT = cols(1, 0, 512)
    pool_y = cols(1, 512, 1024)
    v_tok = cols(1, 1024, 1536).rearrange("p (t c) -> p t c", c=256)
    u_tok = cols(1, 1536, 2048).rearrange("p (t c) -> p t c", c=256)
    gka = cols(2, 0, 512).rearrange("p (t c) -> p t c", c=256)
    gv = cols(2, 512, 1024).rearrange("p (t c) -> p t c", c=256)
    gr = cols(2, 1536, 2048)
    pool_m = cols(3, 0, 1536).rearrange("p (g s) -> p g s", s=3 * P)
    pool_wt = cols(3, 1536, 1664).rearrange("p (g d) -> p g d", d=64)
    pool_sc = cols(3, 1664, 1666)
    cmp_w1 = cols(4, 0, 2048).rearrange("p (v j o) -> p v j o", v=2, o=64)
    cmp_pe = cols(5, 0, 32).rearrange("p (v j) -> p v j", v=2)
    cmp_w2 = cols(5, 32, 160, slice(0, 64)).rearrange("p (v o) -> p v o", v=2)
    wa2 = cols(5, 160, 288, slice(0, 17))
    gla_g = cols(5, 288, 544)
    head_mask = cols(5, 544, 800)
    blocks = cols(5, 800, 1760).rearrange("p (v j n) -> p v j n", v=2, n=2 * N_CMP)
    gelu_T = cols(5, 1760, 1820, slice(0, 64))
    kcT = cols(5, 1824, 1839)
    vc = cols(5, 1840, 1968, slice(0, N_CMP)).rearrange("p (g d) -> p g d", d=64)
    E1, E2, E3 = cols(8, 0, 256), cols(8, 256, 512), cols(8, 512, 768)
    qtT, ktT = cols(8, 768, 1024), cols(8, 1024, 1280)
    k3 = cols(8, 1280, 1536).rearrange("p (t c) -> p t c", c=P)
    o_gla = cols(8, 1536, 2048)
    att = cols(9, 0, 1024).rearrange("p (t c) -> p t c", c=512)
    S_gla = cols(9, 1024, 2048).rearrange("p (c v) -> p c v", v=256)
    ga_T = cols(6, 0, 256, slice(0, 17))
    absz, la = cols(6, 256, 512), cols(6, 512, 768)
    q_heads = cols(7, 0, 1024).rearrange("p (t c) -> p t c", c=512)
    sq = cols(6, 768, 1280)
    gate = small[:, 66:114].rearrange("p (h b t) -> p h b t", b=3, t=2)
    tanh_g = small[:, 114:162].rearrange("p (t c) -> p t c", c=24)
    ss_gla, rs_gla = small[:, 162:170], small[:, 170:178]
    stat = small[:, 178:226].rearrange("p (r c) -> p r c", c=24)

    MIX_LOADS = 13
    mix_landed = signal("mix_weights_landed", MIX_LOADS)
    mix_set = signal("mix_cleared", 2)
    mix_act = signal("mix_projected_by_act", 6)
    mix_dve = signal("mix_projected_by_dve", 7)
    cmp_pre = signal("compress_hidden", 1)
    cmp_act = signal("compress_gelu", 1)
    cmp_out = signal("compressed", 1)
    cmp_set = signal("compressed_copied", 2)
    ga_turned = signal("decay_input_turned", 1)
    ga_set = signal("decay_input_set", 1)
    la_pre = signal("log_decay_product", 1)
    la_ln = signal("log_decay_logs", 1)
    la_set = signal("log_decay_set", 1)
    b_sum = signal("decay_sums", 1)
    b_exp = signal("decay_exps", 3)
    qk_set = signal("gla_q_k_set", 4)
    gate_tanh = signal("gate_tanh", 1)
    at_done = signal("gla_scores", 2)
    at_set = signal("gla_scores_masked", 2)
    ds_done = signal("gla_state_products", 3)
    s_set = signal("gla_state_set", 3)
    inter = signal("gla_inter_done", 1)
    intra = signal("gla_intra_done", 1)
    inter_set = signal("gla_inter_copied", 1)
    gla_ss = signal("gla_square_sums", 1)
    gla_rs = signal("gla_rms", 1)
    gla_o = signal("gla_output", 1)
    gla_turned = signal("gla_output_turned", 1)
    pool_done = signal("pool_means", 1)
    pool_set = signal("pool_means_set", 1)
    pool_out = signal("pool_output", 1)
    pool_scaled = signal("pool_scaled", 4)
    mixT_hi = signal("mix_hi_set", 4)
    mixT_lo = signal("mix_lo_set", 4)
    scored = signal("nsa_scored", 8)
    peaked = signal("nsa_maxima", 8)
    exped = signal("nsa_exps", 8)
    weighed = signal("nsa_weights", 8)
    p_turned = signal("nsa_weights_turned", 8)
    pT_act = signal("nsa_turned_by_act", 8)
    pT_dve = signal("nsa_turned_by_dve", 8)
    summed = signal("nsa_values_summed", 8)
    HEADS = [f + 4 * g for f in range(4) for g in range(2)]

    def mix_pool(pool, l):
        if l:
            pool.wait_ge(ln_done.sem, ln_done.count(3 * l - 2, TT - 1))
        def load(dst, src):
            pool.dma_start(dst, src).then_inc(mix_landed.sem, 1 * 16)
        load(pool_m[:], w["const_pool"].rearrange("p (g s) -> p g s", s=3 * P))
        load(head_mask, w["const_heads"])
        load(cmp_w1[:, 0, :, :], w["cmp_w1"][l, 0].rearrange("(j p) o -> p j o", p=P))
        load(cmp_w1[:, 1, :, :], w["cmp_w1"][l, 1].rearrange("(j p) o -> p j o", p=P))
        for v in range(2):
            load(cmp_pe[:, v, :], w["cmp_pe"][l, v].rearrange("(j r) d -> (r d) j", r=2))
        load(cmp_w2[:], w["cmp_w2"][l].rearrange("v i o -> i v o"))
        load(wa2[0:16, :], w["gla_wa2"][l])
        load(wa2[16:17, :], w["gla_ba"][l:l + 1, :])
        load(gla_g, w["gla_norm_g"][l:l + 1, :].to_broadcast([P, 256]))
        for r in range(2):
            load(pool_wt[64 * r:64 * r + 64, :, :], w["pool_w"][l].rearrange("(g r) c d -> r c g d", r=2)[r])
        load(pool_sc, w["pool_scale"][l].rearrange("(g p) -> p g", p=P))
        nc.gpsimd.memset(S_gla[:, 0, :], 0.0).then_inc(mix_set.sem, 1)
        nc.gpsimd.memset(ga_T, 1.0).then_inc(mix_set.sem, 1)
        pool.wait_ge(gla_ss.sem, gla_ss.count(l, 0))
        nc.gpsimd.tensor_tensor(rs_gla, ss_gla, mhalf[:, 0:8], ALU.pow).then_inc(gla_rs.sem, 1)

    def mix_tensor(pe, l, xpass):
        n0 = start["mix", l]
        wait_turned(pe, xpass)
        for m in range(11):
            if m == 8:
                pe.wait_ge(mix_act.sem, mix_act.count(l, 0))
            if m == 9:
                pe.wait_ge(mix_act.sem, mix_act.count(l, 1))
            if m == 10:
                pe.wait_ge(mix_dve.sem, mix_dve.count(l, 1))
            if m in (0, 1, 2, 3, 4, 7):
                features_product(pe, n0 + m, m % 8)
            else:
                tokens_product(pe, n0 + m, m % 8, 168 if m == 8 else CW)
        pe.wait_ge(mix_act.sem, mix_act.count(l, 5))
        pe.wait_ge(mix_dve.sem, mix_dve.count(l, 6))
        pe.wait_ge(mix_landed.sem, 16 * MIX_LOADS * (l + 1))
        pe.wait_ge(mix_set.sem, mix_set.count(l, 1))
        for t in range(TT):
            last = nc.tensor.transpose(ps[0:16, 1, t * P:(t + 1) * P], gka[:, t, 152:168], ident)
        last.then_inc(ga_turned.sem, 1)
        for v in range(2):
            for j in range(16):
                last = nc.tensor.matmul(ps[0:64, 0, 64 * v:64 * v + 30], cmp_w1[:, v, j, :], blocks[:, v, j, :],
                                        start=(j == 0), stop=(j == 15))
        last.then_inc(cmp_pre.sem, 1)
        for g in range(4):
            o = ps[64 * (g % 2):64 * (g % 2) + 64, 2, (g // 2) * SEQ:(g // 2 + 1) * SEQ]
            nc.tensor.matmul(o, u_tok[:, 0, 64 * g:64 * g + 64], pool_m[:, g, 0:SEQ], start=True, stop=False)
            last = nc.tensor.matmul(o[:, P:SEQ], u_tok[:, 1, 64 * g:64 * g + 64], pool_m[:, g, SEQ:3 * P], start=False, stop=True)
        last.then_inc(pool_done.sem, 1)
        pe.wait_ge(ga_set.sem, ga_set.count(l, 0))
        for t in range(TT):
            last = nc.tensor.matmul(ps[:, 3, t * P:(t + 1) * P], ga_T[:, t * P:(t + 1) * P], wa2, start=True, stop=True)
        last.then_inc(la_pre.sem, 1)
        pe.wait_ge(cmp_act.sem, cmp_act.count(l, 0))
        for g in range(2):
            nc.tensor.matmul(ps[64 * g:64 * g + 64, 0, 0:N_CMP], cmp_w2[:, 0, :], gelu_T[:, N_CMP * g:N_CMP * (g + 1)],
                             start=True, stop=True)
        for g in range(2):
            last = nc.tensor.matmul(ps[0:N_CMP, 1, 64 * g:64 * g + 64],
                                    gelu_T[:, 30 + N_CMP * g:30 + N_CMP * (g + 1)], cmp_w2[:, 1, :], start=True, stop=True)
        last.then_inc(cmp_out.sem, 1)
        pe.wait_ge(pool_set.sem, pool_set.count(l, 0))
        for g in range(4):
            r = slice(64 * (g % 2), 64 * (g % 2) + 64)
            last = nc.tensor.matmul(ps[r, 6 + g % 2, (g // 2) * SEQ:(g // 2 + 1) * SEQ], pool_wt[r, g // 2, :],
                                    pooledT[r, (g // 2) * SEQ:(g // 2 + 1) * SEQ], start=True, stop=True)
        last.then_inc(pool_out.sem, 1)
        pe.wait_ge(la_set.sem, la_set.count(l, 0))
        for t in range(TT):
            s = slice(t * P, (t + 1) * P)
            nc.tensor.matmul(ps[:, 4, s], la[:, s], consts[:, c_at["upto"]], start=True, stop=True)
            last = nc.tensor.matmul(ps[:, 4, SEQ + t * P:SEQ + (t + 1) * P], consts[:, c_at["after"]], la[:, s],
                                    start=True, stop=True)
        last.then_inc(b_sum.sem, 1)
        for t in range(TT):
            pe.wait_ge(qk_set.sem, qk_set.count(l, 3))
            nc.tensor.matmul(ps[:, 2 + t, :], ktT[:, t * P:(t + 1) * P], q_heads[:, t, :], start=True, stop=True).then_inc(at_done.sem, 1)
        pe.wait_ge(pool_scaled.sem, pool_scaled.count(l, 3))
        for c in range(4):
            if c:
                pe.wait_ge(s_set.sem, s_set.count(l, c - 1))
            r = slice(64 * (c % 2), 64 * (c % 2) + 64)
            last = nc.tensor.matmul(ps[r, 6, (c // 2) * 256:(c // 2 + 1) * 256], qtT[:, 64 * c:64 * c + 64], S_gla[:, c, :],
                                    start=True, stop=True)
            if c < 3:
                nc.tensor.matmul(ps[:, c % 2, 0:256], k3[r, c // 2, :], gv[r, c // 2, :], start=True,
                                 stop=True).then_inc(ds_done.sem, 1)
        last.then_inc(inter.sem, 1)
        for t in range(TT):
            pe.wait_ge(at_set.sem, at_set.count(l, t))
            for h in range(4):
                last = nc.tensor.matmul(ps[:, 7, t * 256 + 64 * h:t * 256 + 64 * h + 64], att[:, t, h * P:(h + 1) * P],
                                        gv[:, t, 64 * h:64 * h + 64], start=True, stop=True)
        last.then_inc(intra.sem, 1)
        pe.wait_ge(gla_o.sem, gla_o.count(l, 0))
        for f in range(2):
            for t in range(TT):
                last = nc.tensor.transpose(ps[:, 4, f * SEQ + t * P:f * SEQ + (t + 1) * P],
                                           o_gla[:, t * 256 + f * P:t * 256 + (f + 1) * P], ident)
        last.then_inc(gla_turned.sem, 1)

        pe.wait_ge(cmp_set.sem, cmp_set.count(l, 1))
        pe.wait_ge(mixT_lo.sem, mixT_lo.count(l, 1))
        def scores(e):
            h = HEADS[e]
            f, g = h % 4, h // 4
            r = slice(64 * g, 64 * g + 64)
            if e >= 2:
                pe.wait_ge(peaked.sem, peaked.count(l, e - 2))
            for b in range(2):
                bank = 2 * (e % 2) + b
                nc.tensor.matmul(ps[:, bank, 0:P], qT[r, f, 0:P], kT[r, b, 0:P], start=True, stop=True)
                last = nc.tensor.matmul(ps[:, bank, P:3 * P], qT[r, f, P:SEQ], kT[r, b, :], start=True, stop=True)
            for t in range(TT):
                last = nc.tensor.matmul(ps[:, 2 * (e % 2), 384 + N_CMP * t:384 + N_CMP * (t + 1)],
                                        qT[r, f, t * P:(t + 1) * P], kcT[r, :], start=True, stop=True)
            last.then_inc(scored.sem, 1)

        def values(e):
            h = HEADS[e]
            f, g = h % 4, h // 4
            E = probs(e)
            pe.wait_ge(weighed.sem, weighed.count(l, e))
            if e:
                pe.wait_ge(pT_act.sem, pT_act.count(l, e - 1))
                pe.wait_ge(pT_dve.sem, pT_dve.count(l, e - 1))
            for b in range(2):
                for q in range(3):
                    nc.tensor.transpose(ps[:, 4 + b, q * P:(q + 1) * P], E[:, 384 * b + q * P:384 * b + (q + 1) * P], ident)
                last = nc.tensor.transpose(ps[0:N_CMP, 4 + b, 384:512], E[:, 768 + N_CMP * b:768 + N_CMP * (b + 1)], ident)
            last.then_inc(p_turned.sem, 1)
            pe.wait_ge(pT_act.sem, pT_act.count(l, e))
            pe.wait_ge(pT_dve.sem, pT_dve.count(l, e))
            T = turned_probs(e)
            o = ps[64 * g:64 * g + 64, 6 + f // 2, (f % 2) * SEQ:(f % 2 + 1) * SEQ]
            for b in range(2):
                nc.tensor.matmul(o, v_tok[:, 0, P * b + 64 * g:P * b + 64 * g + 64], T[:, 384 * b:384 * b + SEQ],
                                 start=(b == 0), stop=False)
                nc.tensor.matmul(o[:, P:SEQ], v_tok[:, 1, P * b + 64 * g:P * b + 64 * g + 64],
                                 T[:, 384 * b + SEQ:384 * b + 384], start=False, stop=False)
            nc.tensor.matmul(o, vc[:, g, :], T[0:N_CMP, 768:768 + SEQ], start=False, stop=True).then_inc(summed.sem, 1)

        for e in range(9):
            if e < 8:
                scores(e)
            if e:
                values(e - 1)
        n1 = start["mix_out", l]
        open_accumulators(pe)
        pair = lambda t, r: t[:, 2 * r:2 * r + 2, :].rearrange("p k s -> p (k s)")
        for r in range(2):
            pe.wait_ge(mixT_lo.sem, mixT_lo.count(l, 2 + r))
            rows_product(pe, n1 + r, pair(aT_hi, r), pair(aT_lo, r))
        last_rows(pe, [(n1 + r, pair(aT_hi, r), pair(aT_lo, r), lambda: pe.wait_ge(mixT_lo.sem, mixT_lo.count(l, 1)))
                       for r in (2, 3)], 3 * l + 1)

    def probs(e):
        return cols(6, 1024 * (e % 2), 1024 * (e % 2) + 800)

    def turned_probs(e):
        return cols(7, 1024 * (e % 2), 1024 * (e % 2) + 1024)

    def mix_scalar(act, l):
        n0 = start["mix", l]
        dst = {0: cols(0, 0, 512), 1: cols(0, 512, 1024), 4: cols(0, 1024, 1536), 6: cols(1, 1536, 2048),
               7: cols(0, 1536, 2048)}
        for m in range(11):
            split_high(act, n0 + m + 3)
            if m in dst or m == 10:
                act.wait_ge(weights_used, n0 + m + 1)
            if m in dst:
                nc.scalar.copy(dst[m], ps[:, m % 8, :]).then_inc(mix_act.sem, 1)
        nc.scalar.activation(gr, ps[:, 2, :], ACT.Silu).then_inc(mix_act.sem, 1)
        act.wait_ge(mix_dve.sem, mix_dve.count(l, 5))
        nc.scalar.activation(tanh_g, gka[:, :, 128:152], ACT.Tanh, scale=0.5).then_inc(gate_tanh.sem, 1)
        act.wait_ge(ga_turned.sem, ga_turned.count(l, 0))
        act.wait_ge(mix_set.sem, mix_set.count(l, 1))
        nc.scalar.copy(ga_T[0:16, :], ps[0:16, 1, 0:SEQ]).then_inc(ga_set.sem, 1)
        act.wait_ge(cmp_pre.sem, cmp_pre.count(l, 0))
        nc.scalar.activation(gelu_T.rearrange("p (v n) -> p v n", v=2),
                             ps[0:64, 0, 0:128].rearrange("p (v n) -> p v n", v=2)[:, :, 0:30],
                             ACT.Gelu_apprx_tanh).then_inc(cmp_act.sem, 1)
        act.wait_ge(pool_done.sem, pool_done.count(l, 0))
        nc.scalar.copy(pooledT, ps[:, 2, :]).then_inc(pool_set.sem, 1)
        ch = Chain(act, act_chain)
        ch.n = act_steps[0]
        act.wait_ge(la_pre.sem, la_pre.count(l, 0))
        ch.link(nc.scalar.activation(absz, ps[:, 3, 0:SEQ], ACT.Abs))
        ch.link(nc.scalar.activation(absz, absz, ACT.Exp, scale=-1.0))
        nc.scalar.activation(absz, absz, ACT.Ln, bias=1.0).then_inc(la_ln.sem, 1)
        act_steps[0] = ch.n
        act.wait_ge(b_sum.sem, b_sum.count(l, 0))
        nc.scalar.activation(E1, ps[:, 4, 0:SEQ], ACT.Exp, scale=1.0 / 16).then_inc(b_exp.sem, 1)
        nc.scalar.activation(E2, ps[:, 4, 0:SEQ], ACT.Exp, scale=-1.0 / 16).then_inc(b_exp.sem, 1)
        nc.scalar.activation(E3, ps[:, 4, SEQ:512], ACT.Exp, scale=1.0 / 16).then_inc(b_exp.sem, 1)
        act.wait_ge(pool_scaled.sem, pool_scaled.count(l, 3))
        nc.scalar.copy(aT_hi[:, 4:6, :], pool_y.rearrange("p (k s) -> p k s", s=SEQ)).then_inc(mixT_hi.sem, 1)
        act.wait_ge(inter.sem, inter.count(l, 0))
        nc.scalar.copy(o_gla, ps[:, 6, :]).then_inc(inter_set.sem, 1)
        act.wait_ge(gla_turned.sem, gla_turned.count(l, 0))
        nc.scalar.copy(aT_hi[:, 6:8, :], ps[:, 4, :].rearrange("p (k s) -> p k s", s=SEQ)).then_inc(mixT_hi.sem, 1)

        def exps(e):
            E, st = probs(e), stat[:, e % 2, :]
            act.wait_ge(peaked.sem, peaked.count(l, e))
            for k, s in enumerate(PART):
                last = nc.scalar.activation(E[:, s], E[:, s], ACT.Exp, bias=st[:, 6 + k:7 + k], scale=0.125,
                                            accum_out=st[:, 12 + k:13 + k])
            last.then_inc(exped.sem, 1)

        def copies(e):
            T = turned_probs(e)
            act.wait_ge(p_turned.sem, p_turned.count(l, e))
            if e >= 2:
                act.wait_ge(summed.sem, summed.count(l, e - 2))
            nc.scalar.copy(T[:, 0:768].rearrange("p (b s) -> p b s", b=2), ps[:, 4:6, 0:384]).then_inc(pT_act.sem, 1)

        for e in range(9):
            if e < 8:
                exps(e)
            if e:
                copies(e - 1)
            if e in (4, 8):
                act.wait_ge(summed.sem, summed.count(l, e - 1))
                a = 0 if e == 4 else 2
                nc.scalar.copy(aT_hi[:, a:a + 2, :], ps[:, 6 + a // 2, :].rearrange("p (k s) -> p k s", s=SEQ)).then_inc(mixT_hi.sem, 1)
        for r in range(2):
            split_high(act, start["mix_out", l] + r + 3)

    PART = [slice(0, P), slice(P, 384), slice(384, 384 + P), slice(384 + P, 768),
            slice(768, 768 + N_CMP), slice(768 + N_CMP, 768 + 2 * N_CMP)]

    def mix_vector(dve, l):
        n0 = start["mix", l]
        ch = Chain(dve, dve_chain)
        ch.n = dve_steps[0]
        for m in range(11):
            split_low(dve, n0 + m + 3)
            if m in (2, 3, 5, 8, 9):
                dve.wait_ge(weights_used, n0 + m + 1)
            if m in (2, 3):
                v = m - 2
                if v == 0:
                    dve.wait_ge(mix_landed.sem, 16 * MIX_LOADS * (l + 1))
                for r in range(2):
                    rows = slice(64 * r, 64 * r + 64)
                    src = window_view(ps[rows, m, :], r)
                    nc.vector.tensor_tensor(
                        blocks[rows, v, :, :].rearrange("p j (g n) -> p j g n", g=2), src,
                        cmp_pe[rows, v, :].unsqueeze(2).unsqueeze(3).to_broadcast([64, 16, 2, N_CMP]),
                        ALU.add).then_inc(mix_dve.sem, 1)
            elif m == 5:
                nc.vector.tensor_copy(cols(1, 1024, 1536), ps[:, 5, :]).then_inc(mix_dve.sem, 1)
            elif m == 8:
                nc.vector.tensor_copy(gka[:, :, 0:168], ps[:, 0, :].rearrange("p (t c) -> p t c", t=2)[:, :, 0:168]).then_inc(mix_dve.sem, 1)
            elif m == 9:
                nc.vector.tensor_copy(cols(2, 512, 1024), ps[:, 1, :]).then_inc(mix_dve.sem, 1)
        dve.wait_ge(gate_tanh.sem, gate_tanh.count(l, 0))
        tg = tanh_g.rearrange("p t (h b) -> p h b t", b=3)
        for k, b in enumerate((1, 2, 0)):
            m = ch.mark(nc.vector.tensor_scalar(gate[:, :, k, :], tg[:, :, b, :], 0.5, 0.5, ALU.mult, ALU.add))
        ch.wait(m)
        ch.link(nc.vector.tensor_tensor(gate[:, :, 2, :], gate[:, :, 2, :],
                                        consts[:, c_at["has_cmp"]].unsqueeze(1).to_broadcast([P, 8, 2]), ALU.mult))
        dve.wait_ge(la_ln.sem, la_ln.count(l, 0))
        nc.vector.scalar_tensor_tensor(out=la, in0=ps[:, 3, 0:SEQ], scalar=0.0, in1=absz, op0=ALU.min,
                                       op1=ALU.subtract).then_inc(la_set.sem, 1)
        dve.wait_ge(cmp_out.sem, cmp_out.count(l, 0))
        nc.vector.tensor_copy(kcT, ps[:, 0, 0:N_CMP]).then_inc(cmp_set.sem, 1)
        nc.vector.tensor_copy(vc.rearrange("p g d -> p (g d)"), ps[0:N_CMP, 1, 0:P]).then_inc(cmp_set.sem, 1)
        dve.wait_ge(pool_out.sem, pool_out.count(l, 0))
        for g in range(4):
            r = slice(64 * (g % 2), 64 * (g % 2) + 64)
            c = slice((g // 2) * SEQ, (g // 2 + 1) * SEQ)
            nc.vector.tensor_scalar(pool_y[r, c], ps[r, 6 + g % 2, c], pool_sc[r, g // 2:g // 2 + 1], None,
                                    ALU.mult).then_inc(pool_scaled.sem, 1)
        dve.wait_ge(b_exp.sem, b_exp.count(l, 0))
        nc.vector.scalar_tensor_tensor(out=qtT, in0=gqT, scalar=32.0 ** -0.5, in1=E1, op0=ALU.mult,
                                       op1=ALU.mult).then_inc(qk_set.sem, 1)
        dve.wait_ge(qk_set.sem, qk_set.count(l, 0))
        for t in range(TT):
            m = ch.mark(nc.vector.tensor_tensor(
                q_heads[:, t, :].rearrange("p (h s) -> p h s", h=4),
                qtT[:, t * P:(t + 1) * P].unsqueeze(1).to_broadcast([P, 4, P]),
                head_mask.rearrange("p (h v) -> p h v", h=4)[:, :, 0:1].to_broadcast([P, 4, P]), ALU.mult))
        dve.wait_ge(b_exp.sem, b_exp.count(l, 1))
        nc.vector.tensor_tensor(ktT, gkT, E2, ALU.mult).then_inc(qk_set.sem, 1)
        dve.wait_ge(b_exp.sem, b_exp.count(l, 2))
        nc.vector.tensor_tensor(k3[:], gka[:, :, 0:P], E3.rearrange("p (t c) -> p t c", c=P), ALU.mult).then_inc(qk_set.sem, 1)
        ch.wait(m)
        dve.wait_ge(mixT_hi.sem, mixT_hi.count(l, 0))
        nc.vector.tensor_tensor(aT_lo[:, 4:6, :], pool_y.rearrange("p (k s) -> p k s", s=SEQ),
                                aT_hi[:, 4:6, :].bitcast(F32), ALU.subtract).then_inc(mixT_lo.sem, 1)
        nc.vector.memset(stat[:, 0, 18:24], 0.0).then_inc(qk_set.sem, 1)
        for t in range(TT):
            dve.wait_ge(at_done.sem, at_done.count(l, t))
            nc.vector.tensor_tensor(att[:, t, :].rearrange("p (h s) -> p h s", h=4),
                                    ps[:, 2 + t, :].rearrange("p (h s) -> p h s", h=4),
                                    consts[:, c_at["upto"]].unsqueeze(1).to_broadcast([P, 4, P]),
                                    ALU.mult).then_inc(at_set.sem, 1)
        for c in range(3):
            dve.wait_ge(ds_done.sem, ds_done.count(l, c))
            ch.link(nc.vector.tensor_tensor(sq[:, 0:256], ps[:, c % 2, 0:256], head_mask, ALU.mult))
            if c:
                dve.wait_ge(s_set.sem, s_set.count(l, c - 1))
            else:
                dve.wait_ge(mix_set.sem, mix_set.count(l, 0))
            nc.vector.scalar_tensor_tensor(out=S_gla[:, c + 1, :], in0=S_gla[:, c, :], scalar=E1[:, 64 * c + 63:64 * c + 64],
                                           in1=sq[:, 0:256], op0=ALU.mult, op1=ALU.add).then_inc(s_set.sem, 1)
        dve.wait_ge(s_set.sem, s_set.count(l, 2))
        dve.wait_ge(inter_set.sem, inter_set.count(l, 0))
        dve.wait_ge(intra.sem, intra.count(l, 0))
        ch.link(nc.vector.tensor_tensor(o_gla, o_gla, ps[:, 7, :], ALU.add))
        ch.link(nc.vector.tensor_tensor(sq, o_gla, o_gla, ALU.mult))
        ch.link(nc.vector.tensor_reduce(ss_gla, sq.rearrange("p (h v) -> p h v", v=64), AX.X, ALU.add))
        nc.vector.tensor_scalar(ss_gla, ss_gla, 1.0 / 64, RMS_EPS, ALU.mult, ALU.add).then_inc(gla_ss.sem, 1)
        ch.link(nc.vector.tensor_tensor(o_gla.rearrange("p (t c) -> p t c", t=2), o_gla.rearrange("p (t c) -> p t c", t=2),
                                        gla_g.unsqueeze(1).to_broadcast([P, 2, 256]), ALU.mult))
        ch.link(nc.vector.tensor_tensor(o_gla, o_gla, gr, ALU.mult))
        dve.wait_ge(gla_rs.sem, gla_rs.count(l, 0))
        oh = o_gla.rearrange("p (h v) -> p h v", v=64)
        nc.vector.tensor_tensor(oh, oh, rs_gla.unsqueeze(2).to_broadcast([P, 8, 64]), ALU.mult).then_inc(gla_o.sem, 1)
        dve.wait_ge(mixT_hi.sem, mixT_hi.count(l, 1))
        nc.vector.tensor_tensor(aT_lo[:, 6:8, :], ps[:, 4, :].rearrange("p (k s) -> p k s", s=SEQ),
                                aT_hi[:, 6:8, :].bitcast(F32), ALU.subtract).then_inc(mixT_lo.sem, 1)

        causal, cmpm = consts[:, c_at["causal"]], consts[:, c_at["cmp_mask"]]

        def peaks(e):
            E, st = probs(e), stat[:, e % 2, :]
            b0 = 2 * (e % 2)
            dve.wait_ge(scored.sem, scored.count(l, e))
            if e >= 2:
                dve.wait_ge(p_turned.sem, p_turned.count(l, e - 2))
            src = [ps[:, b0, 0:P], ps[:, b0, P:384], ps[:, b0 + 1, 0:P], ps[:, b0 + 1, P:384],
                   ps[:, b0, 384:384 + N_CMP], ps[:, b0, 384 + N_CMP:384 + 2 * N_CMP]]
            mask = [causal[:, 0:P], causal[:, P:384]] * 2 + [cmpm[:, 0:N_CMP], cmpm[:, N_CMP:2 * N_CMP]]
            for k in range(6):
                m = ch.mark(nc.vector.tensor_tensor_reduce(out=E[:, PART[k]], in0=src[k], in1=mask[k], scale=1.0,
                                                           scalar=-3.0e38, op0=ALU.add, op1=ALU.max,
                                                           accum_out=st[:, k:k + 1]))
            ch.wait(m)
            nc.vector.tensor_scalar(st[:, 6:12], st[:, 0:6], -0.125, None, ALU.mult).then_inc(peaked.sem, 1)

        def weights(e):
            E, st, h = probs(e), stat[:, e % 2, :], HEADS[e]
            dve.wait_ge(exped.sem, exped.count(l, e))
            ch.link(nc.vector.reciprocal(st[:, 18:24], st[:, 12:18]))
            ch.link(nc.vector.tensor_tensor(st[:, 18:24], st[:, 18:24], gate[:, h, :, :].rearrange("p b t -> p (b t)"), ALU.mult))
            for k, s in enumerate(PART):
                last = nc.vector.tensor_scalar(E[:, s], E[:, s], st[:, 18 + k:19 + k], None, ALU.mult)
                if k < 5:
                    ch.mark(last)
            last.then_inc(weighed.sem, 1)

        def copies(e):
            T = turned_probs(e)
            dve.wait_ge(pT_act.sem, pT_act.count(l, e))
            nc.vector.tensor_copy(T[0:N_CMP, 768:1024].rearrange("p (b s) -> p b s", b=2), ps[0:N_CMP, 4:6, 384:512]).then_inc(pT_dve.sem, 1)

        for e in range(9):
            if e < 8:
                peaks(e)
            if e:
                copies(e - 1)
            if e < 8:
                weights(e)
            if e in (4, 8):
                a = 0 if e == 4 else 2
                dve.wait_ge(mixT_hi.sem, mixT_hi.count(l, 2 + a // 2))
                nc.vector.tensor_tensor(aT_lo[:, a:a + 2, :], ps[:, 6 + a // 2, :].rearrange("p (k s) -> p k s", s=SEQ),
                                        aT_hi[:, a:a + 2, :].bitcast(F32), ALU.subtract).then_inc(mixT_lo.sem, 1)
        dve_steps[0] = ch.n
        for r in range(2):
            split_low(dve, start["mix_out", l] + r + 3)

    def window_view(bank, r):
        base = bank[:, r:r + 1]
        return bass.AP(base.tensor, base.offset, [base.ap[0], [2, 16], [SEQ, 2], [CMP_STRIDE, N_CMP]])


    H = Z
    M = ws[9].rearrange("p (t c) -> p t c", c=D)
    junk = ws[1].rearrange("p (t c) -> p t c", c=D)
    pre_g = ws[7][:, 0:D]
    diag = ws[7][:, D:D + 2 * P].rearrange("p (t s) -> p t s", t=TT)
    ss2, ve2, rs2 = small[:, 226:228], small[:, 228:230], small[:, 230:232]
    ss3, ve3, rs3 = small[:, 232:236], small[:, 236:238], small[:, 238:240]
    ROOT_D = 32.0
    assert ROOT_D ** 2 == D

    pre_gain = signal("prenorm_gain_landed", 1)
    pre_sq = signal("prenorm_squares", TT)
    pre_rs = signal("prenorm_rsqrt", TT)
    pre_done = signal("prenorm_done", TT)
    add_gain = signal("addnorm_gain_landed", 1)
    add_sq = signal("addnorm_squares", 4)
    add_var = signal("addnorm_mean_square", TT)
    add_rs = signal("addnorm_rsqrt", TT)
    add_done = signal("addnorm_done", TT)

    def wait_x(eng, q, t):
        if q:
            eng.wait_ge(add_done.sem, add_done.count(q - 1, t))
        else:
            eng.wait_ge(ln_done.sem, ln_done.count(3 * DEPTH - 1, t))

    def prenorm_scalar(act, q):
        for t in range(TT):
            wait_x(act, q, t)
            nc.scalar.activation(junk[:, t, :], x[:, t, :], ACT.Square, accum_out=ss2[:, t:t + 1]).then_inc(pre_sq.sem, 1)

    def scaled_x(dve, q, t):
        wait_x(dve, q, t)
        if t == 0:
            dve.wait_ge(pre_gain.sem, 16 * (q + 1))
        nc.vector.scalar_tensor_tensor(out=H[:, t, :], in0=x[:, t, :], scalar=ROOT_D, in1=pre_g, op0=ALU.mult, op1=ALU.mult)

    def token_factors(dve, q, t):
        dve.wait_ge(pre_rs.sem, pre_rs.count(q, t))
        nc.vector.tensor_scalar(diag[:, t, :], ident, rs2[:, t:t + 1], None, ALU.mult).then_inc(pre_done.sem, 1)

    def load_pre_gain(pool, q):
        if q % 2:
            pool.wait_ge(out_set.sem, out_set.count(q // 2, TT - 1))
        elif q:
            pool.wait_ge(pre_done.sem, pre_done.count(q - 1, TT - 1))
        pool.dma_start(pre_g, w["norm_g_2"][q // 2, 2 * (q % 2):2 * (q % 2) + 1, :].to_broadcast([P, D])).then_inc(pre_gain.sem, 16)

    def prenorm_pool(pool, q):
        for t in range(TT):
            pool.wait_ge(pre_sq.sem, pre_sq.count(q, t))
            nc.gpsimd.tensor_tensor(ve2[:, t:t + 1], ss2[:, t:t + 1], eps_d, ALU.add).then_inc(pool_chain, 1)
            pool_steps[0] += 1
            pool.wait_ge(pool_chain, pool_steps[0])
            nc.gpsimd.tensor_tensor(rs2[:, t:t + 1], ve2[:, t:t + 1], mhalf[:, 0:1], ALU.pow).then_inc(pre_rs.sem, 1)

    def prenorm_is_done(q):
        return lambda pe, t: pe.wait_ge(pre_done.sem, pre_done.count(q, t))

    def addnorm_scalar(act, a):
        for b in range(4):
            wait_y(act, 3 * DEPTH + a, b, add_last[a])
            nc.scalar.activation(junk[:, b // 2, b % 2 * 512:b % 2 * 512 + 512], ps[:, b, :], ACT.Square,
                                 accum_out=ss3[:, b:b + 1]).then_inc(add_sq.sem, 1)

    def addnorm_vector(dve, a):
        ch = Chain(dve, dve_chain)
        ch.n = dve_steps[0]
        following = a + 1 < 2 * DEPTH_2
        dve.wait_ge(add_gain.sem, 16 * (a + 1))
        for t in range(TT):
            for half in range(2):
                b, c = 2 * t + half, slice(512 * half, 512 * half + 512)
                dve.wait_ge(add_sq.sem, add_sq.count(a, b))
                if half:
                    nc.vector.scalar_tensor_tensor(out=ve3[:, t:t + 1], in0=ss3[:, b - 1:b], scalar=D * RMS_EPS, in1=ss3[:, b:b + 1],
                                                   op0=ALU.add, op1=ALU.add).then_inc(add_var.sem, 1)
                m = ch.mark(nc.vector.scalar_tensor_tensor(out=Z[:, t, c], in0=ps[:, b, :], scalar=ROOT_D, in1=gb[:, 1, c],
                                                           op0=ALU.mult, op1=ALU.mult))
            ch.wait(m)
            dve.wait_ge(add_rs.sem, add_rs.count(a, t))
            nc.vector.scalar_tensor_tensor(out=x[:, t, :], in0=Z[:, t, :], scalar=rs3[:, t:t + 1], in1=x[:, t, :],
                                           op0=ALU.mult, op1=ALU.add).then_inc(add_done.sem, 1)
            if following:
                scaled_x(dve, a + 1, t)
                if t:
                    token_factors(dve, a + 1, 0)
                    token_factors(dve, a + 1, 1)
        dve_steps[0] = ch.n

    def prenorm_vector(dve, q):
        if q == 0:
            for t in range(TT):
                scaled_x(dve, q, t)
            for t in range(TT):
                token_factors(dve, q, t)

    def addnorm_pool(pool, a):
        if a:
            pool.wait_ge(add_done.sem, add_done.count(a - 1, TT - 1))
        pool.dma_start(gb[:, 1, :], w["norm_g_2"][a // 2, 1 + 2 * (a % 2):2 + 2 * (a % 2), :].to_broadcast([P, D])).then_inc(add_gain.sem, 16)
        if a + 1 < 2 * DEPTH_2:
            load_pre_gain(pool, a + 1)
        for t in range(TT):
            pool.wait_ge(add_var.sem, add_var.count(a, t))
            nc.gpsimd.tensor_tensor(rs3[:, t:t + 1], ve3[:, t:t + 1], mhalf[:, 0:1], ALU.pow).then_inc(add_rs.sem, 1)

    add_last = []
    for i in range(DEPTH_2):
        add_last += [start["out", i] + 3, start["mlp", i] + 2 * MLP_STEPS - 1]


    HN = 8
    param = gb[:, 0, :]
    m_landed = semaphore("mixer_parameters_landed")
    out_ss = signal("mixer_head_squares", 1)
    out_rs = signal("mixer_head_rsqrt", 1)
    out_set = signal("mixer_output_set", TT)
    ss_h, rs_h = small[:, 240:256], small[:, 256:272]
    M4 = ws[9].rearrange("p (t h v) -> p t h v", t=TT, v=P)

    def head_norm_vector(dve, i, ch, factors):
        sqs = ws[8].rearrange("p (h v) -> p h v", v=P)
        flat = ws[9].rearrange("p (h v) -> p h v", v=P)
        ch.link(nc.vector.tensor_tensor(sqs, flat, flat, ALU.mult))
        ch.link(nc.vector.tensor_reduce(ss_h, sqs, AX.X, ALU.add))
        nc.vector.tensor_scalar(ss_h, ss_h, 1.0 / P, RMS_EPS, ALU.mult, ALU.add).then_inc(out_ss.sem, 1)
        for fac in factors:
            ch.link(nc.vector.tensor_tensor(M4, M4, fac, ALU.mult))
        dve.wait_ge(out_rs.sem, out_rs.count(i, 0))
        for t in range(TT):
            nc.vector.tensor_tensor(M4[:, t, :, :], M4[:, t, :, :],
                                    rs_h[:, HN * t:HN * (t + 1)].unsqueeze(2).to_broadcast([P, HN, P]),
                                    ALU.mult).then_inc(out_set.sem, 1)

    def head_norm_pool(pool, i):
        pool.wait_ge(out_ss.sem, out_ss.count(i, 0))
        nc.gpsimd.tensor_tensor(rs_h, ss_h, mhalf[:, 0:16], ALU.pow).then_inc(out_rs.sem, 1)

    def out_tensor(pe, i, xpass):
        turn_tensor(pe, xpass, M, lambda pe, t: pe.wait_ge(out_set.sem, out_set.count(i, t)))
        open_accumulators(pe)
        pair = lambda t, r: t[:, 2 * r:2 * r + 2, :].rearrange("p k s -> p (k s)")
        first, second = (lambda k=k: pe.wait_ge(aT_lo_set.sem, aT_lo_set.count(xpass, k)) for k in (2, 3))
        first()
        for r in range(2):
            rows_product(pe, start["out", i] + r, pair(aT_hi, r), pair(aT_lo, r))
        last_rows(pe, [(start["out", i] + r, pair(aT_hi, r), pair(aT_lo, r), second) for r in (2, 3)], 3 * DEPTH + 2 * i)

    def out_scalar(act, i, xpass):
        turn_scalar(act, xpass)
        for r in range(2):
            split_high(act, start["out", i] + r + 3)

    def out_vector(dve, i, xpass):
        turn_vector(dve, xpass)
        for r in range(2):
            split_low(dve, start["out", i] + r + 3)

    
    loads_before = [0, 5, 8, 11]

    def loader(pool):
        def load(dst, src):
            pool.dma_start(dst, src).then_inc(m_landed, 16)
        return load

    def wait_params(eng, i):
        eng.wait_ge(m_landed, 16 * (loads_before + [16])[i + 1])

    def mixer_pool(pool, i):
        pool.wait_ge(pre_done.sem, pre_done.count(2 * i, TT - 1))
        (gdn_pool, mlstm_pool, diff_pool)[i % 3](pool, i)
        head_norm_pool(pool, i)

    def mixer_tensor(pe, i, xpass, xpass_out):
        wait_turned(pe, xpass)
        (gdn_tensor, mlstm_tensor, diff_tensor)[i % 3](pe, i)
        out_tensor(pe, i, xpass_out)

    def mixer_scalar(act, i, xpass_out):
        ch = Chain(act, act_chain)
        ch.n = act_steps[0]
        (gdn_scalar, mlstm_scalar, diff_scalar)[i % 3](act, i, ch)
        act_steps[0] = ch.n
        out_scalar(act, i, xpass_out)

    def mixer_vector(dve, i, xpass_out):
        ch = Chain(dve, dve_chain)
        ch.n = dve_steps[0]
        (gdn_vector, mlstm_vector, diff_vector)[i % 3](dve, i, ch)
        dve_steps[0] = ch.n
        out_vector(dve, i, xpass_out)


    qT4 = cols(0, 0, 1024).rearrange("p (f s) -> p f s", s=SEQ)
    kT4 = cols(0, 1024, 2048).rearrange("p (f s) -> p f s", s=SEQ)
    v8 = ws[4].rearrange("p (t c) -> p t c", c=D)
    og = ws[5].rearrange("p (t c) -> p t c", c=D)
    tri = param[:, 0:P]
    gate_b = param[:, P:P + 16]
    ml_gain = ws[3][:, 0:D]
    raw_g = small[:, 272:304].rearrange("p (t c) -> p t c", c=16)
    lnf = small[:, 304:320].rearrange("p (t h) -> p t h", h=HN)
    absf = small[:, 320:336].rearrange("p (t h) -> p t h", h=HN)
    Bsum = small[:, 336:352].rearrange("p (t h) -> p t h", h=HN)
    cgate = small[:, 352:368].rearrange("p (t h) -> p t h", h=HN)
    ml_st = small[:, 368:400].rearrange("p (r c) -> p r c", c=16)

    ml_pre = signal("mlstm_gate_biased", 1)
    ml_tanh = signal("mlstm_gate_tanh", 1)
    ml_cap = signal("mlstm_gate_capped", 1)
    ml_ln = signal("mlstm_log_set", 1)
    ml_lf = signal("mlstm_log_forget", 1)
    ml_B = signal("mlstm_running_sum", 1)
    ml_c = signal("mlstm_key_bias", 1)
    ml_act = signal("mlstm_projected_by_act", 8)
    ml_dve = signal("mlstm_projected_by_dve", 4)
    taken = signal("values_taken", HN)

    def mlstm_pool(pool, i):
        load = loader(pool)
        load(tri, w["const_tri"])
        load(gate_b, w["mlstm_gate_b_2"].rearrange("n a h -> n (a h)").to_broadcast([P, 16]))
        load(ml_gain, w["mlstm_norm_g_2"].to_broadcast([P, D]))

    def mlstm_tensor(pe, i):
        n0 = start["in", i]
        tokens_product(pe, n0, 7, 16)
        for m in range(1, 13):
            if m > 4:
                e = m - 4
                if e <= 4:
                    pe.wait_ge(ml_act.sem, ml_act.count(0, e - 1))
                else:
                    pe.wait_ge(ml_dve.sem, ml_dve.count(0, e - 5))
            if m <= 4:
                features_product(pe, n0 + m, (m - 1) % 4)
            else:
                tokens_product(pe, n0 + m, (m - 1) % 4)
        wait_params(pe, i)
        pe.wait_ge(ml_lf.sem, 1)
        for t in range(TT):
            o = ps[:, 6, HN * t:HN * (t + 1)]
            if t:
                nc.tensor.matmul(o, tri[:, P - 1:P].to_broadcast([P, P]), lnf[:, 0, :], start=True, stop=False)
            last = nc.tensor.matmul(o, tri, lnf[:, t, :], start=(t == 0), stop=True)
        last.then_inc(ml_B.sem, 1)
        pe.wait_ge(ml_c.sem, 1)
        pe.wait_ge(ml_act.sem, ml_act.count(0, 7))

        def scores(h):
            r = slice(64 * (h % 2), 64 * (h % 2) + 64)
            if h >= 2:
                pe.wait_ge(weighed.sem, weighed.count(2, h - 2))
            b = h % 2
            nc.tensor.matmul(ps[:, b, 0:P], qT4[r, h // 2, 0:P], kT4[r, h // 2, 0:P], start=True, stop=True)
            nc.tensor.matmul(ps[:, b, P:384], qT4[r, h // 2, P:SEQ], kT4[r, h // 2, :], start=True, stop=True)
            for t in range(TT):
                last = nc.tensor.matmul(ps[:, 2 + b, t * P:(t + 1) * P], cgate[:, t, h:h + 1].to_broadcast([P, P]),
                                        ident, start=True, stop=True)
            last.then_inc(scored.sem, 1)

        for h in range(HN + 1):
            if h < HN:
                scores(h)
            if h:
                pe.wait_ge(weighed.sem, weighed.count(2, h - 1))
                weighted_values(pe, h - 1, 0)

    def weighted_values(pe, h, turn):
        b = h % 2
        E = head_probs(h)
        if h >= 2:
            pe.wait_ge(pT_act.sem, pT_act.count(DEPTH + turn, h - 2))
        for q in range(3):
            last = nc.tensor.transpose(ps[:, 4 + b, q * P:(q + 1) * P], E[:, q * P:(q + 1) * P], ident)
        last.then_inc(p_turned.sem, 1)
        T = head_turned(h)
        pe.wait_ge(pT_act.sem, pT_act.count(DEPTH + turn, h))
        if h >= 2:
            pe.wait_ge(taken.sem, taken.count(turn, h - 2))
        v = slice(h * P, (h + 1) * P)
        nc.tensor.matmul(ps[:, 6 + b, 0:P], T[:, 0:P], v8[:, 0, v], start=True, stop=True)
        nc.tensor.matmul(ps[:, 6 + b, P:SEQ], T[:, P:SEQ], v8[:, 0, v], start=True, stop=False)
        nc.tensor.matmul(ps[:, 6 + b, P:SEQ], T[:, SEQ:384], v8[:, 1, v], start=False, stop=True).then_inc(summed.sem, 1)

    def head_probs(h):
        return cols(6, 1024 * (h % 2), 1024 * (h % 2) + 768)

    def head_turned(h):
        return cols(7, 512 * (h % 2), 512 * (h % 2) + 384)

    def mlstm_scalar(act, i, ch):
        n0 = start["in", i]
        split_high(act, n0 + 3)
        act.wait_ge(ml_pre.sem, 1)
        nc.scalar.activation(raw_g[:], raw_g[:], ACT.Tanh, scale=1.0 / 15).then_inc(ml_tanh.sem, 1)
        for m in range(1, 13):
            split_high(act, n0 + m + 3)
            b = (m - 1) % 4
            if m <= 4:
                act.wait_ge(weights_used, n0 + m + 1)
                dst = cols(0, 512 * (m - 1), 512 * m)
                nc.scalar.copy(dst, ps[:, b, :]).then_inc(ml_act.sem, 1)
            elif m >= 9:
                act.wait_ge(weights_used, n0 + m + 1)
                c = slice(CW * (m - 9), CW * (m - 8))
                nc.scalar.activation(og[:, :, c], ps[:, b, :].rearrange("p (t c) -> p t c", t=TT), ACT.Tanh, scale=0.5).then_inc(ml_act.sem, 1)
        act.wait_ge(ml_cap.sem, 1)
        ch.link(nc.scalar.activation(absf[:], raw_g[:, :, 8:16], ACT.Abs))
        ch.link(nc.scalar.activation(absf[:], absf[:], ACT.Exp, scale=-1.0))
        nc.scalar.activation(absf[:], absf[:], ACT.Ln, bias=1.0).then_inc(ml_ln.sem, 1)

        def copies(h):
            act.wait_ge(p_turned.sem, p_turned.count(2, h))
            if h >= 2:
                act.wait_ge(summed.sem, summed.count(2, h - 2))
            nc.scalar.copy(head_turned(h), ps[:, 4 + h % 2, 0:384]).then_inc(pT_act.sem, 1)

        for h in range(HN + 1):
            if h < HN:
                st, E = ml_st[:, h % 2, :], cols(6, 1024 * (h % 2) + 512, 1024 * (h % 2) + 896)
                act.wait_ge(peaked.sem, peaked.count(2, h))
                nc.scalar.activation(E[:, 0:P], E[:, 0:P], ACT.Exp, bias=st[:, 2:3])
                nc.scalar.activation(E[:, P:384], E[:, P:384], ACT.Exp, bias=st[:, 3:4])
                nc.scalar.activation(st[:, 4:6], st[:, 4:6], ACT.Exp).then_inc(exped.sem, 1)
            if h:
                copies(h - 1)

    def mlstm_vector(dve, i, ch):
        n0 = start["in", i]
        split_low(dve, n0 + 3)
        wait_params(dve, i)
        dve.wait_ge(weights_used, n0 + 1)
        nc.vector.tensor_tensor(raw_g[:], ps[:, 7, :].rearrange("p (t c) -> p t c", t=TT)[:, :, 0:16],
                                gate_b.unsqueeze(1).to_broadcast([P, TT, 16]), ALU.add).then_inc(ml_pre.sem, 1)
        for m in range(1, 13):
            split_low(dve, n0 + m + 3)
            if 5 <= m <= 8:
                dve.wait_ge(weights_used, n0 + m + 1)
                c = slice(CW * (m - 5), CW * (m - 4))
                nc.vector.tensor_copy(v8[:, :, c], ps[:, (m - 1) % 4, :].rearrange("p (t c) -> p t c", t=TT)).then_inc(ml_dve.sem, 1)
        dve.wait_ge(ml_tanh.sem, 1)
        nc.vector.tensor_scalar(raw_g[:], raw_g[:], 15.0, None, ALU.mult).then_inc(ml_cap.sem, 1)
        dve.wait_ge(ml_act.sem, ml_act.count(0, 7))
        ch.link(nc.vector.tensor_scalar(og[:], og[:], 0.5, 0.5, ALU.mult, ALU.add))
        ch.link(nc.vector.tensor_tensor(og[:], og[:], ml_gain.unsqueeze(1).to_broadcast([P, TT, D]), ALU.mult))
        dve.wait_ge(ml_ln.sem, 1)
        dve.wait_ge(ml_cap.sem, 1)
        nc.vector.scalar_tensor_tensor(out=lnf[:], in0=raw_g[:, :, 8:16], scalar=0.0, in1=absf[:], op0=ALU.min,
                                       op1=ALU.subtract).then_inc(ml_lf.sem, 1)
        dve.wait_ge(ml_B.sem, 1)
        m = ch.mark(nc.vector.tensor_copy(Bsum[:], ps[:, 6, 0:16].rearrange("p (t h) -> p t h", h=HN)))
        nc.vector.tensor_tensor(cgate[:], raw_g[:, :, 0:8], ps[:, 6, 0:16].rearrange("p (t h) -> p t h", h=HN),
                                ALU.subtract).then_inc(ml_c.sem, 1)
        ch.wait(m)
        causal = consts[:, c_at["causal"]]

        def peaks(h):
            st, b = ml_st[:, h % 2, :], h % 2
            E = cols(6, 1024 * b + 512, 1024 * b + 896)
            dve.wait_ge(scored.sem, scored.count(2, h))
            ch.mark(nc.vector.tensor_tensor_reduce(out=E[:, 0:P], in0=ps[:, 2 + b, 0:P], in1=causal[:, 0:P], scale=1.0,
                                                   scalar=-3.0e38, op0=ALU.add, op1=ALU.max, accum_out=st[:, 0:1]))
            ch.link(nc.vector.tensor_tensor_reduce(out=E[:, P:384], in0=ps[:, 2 + b, 0:SEQ], in1=causal[:, P:384], scale=1.0,
                                                   scalar=-3.0e38, op0=ALU.add, op1=ALU.max, accum_out=st[:, 1:2]))
            ch.link(nc.vector.tensor_scalar(st[:, 2:4], st[:, 0:2], 0.0, -1.0, ALU.max, ALU.mult))
            nc.vector.tensor_tensor(st[:, 4:6], st[:, 2:4], Bsum[:, :, h], ALU.subtract).then_inc(peaked.sem, 1)

        def weights(h):
            st, b = ml_st[:, h % 2, :], h % 2
            E, Pw = cols(6, 1024 * b + 512, 1024 * b + 896), head_probs(h)
            dve.wait_ge(exped.sem, exped.count(2, h))
            if h >= 2:
                dve.wait_ge(p_turned.sem, p_turned.count(2, h - 2))
            ch.mark(nc.vector.tensor_tensor_reduce(out=Pw[:, 0:P], in0=ps[:, b, 0:P], in1=E[:, 0:P], scale=0.125, scalar=0.0,
                                                   op0=ALU.mult, op1=ALU.add, accum_out=st[:, 6:7]))
            nc.vector.tensor_tensor_reduce(out=Pw[:, P:384], in0=ps[:, b, P:384], in1=E[:, P:384], scale=0.125, scalar=0.0,
                                           op0=ALU.mult, op1=ALU.add, accum_out=st[:, 7:8]).then_inc(weighed.sem, 1)
            dve.wait_ge(weighed.sem, weighed.count(2, h))
            ch.link(nc.vector.scalar_tensor_tensor(out=st[:, 8:10], in0=st[:, 6:8], scalar=-1.0, in1=st[:, 6:8],
                                                   op0=ALU.mult, op1=ALU.max))
            ch.link(nc.vector.tensor_tensor(st[:, 8:10], st[:, 8:10], st[:, 4:6], ALU.max))
            ch.link(nc.vector.reciprocal(st[:, 10:12], st[:, 8:10]))

        def scaled(h):
            st, b = ml_st[:, h % 2, :], h % 2
            dve.wait_ge(summed.sem, summed.count(2, h))
            ch.mark(nc.vector.tensor_scalar(M4[:, 0, h, :], ps[:, 6 + b, 0:P], st[:, 10:11], None, ALU.mult))
            nc.vector.tensor_scalar(M4[:, 1, h, :], ps[:, 6 + b, P:SEQ], st[:, 11:12], None, ALU.mult).then_inc(taken.sem, 1)

        for h in range(HN + 1):
            if h < HN:
                peaks(h)
                weights(h)
            if h:
                scaled(h - 1)
        dve.wait_ge(taken.sem, taken.count(0, HN - 1))
        head_norm_vector(dve, i, ch, [og.rearrange("p t (h v) -> p t h v", v=P)])


    q_tok = ws[1].rearrange("p (t h c) -> p t h c", t=TT, c=64)
    k_tok = ws[3].rearrange("p (t h c) -> p t h c", t=TT, c=64)
    qT8 = ws[0].rearrange("p (f s) -> p f s", s=SEQ)
    kT8 = ws[2].rearrange("p (f s) -> p f s", s=SEQ)
    rope = param[:, 0:2 * ROT].rearrange("p (t a c) -> p t a c", t=TT, a=2)
    lam_p = param[:, 32:288]
    df_gain = param[:, 288:416]
    chunk_mask = param[:, 416:800]
    rt = ws[8].rearrange("p (k t h c) -> p k t h c", k=8, t=TT, c=8)
    df_st = small[:, 400:480].rearrange("p (r c) -> p r c", c=40)
    lam = small[:, 480:488]
    LAMBDA_INIT = 0.8 - 0.6 * math.exp(-0.3 * 2)

    df_act = signal("diff_projected_by_act", 12)
    df_rot = signal("diff_rotated", 2)
    df_turned = signal("diff_qk_turned", 8)
    df_tcopy = signal("diff_qk_turned_copied", 8)
    df_lam = signal("diff_lambda_sums", 1)
    df_lexp = signal("diff_lambda_exps", 1)

    def diff_pool(pool, i):
        load = loader(pool)
        load(param[:, 0:2 * ROT], w["const_rope"])
        load(lam_p, w["diff_lambda_2"].rearrange("n a d -> n (a d)").to_broadcast([P, 256]))
        load(chunk_mask, w["const_chunks"])

    def diff_gain_scalar(act):
        act.dma_start(df_gain, w["diff_norm_g_2"].to_broadcast([P, P])).then_inc(df_gain_landed, 16)

    df_gain_landed = semaphore("diff_gain_landed")

    def diff_tensor(pe, i):
        n0 = start["in", i]
        for m in range(12):
            if m >= 4:
                pe.wait_ge(df_act.sem, df_act.count(0, m - 4))
            tokens_product(pe, n0 + m, m % 4)
        for v, src in ((0, ws[1]), (1, ws[3])):
            pe.wait_ge(df_rot.sem, df_rot.count(0, v))
            for b in range(4):
                if v:
                    pe.wait_ge(df_tcopy.sem, df_tcopy.count(0, b))
                for a in range(2):
                    for t in range(TT):
                        f = 2 * b + a
                        last = nc.tensor.transpose(ps[:, 4 + b, a * SEQ + t * P:a * SEQ + (t + 1) * P],
                                                   src[:, t * D + f * P:t * D + (f + 1) * P], ident)
                last.then_inc(df_turned.sem, 1)
        pe.wait_ge(df_tcopy.sem, df_tcopy.count(0, 7))
        pe.wait_ge(df_act.sem, df_act.count(0, 11))

        def scores(h):
            if h >= 2:
                pe.wait_ge(peaked.sem, peaked.count(3, h - 2))
            for c in range(2):
                r, b = slice(64 * c, 64 * c + 64), 2 * (h % 2) + c
                nc.tensor.matmul(ps[:, b, 0:P], qT8[r, h, 0:P], kT8[r, h, 0:P], start=True, stop=True)
                last = nc.tensor.matmul(ps[:, b, P:384], qT8[r, h, P:SEQ], kT8[r, h, :], start=True, stop=True)
            last.then_inc(scored.sem, 1)

        for h in range(HN + 1):
            if h < HN:
                scores(h)
            if h:
                pe.wait_ge(weighed.sem, weighed.count(3, h - 1))
                weighted_values(pe, h - 1, 1)

    def diff_scalar(act, i, ch):
        n0 = start["in", i]
        act.wait_ge(pre_done.sem, pre_done.count(2 * i, TT - 1))
        diff_gain_scalar(act)
        dst = [ws[1], ws[3], ws[4]]
        for m in range(12):
            split_high(act, n0 + m + 3)
            act.wait_ge(weights_used, n0 + m + 1)
            c = slice(CW * (m % 4), CW * (m % 4 + 1))
            nc.scalar.copy(dst[m // 4].rearrange("p (t c) -> p t c", c=D)[:, :, c],
                           ps[:, m % 4, :].rearrange("p (t c) -> p t c", t=TT)).then_inc(df_act.sem, 1)
        act.wait_ge(df_lam.sem, 1)
        nc.scalar.activation(lam[:, 2:4], lam[:, 0:2], ACT.Exp).then_inc(df_lexp.sem, 1)
        for b in range(8):
            act.wait_ge(df_turned.sem, df_turned.count(0, b))
            nc.scalar.copy((qT8, kT8)[b // 4][:, 2 * (b % 4):2 * (b % 4) + 2, :],
                           ps[:, 4 + b % 4, :].rearrange("p (a s) -> p a s", a=2)).then_inc(df_tcopy.sem, 1)
        for h in range(HN + 1):
            if h < HN:
                st, E = df_st[:, h % 2, :], head_probs(h)
                act.wait_ge(peaked.sem, peaked.count(3, h))
                for k, s in enumerate(DIFF_PART):
                    last = nc.scalar.activation(E[:, s], E[:, s], ACT.Exp, bias=st[:, 4 + k:5 + k], scale=0.125,
                                                accum_out=st[:, 8 + k:9 + k])
                last.then_inc(exped.sem, 1)
            if h:
                act.wait_ge(p_turned.sem, p_turned.count(3, h - 1))
                if h >= 3:
                    act.wait_ge(summed.sem, summed.count(3, h - 3))
                nc.scalar.copy(head_turned(h - 1), ps[:, 4 + (h - 1) % 2, 0:384]).then_inc(pT_act.sem, 1)
                act.wait_ge(summed.sem, summed.count(3, h - 1))
                nc.scalar.copy(M4[:, :, h - 1, :], ps[:, 6 + (h - 1) % 2, 0:SEQ].rearrange("p (t v) -> p t v", t=TT)).then_inc(taken.sem, 1)

    DIFF_PART = [slice(0, P), slice(P, 384), slice(384, 512), slice(512, 768)]

    def diff_vector(dve, i, ch):
        n0 = start["in", i]
        wait_params(dve, i)
        ch.link(nc.vector.tensor_tensor_reduce(out=rt[:, 7, 0, :, :].rearrange("p h c -> p (h c)")[:, 0:64], in0=lam_p[:, 0:64],
                                               in1=lam_p[:, 64:128], scale=1.0, scalar=0.0, op0=ALU.mult, op1=ALU.add,
                                               accum_out=lam[:, 0:1]))
        nc.vector.tensor_tensor_reduce(out=rt[:, 7, 1, :, :].rearrange("p h c -> p (h c)")[:, 0:64], in0=lam_p[:, 128:192],
                                       in1=lam_p[:, 192:256], scale=1.0, scalar=0.0, op0=ALU.mult, op1=ALU.add,
                                       accum_out=lam[:, 1:2]).then_inc(df_lam.sem, 1)

        def rotate(v, tok):
            x1, x2 = tok[:, :, :, 0:8], tok[:, :, :, 8:16]
            cs = [rope[:, :, a, :].unsqueeze(2).to_broadcast([P, TT, 16, 8]) for a in range(2)]
            k0 = 0
            marks = []
            for k, (a, b) in enumerate(((x1, cs[0]), (x2, cs[1]), (x1, cs[1]), (x2, cs[0]))):
                for t in range(TT):
                    marks.append(ch.mark(nc.vector.tensor_tensor(rt[:, k0 + k, t, :, :], a[:, t], b[:, t], ALU.mult)))
            ch.wait()
            for t in range(TT):
                ch.mark(nc.vector.tensor_tensor(x1[:, t], rt[:, k0, t], rt[:, k0 + 1, t], ALU.subtract))
                last = nc.vector.tensor_tensor(x2[:, t], rt[:, k0 + 2, t], rt[:, k0 + 3, t], ALU.add)
                if t == 0:
                    ch.mark(last)
            last.then_inc(df_rot.sem, 1)
            dve.wait_ge(df_rot.sem, df_rot.count(0, v))

        for m in range(12):
            split_low(dve, n0 + m + 3)
            if m in (5, 9):
                dve.wait_ge(df_act.sem, df_act.count(0, m - 2))
                rotate(m // 8, (q_tok, k_tok)[m // 8])
        dve.wait_ge(df_lexp.sem, 1)
        ch.link(nc.vector.tensor_tensor(lam[:, 4:5], lam[:, 3:4], lam[:, 2:3], ALU.subtract))
        ch.link(nc.vector.tensor_scalar(lam[:, 5:6], lam[:, 4:5], LAMBDA_INIT, None, ALU.subtract))

        def peaks(h):
            E, st, b0 = head_probs(h), df_st[:, h % 2, :], 2 * (h % 2)
            dve.wait_ge(scored.sem, scored.count(3, h))
            if h >= 2:
                dve.wait_ge(p_turned.sem, p_turned.count(3, h - 2))
            for k, s in enumerate(DIFF_PART):
                c = (slice(0, P), slice(P, 384))[k % 2]
                ch.mark(nc.vector.tensor_tensor_reduce(out=E[:, s], in0=ps[:, b0 + k // 2, c], in1=chunk_mask[:, c], scale=1.0,
                                                       scalar=-3.0e38, op0=ALU.add, op1=ALU.max, accum_out=st[:, k:k + 1]))
            ch.wait()
            nc.vector.tensor_scalar(st[:, 4:8], st[:, 0:4], -0.125, None, ALU.mult).then_inc(peaked.sem, 1)

        def weights(h):
            E, st = head_probs(h), df_st[:, h % 2, :]
            dve.wait_ge(exped.sem, exped.count(3, h))
            ch.link(nc.vector.reciprocal(st[:, 12:16], st[:, 8:12]))
            ch.link(nc.vector.tensor_scalar(st[:, 14:16], st[:, 14:16], lam[:, 5:6], None, ALU.mult))
            for t in range(TT):
                ch.mark(nc.vector.tensor_scalar(E[:, DIFF_PART[2 + t]], E[:, DIFF_PART[2 + t]], st[:, 14 + t:15 + t], None, ALU.mult))
            ch.wait()
            for t in range(TT):
                last = nc.vector.scalar_tensor_tensor(out=E[:, DIFF_PART[t]], in0=E[:, DIFF_PART[t]], scalar=st[:, 12 + t:13 + t],
                                                      in1=E[:, DIFF_PART[2 + t]], op0=ALU.mult, op1=ALU.add)
                if t == 0:
                    ch.mark(last)
            last.then_inc(weighed.sem, 1)

        for h in range(HN):
            peaks(h)
            weights(h)
        dve.wait_ge(df_gain_landed, 16)
        ch.link(nc.vector.tensor_scalar(df_gain, df_gain, 1.0 - LAMBDA_INIT, None, ALU.mult))
        dve.wait_ge(taken.sem, taken.count(1, HN - 1))
        head_norm_vector(dve, i, ch, [df_gain.unsqueeze(1).unsqueeze(1).to_broadcast([P, TT, HN, P])])


    g_qT = ws[0].rearrange("p (f s) -> p f s", s=SEQ)
    g_kT = ws[1].rearrange("p (f s) -> p f s", s=SEQ)
    g_vT = ws[9].rearrange("p (f s) -> p f s", s=SEQ)
    g_kbT = ws[8].rearrange("p (f s) -> p f s", s=SEQ)

    def by_head(k):
        return ws[k].rearrange("p (t h v) -> p t h v", t=TT, v=P)

    g_kb, g_k, g_v, g_z, g_dec, g_A, g_Y, g_T, g_TT = (by_head(k) for k in (2, 3, 4, 5, 6, 7, 1, 8, 9))
    g_value, g_kcdT, g_S2 = by_head(1), by_head(7), ws[8].rearrange("p (r c) -> p r c", r=2)
    g_Sd = ws[2][:, 0:D]
    levels = param[:, 0:LEVELS * P].rearrange("p (v s) -> p v s", s=P)
    g_gain = param[:, 768:896]
    conv_rows = param[0:96, 896:1024]
    conv_w = small[:, 488:584].rearrange("p (j f) -> p j f", j=4)
    a_log, dt_b = small[:, 584:592], small[:, 592:600]
    th = lambda k: small[:, 272 + 16 * k:288 + 16 * k].rearrange("p (t h) -> p t h", h=HN)
    g_g, g_ln, g_beta, g_gc, g_eg, g_es, g_brk, g_rkes = (th(k) for k in range(8))
    g_el = small[:, 400:432].rearrange("p (c h) -> p c h", h=HN)
    g_r = small[:, 432:464].rearrange("p (a t h) -> p a t h", a=2, h=HN)
    g_ea = small[:, 464:472]

    gp = lambda name, per: signal("gdn_" + name, per)
    gd_cwT, gd_cw = gp("taps_turned", 1), gp("taps_set", 1)
    gd_u, gd_lnset, gd_tb, gd_g = gp("decay_input", 1), gp("decay_logs", 1), gp("beta_tanh", 1), gp("log_decay", 1)
    gd_tap0, gd_conv, gd_silu = gp("first_tap", 12), gp("convolved", 12), gp("activated", 12)
    gd_z = gp("output_gate", 4)
    gd_sums, gd_sexp, gd_rows, gd_D, gd_Dexp, gd_dec = (gp("chunk_sums", 1), gp("chunk_exps", 3), gp("sum_rows", 4),
                                                        gp("differences", 4), gp("decays", 4), gp("decays_masked", 4))
    gd_sq, gd_ss, gd_ssx, gd_r = gp("squares", 2), gp("square_sums", 1), gp("square_sums_set", 1), gp("norms", 1)
    gd_kt, gd_kc, gd_vt, gd_vc = gp("k_turned", 4), gp("k_copied", 4), gp("v_turned", 4), gp("v_scaled", 4)
    gd_kb, gd_kbt, gd_kbc = gp("beta_k", 4), gp("beta_k_turned", 4), gp("beta_k_copied", 4)
    gd_a, gd_as, gd_at, gd_ats = gp("a_product", 4), gp("a_set", 4), gp("attn_product", 4), gp("attn_set", 4)
    gd_kbe, gd_kst = gp("beta_k_decayed", 4), gp("state_keys", 4)
    inv_y, inv_ys, inv_z, inv_t = (gp("inverse_right", 4 * LEVELS), gp("inverse_right_set", 4 * LEVELS),
                                   gp("inverse_both", 4 * LEVELS), gp("inverse_set", 4 * LEVELS))
    gd_val, gd_vals, gd_kcd, gd_kcds = gp("values", 4), gp("values_set", 4), gp("state_reads", 4), gp("state_reads_set", 4)
    gd_p1, gd_vn, gd_p2, gd_S = gp("read_of_state", 3), gp("new_values", 3), gp("state_gain", 3), gp("state", 3)
    gd_o1, gd_o1t, gd_o2, gd_o2t = gp("state_output", 3), gp("state_output_taken", 3), gp("chunk_output", 2), gp("chunk_output_taken", 2)

    UNITS = [(t, half) for t in range(TT) for half in range(2)]

    def gdn_pool(pool, i):
        j = i // 3
        load = loader(pool)
        load(levels[:], w["const_levels"].rearrange("p (v s) -> p v s", s=P))
        load(conv_rows, w["gdn_conv_2"][j].rearrange("j (f c) -> (j f) c", c=P))
        load(g_gain, w["gdn_norm_g_2"][j:j + 1, :].to_broadcast([P, P]))
        load(a_log, w["gdn_a_log_2"][j:j + 1, :].to_broadcast([P, HN]))
        load(dt_b, w["gdn_dt_bias_2"][j:j + 1, :].to_broadcast([P, HN]))
        pool.wait_ge(gd_ssx.sem, gd_ssx.count(j, 0))
        flat = small[:, 432:464]
        nc.gpsimd.tensor_tensor(flat, flat, mhalf[:, 0:32], ALU.pow).then_inc(gd_r.sem, 1)

    def gdn_tensor(pe, i):
        j, n0 = i // 3, start["in", i]
        wait_params(pe, i)
        tokens_product(pe, n0, 3, GDN_AB)
        nc.tensor.transpose(ps[:, 7, 0:96], conv_rows, ident[0:96, 0:96]).then_inc(gd_cwT.sem, 1)
        upto, after = consts[:, c_at["upto"]], consts[:, c_at["after"]]
        for m in range(1, 17):
            if m >= 4:
                s, e = (gd_conv, m - 4) if m - 3 <= 12 else (gd_z, m - 16)
                pe.wait_ge(s.sem, s.count(j, e))
            if m <= 12:
                features_product(pe, n0 + m, (m - 1) % 3)
            else:
                tokens_product(pe, n0 + m, (m - 1) % 3)
            if m == 3:
                pe.wait_ge(gd_g.sem, gd_g.count(j, 0))
                pe.wait_ge(gd_tb.sem, gd_tb.count(j, 0))
                for t in range(TT):
                    nc.tensor.matmul(ps[:, 3, 8 * t:8 * t + 8], upto, g_g[:, t, :], start=True, stop=True)
                    nc.tensor.matmul(ps[:, 3, 16 + 8 * t:24 + 8 * t], after, g_g[:, t, :], start=True, stop=True)
                    for c in range(2):
                        e = 32 + 8 * (2 * t + c)
                        last = nc.tensor.matmul(ps[:, 3, e:e + 8], upto[:, 64 * c + 63:64 * c + 64].to_broadcast([P, P]),
                                                g_g[:, t, :], start=True, stop=True)
                last.then_inc(gd_sums.sem, 1)
                pe.wait_ge(gd_cw.sem, gd_cw.count(j, 0))
                for u, (t, half) in enumerate(UNITS):
                    for q in range(4):
                        h = 4 * half + q
                        last = nc.tensor.matmul(ps[:, 4 + u, q * P:(q + 1) * P], g_g[:, t, h:h + 1].to_broadcast([P, P]), upto,
                                                start=True, stop=True)
                    last.then_inc(gd_rows.sem, 1)
            if m == 13:
                pe.wait_ge(gd_sq.sem, gd_sq.count(j, 1))
                pe.wait_ge(gd_sexp.sem, gd_sexp.count(j, 2))
                for a, sqT in ((0, g_kbT), (1, ws[7].rearrange("p (f s) -> p f s", s=SEQ))):
                    for t in range(TT):
                        for h in range(HN):
                            e = 64 + 16 * a + 8 * t + h
                            last = nc.tensor.matmul(ps[:, 3, e:e + 1], sqT[:, h, t * P:(t + 1) * P], ones[:], start=True, stop=True)
                last.then_inc(gd_ss.sem, 1)
                for u, (t, half) in enumerate(UNITS):
                    pe.wait_ge(gd_D.sem, gd_D.count(j, u))
                    for q in range(4):
                        last = nc.tensor.transpose(ps[:, 4 + u, q * P:(q + 1) * P], g_kT[:, 4 * half + q, t * P:(t + 1) * P], ident)
                    last.then_inc(gd_kt.sem, 1)
        for u, (t, half) in enumerate(UNITS):
            pe.wait_ge(gd_kc.sem, gd_kc.count(j, u))
            if u == 0:
                pe.wait_ge(gd_silu.sem, gd_silu.count(j, 11))
            for q in range(4):
                last = nc.tensor.transpose(ps[:, 4 + u, q * P:(q + 1) * P], g_vT[:, 4 * half + q, t * P:(t + 1) * P], ident)
            last.then_inc(gd_vt.sem, 1)
        pe.wait_ge(gd_kb.sem, gd_kb.count(j, 3))
        pe.wait_ge(gd_z.sem, gd_z.count(j, 3))
        for b in range(4):
            for a in range(2):
                for t in range(TT):
                    last = nc.tensor.transpose(ps[:, b, a * SEQ + t * P:a * SEQ + (t + 1) * P], g_kb[:, t, 2 * b + a, :], ident)
            last.then_inc(gd_kbt.sem, 1)
        pe.wait_ge(gd_kbc.sem, gd_kbc.count(j, 3))
        for u, (t, half) in enumerate(UNITS):
            pe.wait_ge(gd_vc.sem, gd_vc.count(j, u))
            s = slice(t * P, (t + 1) * P)
            for q in range(4):
                h = 4 * half + q
                last = nc.tensor.matmul(ps[:, 4 + u, q * P:(q + 1) * P], g_kT[:, h, s], g_kbT[:, h, s], start=True, stop=True)
            last.then_inc(gd_a.sem, 1)
        for u, (t, half) in enumerate(UNITS):
            s = slice(t * P, (t + 1) * P)
            for q in range(4):
                h = 4 * half + q
                last = nc.tensor.matmul(ps[:, u, q * P:(q + 1) * P], g_kT[:, h, s], g_qT[:, h, s], start=True, stop=True)
            last.then_inc(gd_at.sem, 1)
        for v in range(LEVELS):
            for u, (t, half) in enumerate(UNITS):
                if v:
                    pe.wait_ge(inv_t.sem, inv_t.count(j, 4 * (v - 1) + u))
                else:
                    pe.wait_ge(gd_ats.sem, gd_ats.count(j, u))
                for q in range(4):
                    h = 4 * half + q
                    last = nc.tensor.matmul(ps[:, u, q * P:(q + 1) * P], g_A[:, t, h, :], g_T[:, t, h, :] if v else ident,
                                            start=True, stop=True)
                last.then_inc(inv_y.sem, 1)
            for u, (t, half) in enumerate(UNITS):
                pe.wait_ge(inv_ys.sem, inv_ys.count(j, 4 * v + u))
                for q in range(4):
                    h = 4 * half + q
                    if 0 < v < LEVELS - 1:
                        nc.tensor.matmul(ps[:, u, q * P:(q + 1) * P], g_TT[:, t, h, :], g_Y[:, t, h, :], start=True, stop=True)
                    last = nc.tensor.matmul(ps[:, 4 + u, q * P:(q + 1) * P], g_Y[:, t, h, :], g_TT[:, t, h, :] if v else ident,
                                            start=True, stop=True)
                last.then_inc(inv_z.sem, 1)
        for u, (t, half) in enumerate(UNITS):
            pe.wait_ge(inv_t.sem, inv_t.count(j, 4 * (LEVELS - 1) + u))
            pe.wait_ge(gd_kbe.sem, gd_kbe.count(j, 3))
            for q in range(4):
                h = 4 * half + q
                last = nc.tensor.matmul(ps[:, u, q * P:(q + 1) * P], g_TT[:, t, h, :], g_v[:, t, h, :], start=True, stop=True)
            last.then_inc(gd_val.sem, 1)
            for q in range(4):
                h = 4 * half + q
                last = nc.tensor.matmul(ps[:, 4 + u, q * P:(q + 1) * P], g_kb[:, t, h, :], g_TT[:, t, h, :], start=True, stop=True)
            last.then_inc(gd_kcd.sem, 1)
        pe.wait_ge(gd_vals.sem, gd_vals.count(j, 3))
        pe.wait_ge(gd_kcds.sem, gd_kcds.count(j, 3))
        pe.wait_ge(gd_kst.sem, gd_kst.count(j, 3))

        def bank_of(b, h):
            return ps[:, b + h // 4, (h % 4) * P:(h % 4 + 1) * P]

        for c in range(4):
            t, r, s = c // 2, slice(64 * (c % 2), 64 * (c % 2) + 64), slice(64 * c, 64 * c + 64)
            if c:
                S = g_S2[:, c % 2, :]
                pe.wait_ge(gd_S.sem, gd_S.count(j, c - 1))
                for h in range(HN):
                    last = nc.tensor.matmul(bank_of(0, h)[r, :], g_kcdT[:, t, h, r], S[:, h * P:(h + 1) * P], start=True, stop=True)
                last.then_inc(gd_p1.sem, 1)
                if c > 1:
                    pe.wait_ge(gd_o1t.sem, gd_o1t.count(j, c - 2))
                for h in range(HN):
                    last = nc.tensor.matmul(bank_of(2, h)[r, :], g_qT[:, h, s], S[:, h * P:(h + 1) * P], start=True, stop=True)
                last.then_inc(gd_o1.sem, 1)
                pe.wait_ge(gd_vn.sem, gd_vn.count(j, c - 1))
            if c < 3:
                for h in range(HN):
                    last = nc.tensor.matmul(bank_of(4, h), g_k[r, t, h, :], g_value[r, t, h, :], start=True, stop=True)
                last.then_inc(gd_p2.sem, 1)
            if c % 2:
                if t:
                    pe.wait_ge(gd_o2t.sem, gd_o2t.count(j, 0))
                for h in range(HN):
                    last = nc.tensor.matmul(bank_of(6, h), g_dec[:, t, h, :], g_value[:, t, h, :], start=True, stop=True)
                last.then_inc(gd_o2.sem, 1)

    def conv_dst(m):
        buf = (g_qT, g_kT, g_vT)[(m - 1) // 4]
        f = 2 * ((m - 1) % 4)
        return buf[:, f:f + 2, :]

    def gdn_scalar(act, i, ch):
        j, n0 = i // 3, start["in", i]
        split_high(act, n0 + 3)
        wait_params(act, i)
        act.wait_ge(weights_used, n0 + 1)
        act.wait_ge(gd_u.sem, gd_u.count(j, 0))
        nc.scalar.activation(g_beta[:], ps[:, 3, :].rearrange("p (t c) -> p t c", t=TT)[:, :, 8:16], ACT.Tanh, scale=0.5).then_inc(gd_tb.sem, 1)
        ch.link(nc.scalar.activation(g_ea, a_log, ACT.Exp))
        ch.link(nc.scalar.activation(g_ln[:], g_g[:], ACT.Abs))
        ch.link(nc.scalar.activation(g_ln[:], g_ln[:], ACT.Exp, scale=-1.0))
        nc.scalar.activation(g_ln[:], g_ln[:], ACT.Ln, bias=1.0).then_inc(gd_lnset.sem, 1)

        def activate(m):
            act.wait_ge(gd_conv.sem, gd_conv.count(j, m - 1))
            nc.scalar.activation(conv_dst(m), conv_dst(m), ACT.Silu).then_inc(gd_silu.sem, 1)

        act.wait_ge(gd_cw.sem, gd_cw.count(j, 0))
        for m in range(1, 17):
            split_high(act, n0 + m + 3)
            act.wait_ge(weights_used, n0 + m + 1)
            b = (m - 1) % 3
            if m <= 12:
                for a in range(2):
                    f = 2 * (m - 1) + a
                    last = nc.scalar.activation(conv_dst(m)[:, a, :], ps[:, b, a * SEQ:(a + 1) * SEQ], ACT.Copy,
                                                scale=conv_w[:, 3, f:f + 1])
                last.then_inc(gd_tap0.sem, 1)
            else:
                c = slice(2 * (m - 13), 2 * (m - 12))
                nc.scalar.activation(g_z[:, :, c, :], ps[:, b, :].rearrange("p (t h v) -> p t h v", t=TT, v=P), ACT.Silu).then_inc(gd_z.sem, 1)
            if 2 <= m <= 13:
                activate(m - 1)
            if m == 4:
                act.wait_ge(gd_sums.sem, gd_sums.count(j, 0))
                for k, (dst, c) in enumerate(((g_eg, 0), (g_es, 16))):
                    nc.scalar.activation(dst[:], ps[:, 3, c:c + 16].rearrange("p (t h) -> p t h", h=HN), ACT.Exp).then_inc(gd_sexp.sem, 1)
                nc.scalar.activation(g_el[:], ps[:, 3, 32:64].rearrange("p (c h) -> p c h", h=HN), ACT.Exp).then_inc(gd_sexp.sem, 1)
                for u, (t, half) in enumerate(UNITS):
                    act.wait_ge(gd_D.sem, gd_D.count(j, u))
                    d = g_dec[:, t, 4 * half:4 * half + 4, :]
                    nc.scalar.activation(d, d, ACT.Exp).then_inc(gd_Dexp.sem, 1)
            if m in (6, 10):
                src, dst = ((ws[0], ws[8]), (ws[1], ws[7]))[m == 10]
                act.wait_ge(gd_silu.sem, gd_silu.count(j, 3 if m == 6 else 7))
                nc.scalar.activation(dst[:], src[:], ACT.Square).then_inc(gd_sq.sem, 1)
        for u, (t, half) in enumerate(UNITS):
            act.wait_ge(gd_kt.sem, gd_kt.count(j, u))
            nc.scalar.copy(g_k[:, t, 4 * half:4 * half + 4, :], ps[:, 4 + u, :].rearrange("p (h v) -> p h v", v=P)).then_inc(gd_kc.sem, 1)
        act.wait_ge(gd_ss.sem, gd_ss.count(j, 0))
        for b in range(4):
            act.wait_ge(gd_kbt.sem, gd_kbt.count(j, b))
            nc.scalar.copy(g_kbT[:, 2 * b:2 * b + 2, :], ps[:, b, :].rearrange("p (a s) -> p a s", a=2)).then_inc(gd_kbc.sem, 1)
        for u, (t, half) in enumerate(UNITS):
            act.wait_ge(gd_val.sem, gd_val.count(j, u))
            nc.scalar.copy(g_value[:, t, 4 * half:4 * half + 4, :], ps[:, u, :].rearrange("p (h v) -> p h v", v=P)).then_inc(gd_vals.sem, 1)

    def gdn_vector(dve, i, ch):
        j, n0 = i // 3, start["in", i]
        upto = consts[:, c_at["upto"]]
        four = lambda s: s.unsqueeze(2).to_broadcast([P, 4, P])
        eight = lambda s, n=P: s.unsqueeze(2).to_broadcast([n, HN, P])
        split_low(dve, n0 + 3)
        wait_params(dve, i)
        dve.wait_ge(weights_used, n0 + 1)
        nc.vector.tensor_tensor(g_g[:], ps[:, 3, :].rearrange("p (t c) -> p t c", t=TT)[:, :, 0:8],
                                dt_b.unsqueeze(1).to_broadcast([P, TT, HN]), ALU.add).then_inc(gd_u.sem, 1)
        dve.wait_ge(gd_cwT.sem, gd_cwT.count(j, 0))
        nc.vector.tensor_copy(conv_w[:], ps[:, 7, 0:96].rearrange("p (j f) -> p j f", j=4)).then_inc(gd_cw.sem, 1)
        dve.wait_ge(gd_lnset.sem, gd_lnset.count(j, 0))
        ch.link(nc.vector.scalar_tensor_tensor(out=g_g[:], in0=g_g[:], scalar=0.0, in1=g_ln[:], op0=ALU.max, op1=ALU.add))
        nc.vector.scalar_tensor_tensor(out=g_g[:], in0=g_g[:], scalar=-1.0, in1=g_ea.unsqueeze(1).to_broadcast([P, TT, HN]),
                                       op0=ALU.mult, op1=ALU.mult).then_inc(gd_g.sem, 1)
        dve.wait_ge(gd_tb.sem, gd_tb.count(j, 0))
        ch.link(nc.vector.tensor_scalar(g_beta[:], g_beta[:], 0.5, 0.5, ALU.mult, ALU.add))
        dve.wait_ge(gd_cw.sem, gd_cw.count(j, 0))
        for m in range(1, 17):
            split_low(dve, n0 + m + 3)
            b = (m - 1) % 3
            if m <= 12:
                dve.wait_ge(gd_tap0.sem, gd_tap0.count(j, m - 1))
                for s in range(1, 4):
                    for a in range(2):
                        f, d = 2 * (m - 1) + a, conv_dst(m)[:, a, s:SEQ]
                        last = nc.vector.scalar_tensor_tensor(out=d, in0=ps[:, b, a * SEQ:(a + 1) * SEQ - s],
                                                              scalar=conv_w[:, 3 - s, f:f + 1], in1=d, op0=ALU.mult, op1=ALU.add)
                        if not (s == 3 and a == 1):
                            ch.mark(last)
                    if s < 3:
                        ch.wait()
                last.then_inc(gd_conv.sem, 1)
            if m == 4:
                dve.wait_ge(gd_sexp.sem, gd_sexp.count(j, 2))
                ch.link(nc.vector.tensor_copy(g_gc[:], ps[:, 3, 0:16].rearrange("p (t h) -> p t h", h=HN)))
                for u, (t, half) in enumerate(UNITS):
                    dve.wait_ge(gd_rows.sem, gd_rows.count(j, u))
                    for q in range(4):
                        h = 4 * half + q
                        last = nc.vector.tensor_scalar(g_dec[:, t, h, :], ps[:, 4 + u, q * P:(q + 1) * P], g_gc[:, t, h:h + 1],
                                                       0.0, ALU.subtract, ALU.min)
                    last.then_inc(gd_D.sem, 1)
        dve.wait_ge(gd_ss.sem, gd_ss.count(j, 0))
        nc.vector.tensor_scalar(small[:, 432:464], ps[:, 3, 64:96], RMS_EPS, None, ALU.add).then_inc(gd_ssx.sem, 1)
        dve.wait_ge(gd_z.sem, gd_z.count(j, 3))
        ch.mark(nc.vector.tensor_tensor(g_z[:], g_z[:], g_gain.unsqueeze(1).unsqueeze(1).to_broadcast([P, TT, HN, P]), ALU.mult))
        for u, (t, half) in enumerate(UNITS):
            hs = slice(4 * half, 4 * half + 4)
            dve.wait_ge(gd_vt.sem, gd_vt.count(j, u))
            nc.vector.tensor_tensor(g_v[:, t, hs, :], ps[:, 4 + u, :].rearrange("p (h v) -> p h v", v=P), four(g_beta[:, t, hs]),
                                    ALU.mult).then_inc(gd_vc.sem, 1)
        dve.wait_ge(gd_r.sem, gd_r.count(j, 0))
        rq, rk = g_r[:, 0, :, :], g_r[:, 1, :, :]
        ch.mark(nc.vector.tensor_scalar(rq, rq, float(P) ** -0.5, None, ALU.mult))
        ch.mark(nc.vector.tensor_tensor(g_brk[:], g_beta[:], rk, ALU.mult))
        dve.wait_ge(gd_sexp.sem, gd_sexp.count(j, 1))
        ch.mark(nc.vector.tensor_tensor(g_rkes[:], g_es[:], rk, ALU.mult))
        ch.wait()
        for u, (t, half) in enumerate(UNITS):
            hs = slice(4 * half, 4 * half + 4)
            dve.wait_ge(gd_kc.sem, gd_kc.count(j, u))
            nc.vector.tensor_tensor(g_kb[:, t, hs, :], g_k[:, t, hs, :], four(g_brk[:, t, hs]), ALU.mult).then_inc(gd_kb.sem, 1)
        for u, (t, half) in enumerate(UNITS):
            dve.wait_ge(gd_Dexp.sem, gd_Dexp.count(j, u))
            for q in range(4):
                h = 4 * half + q
                last = nc.vector.scalar_tensor_tensor(out=g_dec[:, t, h, :], in0=g_dec[:, t, h, :], scalar=rk[:, t, h:h + 1],
                                                      in1=upto, op0=ALU.mult, op1=ALU.mult)
            last.then_inc(gd_dec.sem, 1)
        for u, (t, half) in enumerate(UNITS):
            hs = slice(4 * half, 4 * half + 4)
            dve.wait_ge(gd_dec.sem, gd_dec.count(j, u))
            dve.wait_ge(gd_a.sem, gd_a.count(j, u))
            nc.vector.tensor_tensor(g_A[:, t, hs, :], ps[:, 4 + u, :].rearrange("p (h v) -> p h v", v=P), g_dec[:, t, hs, :],
                                    ALU.mult).then_inc(gd_as.sem, 1)
        for u, (t, half) in enumerate(UNITS):
            hs = slice(4 * half, 4 * half + 4)
            dve.wait_ge(gd_at.sem, gd_at.count(j, u))
            if u == 0:
                dve.wait_ge(gd_as.sem, gd_as.count(j, 3))
            nc.vector.tensor_tensor(g_dec[:, t, hs, :], ps[:, u, :].rearrange("p (h v) -> p h v", v=P), g_dec[:, t, hs, :],
                                    ALU.mult).then_inc(gd_ats.sem, 1)
        bc = lambda m: m.unsqueeze(1).to_broadcast([P, 4, P])
        for v in range(LEVELS):
            for u, (t, half) in enumerate(UNITS):
                hs = slice(4 * half, 4 * half + 4)
                dve.wait_ge(inv_y.sem, inv_y.count(j, 4 * v + u))
                nc.vector.tensor_tensor(g_Y[:, t, hs, :], ps[:, u, :].rearrange("p (h v) -> p h v", v=P), bc(levels[:, v, :]),
                                        ALU.mult).then_inc(inv_ys.sem, 1)
                if v == 0:
                    nc.vector.tensor_tensor(g_kb[:, t, hs, :], g_kb[:, t, hs, :], four(g_eg[:, t, hs]), ALU.mult).then_inc(gd_kbe.sem, 1)
                    nc.vector.tensor_tensor(g_k[:, t, hs, :], g_k[:, t, hs, :], four(g_rkes[:, t, hs]), ALU.mult).then_inc(gd_kst.sem, 1)
            for u, (t, half) in enumerate(UNITS):
                hs = slice(4 * half, 4 * half + 4)
                if v == 0:
                    dve.wait_ge(inv_ys.sem, inv_ys.count(j, u))
                    ch.mark(nc.vector.tensor_tensor(g_T[:, t, hs, :], bc(ident), g_Y[:, t, hs, :], ALU.subtract))
                dve.wait_ge(inv_z.sem, inv_z.count(j, 4 * v + u))
                if 0 < v < LEVELS - 1:
                    ch.mark(nc.vector.tensor_tensor(g_T[:, t, hs, :], g_T[:, t, hs, :], ps[:, u, :].rearrange("p (h v) -> p h v", v=P),
                                                    ALU.subtract))
                nc.vector.tensor_tensor(g_TT[:, t, hs, :], g_TT[:, t, hs, :] if v else bc(ident),
                                        ps[:, 4 + u, :].rearrange("p (h v) -> p h v", v=P), ALU.subtract).then_inc(inv_t.sem, 1)
                if v < LEVELS - 1:
                    dve.wait_ge(inv_t.sem, inv_t.count(j, 4 * v + u))
        for u, (t, half) in enumerate(UNITS):
            hs = slice(4 * half, 4 * half + 4)
            dve.wait_ge(gd_kcd.sem, gd_kcd.count(j, u))
            nc.vector.tensor_copy(g_kcdT[:, t, hs, :], ps[:, 4 + u, :].rearrange("p (h v) -> p h v", v=P)).then_inc(gd_kcds.sem, 1)
        dve.wait_ge(gd_kcds.sem, gd_kcds.count(j, 3))
        ch.mark(nc.vector.memset(M[0:64, 0, :], 0.0))
        pair = lambda b, r=slice(0, P): ps[r, b:b + 2, :].rearrange("p b c -> p (b c)")
        dve.wait_ge(gd_sexp.sem, gd_sexp.count(j, 2))
        for c in range(4):
            t, r = c // 2, slice(64 * (c % 2), 64 * (c % 2) + 64)
            val = g_value[r, t, :, :].rearrange("p h v -> p (h v)")
            if c:
                dve.wait_ge(gd_p1.sem, gd_p1.count(j, c - 1))
                if c == 1:
                    dve.wait_ge(gd_vals.sem, gd_vals.count(j, 3))
                nc.vector.tensor_tensor(val, val, pair(0, r), ALU.subtract).then_inc(gd_vn.sem, 1)
                if c < 3:
                    m = ch.mark(nc.vector.tensor_tensor(g_Sd.rearrange("p (h v) -> p h v", v=P),
                                                        g_S2[:, c % 2, :].rearrange("p (h v) -> p h v", v=P),
                                                        eight(g_el[:, c, :]), ALU.mult))
            if c < 3:
                dve.wait_ge(gd_p2.sem, gd_p2.count(j, c))
                if c:
                    ch.wait(m)
                    nc.vector.tensor_tensor(g_S2[:, (c + 1) % 2, :], g_Sd, pair(4), ALU.add).then_inc(gd_S.sem, 1)
                else:
                    nc.vector.tensor_copy(g_S2[:, 1, :], pair(4)).then_inc(gd_S.sem, 1)
                dve.wait_ge(gd_S.sem, gd_S.count(j, c))
            if c:
                dve.wait_ge(gd_o1.sem, gd_o1.count(j, c - 1))
                nc.vector.tensor_tensor(M4[r, t, :, :], pair(2, r).rearrange("p (h v) -> p h v", v=P),
                                        eight(g_eg[r, t, :], 64), ALU.mult).then_inc(gd_o1t.sem, 1)
            if c % 2:
                dve.wait_ge(gd_o2.sem, gd_o2.count(j, t))
                dve.wait_ge(gd_o1t.sem, gd_o1t.count(j, c - 1))
                nc.vector.tensor_tensor(M[:, t, :], M[:, t, :], pair(6), ALU.add).then_inc(gd_o2t.sem, 1)
                dve.wait_ge(gd_o2t.sem, gd_o2t.count(j, t))
                ch.link(nc.vector.tensor_tensor(M4[:, t, :, :], M4[:, t, :, :], eight(rq[:, t, :]), ALU.mult))
        head_norm_vector(dve, i, ch, [g_z])

    def order_of_stages():
        st, xp, q = [], 0, 0
        for l in range(DEPTH):
            for j in range(2):
                if j == 1:
                    st.append(("mix", l, xp))
                    xp += 0
                    st.append(("norm", q, xp + 1, (1.0, start["mix_out", l] + 3)))
                    q, xp = q + 1, xp + 1
                st.append(("ffn", l, j, xp))
                n_last = start["ffn", l, j] + 3 * FF_STEPS - 1
                final = l == DEPTH - 1 and j == 1
                st.append(("norm", q, None if final else xp + 1, (0.5, n_last)))
                q, xp = q + 1, xp + (0 if final else 1)
        q, a = 0, 0
        n_last = start["ffn", DEPTH - 1, 1] + 3 * FF_STEPS - 1
        for i in range(DEPTH_2):
            st.append(("prenorm", q, xp + 1, n_last))
            q, xp = q + 1, xp + 1
            st.append(("mixer", i, xp, xp + 1))
            xp += 1
            n_last = start["out", i] + 3
            st.append(("addnorm", a))
            a += 1
            st.append(("prenorm", q, xp + 1, n_last))
            q, xp = q + 1, xp + 1
            st.append(("mlp", i, xp))
            n_last = start["mlp", i] + 2 * MLP_STEPS - 1
            st.append(("addnorm", a))
            a += 1
        return st


    dve_steps, act_steps, pool_steps, pe_steps = [0], [0], [0], [0]
    ST = order_of_stages()

    def split_two(split, eng, n_last):
        for n in (n_last + 2, n_last + 3):
            split(eng, n)

    block = ctx.enter_context(nc.Block())

    @block.sync
    def _(sp):
        sp.dma_start(x[:], w["x"][0].rearrange("(t p) d -> p t d", p=P)).then_inc(x_landed, 16)
        sp.dma_start(consts[:], w["const_main"]).then_inc(consts_landed, 16)
        for st in ST:
            if st[0] == "ffn":
                ffn_sync(sp, st[1], st[2])
            elif st[0] == "mlp":
                mlp_sync(sp, st[1])
            elif st[0] == "mix":
                for n in range(start["mix", st[1]], start["mix_out", st[1]] + 4):
                    load_chunk(sp, n)
            elif st[0] == "mixer":
                for n in range(start["in", st[1]], start["out", st[1]] + 4):
                    load_chunk(sp, n)
        sp.wait_ge(add_done.sem, add_done.count(2 * DEPTH_2 - 1, TT - 1))
        sp.dma_start(out[0].rearrange("(t p) d -> p t d", p=P), x[:]).then_inc(out_stored, 16)
        sp.wait_ge(out_stored, 16)

    @block.gpsimd
    def _(pool):
        nc.gpsimd.memset(mhalf, -0.5).then_inc(pool_chain, 1)
        nc.gpsimd.memset(eps_d, D * RMS_EPS).then_inc(pool_chain, 1)
        pool.wait_ge(pool_chain, 2)
        pool_steps[0] = 2
        for st in ST:
            if st[0] == "norm":
                norm_pool(pool, st[1])
            elif st[0] == "mix":
                mix_pool(pool, st[1])
            elif st[0] == "prenorm":
                prenorm_pool(pool, st[1])
            elif st[0] == "addnorm":
                addnorm_pool(pool, st[1])
            elif st[0] == "mixer":
                mixer_pool(pool, st[1])

    @block.scalar
    def _(act):
        for n in range(SPLIT):
            split_high(act, n)
        turn_scalar(act, 0)
        for st in ST:
            if st[0] == "ffn":
                ffn_scalar(act, st[1], st[2])
            elif st[0] == "norm":
                if st[2] is not None:
                    turn_scalar(act, st[2])
                    split_two(split_high, act, st[3][1])
            elif st[0] == "mix":
                mix_scalar(act, st[1])
            elif st[0] == "prenorm":
                prenorm_scalar(act, st[1])
                turn_scalar(act, st[2])
                split_two(split_high, act, st[3])
            elif st[0] == "addnorm":
                addnorm_scalar(act, st[1])
            elif st[0] == "mlp":
                mlp_scalar(act, st[1])
            elif st[0] == "mixer":
                mixer_scalar(act, st[1], st[3])

    @block.vector
    def _(dve):
        nc.vector.memset(ones[:], 1.0)
        nc.vector.memset(zrow[:], 0.0).then_inc(zrow_set, 1)
        for n in range(SPLIT):
            split_low(dve, n)
        turn_vector(dve, 0)
        for st in ST:
            if st[0] == "ffn":
                ffn_vector(dve, st[1], st[2])
            elif st[0] == "norm":
                scale, n_last = st[3]
                norm_vector(dve, st[1], scale, n_last)
                if st[2] is not None:
                    turn_vector(dve, st[2])
                    split_two(split_low, dve, n_last)
            elif st[0] == "mix":
                mix_vector(dve, st[1])
            elif st[0] == "prenorm":
                prenorm_vector(dve, st[1])
                turn_vector(dve, st[2])
                split_two(split_low, dve, st[3])
            elif st[0] == "addnorm":
                addnorm_vector(dve, st[1])
            elif st[0] == "mlp":
                mlp_vector(dve, st[1])
            elif st[0] == "mixer":
                mixer_vector(dve, st[1], st[3])

    @block.tensor
    def _(pe):
        pe.wait_ge(zrow_set, 1)
        pe.wait_ge(consts_landed, 16)
        pe.wait_ge(x_landed, 16)
        turn_tensor(pe, 0, x, lambda pe, t: None)
        for st in ST:
            if st[0] == "ffn":
                ffn_tensor(pe, st[1], st[2], st[3])
            elif st[0] == "norm":
                if st[2] is not None:
                    turn_tensor(pe, st[2], x, norm_done(st[1]))
            elif st[0] == "mix":
                mix_tensor(pe, st[1], st[2])
            elif st[0] == "prenorm":
                turn_tensor(pe, st[2], H, prenorm_is_done(st[1]), scaled=True)
            elif st[0] == "mlp":
                mlp_tensor(pe, st[1], st[2])
            elif st[0] == "mixer":
                mixer_tensor(pe, st[1], st[2], st[3])

    ctx.close()


_INS = [
    "x", "ln_g", "ln_b", "ffn_wg", "ffn_wu", "ffn_wd", "w_in", "w_out", "cmp_pe", "cmp_w1", "cmp_w2", "pool_w",
    "pool_scale", "gla_wa2", "gla_ba", "gla_norm_g", "norm_g_2", "mlp_w1_2", "mlp_w2_2", "gdn_w_in_2",
    "gdn_conv_2", "gdn_a_log_2", "gdn_dt_bias_2", "gdn_norm_g_2", "gdn_w_out_2", "mlstm_w_in_2",
    "mlstm_gate_b_2", "mlstm_norm_g_2", "mlstm_w_out_2", "diff_w_in_2", "diff_lambda_2", "diff_norm_g_2",
    "diff_w_out_2",
]


def kernel(**inputs):
    import numpy as _np
    import concourse.bacc as _bacc
    from concourse.bass_utils import run_bass_kernel_spmd as _run

    nc = _bacc.Bacc("TRN2", target_bir_lowering=False, num_devices=1)
    arrays, w = {}, {}
    for name in _INS:
        arrays[f"in_{name}"] = _np.ascontiguousarray(inputs[name])
    arrays.update(shape_constants())
    for name, a in arrays.items():
        w[name.removeprefix("in_")] = nc.dram_tensor(name, a.shape, F32, kind="ExternalInput").ap()
    out = nc.dram_tensor("out_0", (1, SEQ, D), F32, kind="ExternalOutput").ap()
    two_block_model(nc, w, out)
    r = _run(nc, [arrays], core_ids=[0])
    return r.results[0]["out_0"]
```

```python
from contextlib import ExitStack
import math

import concourse.bass as bass
from concourse import mybir

F32 = mybir.dt.float32
F32R = mybir.dt.float32r
BF16 = mybir.dt.bfloat16
ALU = mybir.AluOpType
ACT = mybir.ActivationFunctionType
AX = mybir.AxisListType

P = 128
D = 1024
KT = D // P
SEQ = 256
TT = SEQ // P
DEPTH = 2
D_FF = 2816
ALPHA = (2.0 * DEPTH) ** 0.25
LN_EPS = 1e-5
RMS_EPS = 1e-6
DEPTH_2 = 4
D_FF_2 = 4096
CHUNK = 64
NEG = -1.0e30

CW = 256
RAW = 3
SPLIT = 3
BODY = 6
assert BODY % RAW == 0 and BODY % SPLIT == 0

FF_STEPS = D_FF // CW
MLP_STEPS = D_FF_2 // CW

NSA_Q, NSA_KC, NSA_VC, NSA_KS, NSA_VS, NSA_KW, NSA_VW = 0, 512, 640, 768, 896, 1024, 1152
NSA_GATE, POOL_U, GLA_Q, GLA_K, GLA_V, GLA_A, GLA_R = 1280, 1304, 1560, 1688, 1816, 2072, 2088
GDN_QKV, GDN_Z, GDN_AB = 3072, 1024, 16
MLSTM_GATES = 3072


class Signal:

    def __init__(self, ctx, nc, name, per):
        self.sem, self.per = ctx.enter_context(nc.semaphore(name)), per

    def count(self, turn, k):
        assert 0 <= k < self.per
        return turn * self.per + k + 1


class Chain:

    def __init__(self, eng, sem):
        self.eng, self.sem, self.n = eng, sem, 0

    def mark(self, ins):
        self.n += 1
        ins.then_inc(self.sem, 1)
        return self.n

    def wait(self, n=None):
        self.eng.wait_ge(self.sem, self.n if n is None else n)

    def link(self, ins):
        self.mark(ins)
        self.wait()


def column_pieces(w, pieces):
    out, at = [], 0
    for c0, n in pieces:
        out.append(("cols", at, n, w[:, c0:c0 + n].rearrange("(k p) c -> p k c", p=P)))
        at += n
    return out


def row_pieces(w, r0):
    return [("rows", 0, 2, w[r0:r0 + 2 * P, :].rearrange("(r p) c -> p r c", p=P))]


def mixed_row_pieces(w, r0):
    out = []
    for r in range(2):
        f = r0 // P + r
        for g in range(2):
            out.append(("half", g, r, w[g * 256 + f * 64:g * 256 + f * 64 + 64, :]))
    return out


def gates_second(wi, gates, n):
    chunks = [column_pieces(wi, [(c, CW)]) for c in range(0, gates, CW)]
    return chunks[:1] + [column_pieces(wi, [(gates, n)])] + chunks[1:]


def weight_plan(w):
    plan, start = [], {}
    for l in range(DEPTH):
        for j in range(2):
            if j == 1:
                start["mix", l] = len(plan)
                wi = w["w_in"][l]
                for f0 in (0, 128):
                    plan.append(column_pieces(wi, [(NSA_Q + f0, 64), (NSA_Q + f0 + 256, 64),
                                                   (NSA_Q + f0 + 64, 64), (NSA_Q + f0 + 320, 64)]))
                for c0 in (NSA_KC, NSA_VC):
                    plan.append(column_pieces(wi, [(c0, 64), (c0, 64), (c0 + 64, 64), (c0 + 64, 64)]))
                plan.append(column_pieces(wi, [(NSA_KS, P), (NSA_KW, P)]))
                plan.append(column_pieces(wi, [(NSA_VS, P), (NSA_VW, P)]))
                plan.append(column_pieces(wi, [(POOL_U, 256)]))
                plan.append(column_pieces(wi, [(GLA_Q, 256)]))
                plan.append(column_pieces(wi, [(GLA_K, P), (NSA_GATE, 24), (GLA_A, 16)]))
                plan.append(column_pieces(wi, [(GLA_V, 256)]))
                plan.append(column_pieces(wi, [(GLA_R, 256)]))
                start["mix_out", l] = len(plan)
                wo = w["w_out"][l]
                plan += [mixed_row_pieces(wo, 0), mixed_row_pieces(wo, 256), row_pieces(wo, 512), row_pieces(wo, 768)]
            start["ffn", l, j] = len(plan)
            wg, wu, wd = w["ffn_wg"][l, j], w["ffn_wu"][l, j], w["ffn_wd"][l, j]
            for i in range(FF_STEPS):
                plan.append(column_pieces(wg, [(i * CW, CW)]))
                plan.append(column_pieces(wu, [(i * CW, CW)]))
                if i:
                    plan.append(row_pieces(wd, (i - 1) * CW))
            plan.append(row_pieces(wd, (FF_STEPS - 1) * CW))
    for i in range(DEPTH_2):
        start["in", i] = len(plan)
        if i % 3 == 0:
            wi, wo = w["gdn_w_in_2"][i // 3], w["gdn_w_out_2"][i // 3]
            plan += gates_second(wi, GDN_QKV + GDN_Z, GDN_AB)
        elif i % 3 == 1:
            wi, wo = w["mlstm_w_in_2"][0], w["mlstm_w_out_2"][0]
            plan += gates_second(wi, MLSTM_GATES, 16)
        else:
            wi, wo = w["diff_w_in_2"][0], w["diff_w_out_2"][0]
            plan += [column_pieces(wi, [(c, CW)]) for c in range(0, 3072, CW)]
        start["out", i] = len(plan)
        plan += [row_pieces(wo, r) for r in range(0, D, CW)]
        start["mlp", i] = len(plan)
        w1, w2 = w["mlp_w1_2"][i], w["mlp_w2_2"][i]
        for s in range(MLP_STEPS):
            plan.append(column_pieces(w1, [(s * CW, CW)]))
            if s:
                plan.append(row_pieces(w2, (s - 1) * CW))
        plan.append(row_pieces(w2, (MLP_STEPS - 1) * CW))
    return plan, start



POOL_WINDOWS = (2, 4, 8, 16)
N_CMP, CMP_STRIDE, CMP_BLOCK = 15, 16, 32
LEVELS = 6
ROT = 16
ROPE_THETA = 500000.0

CONST_AT = {}
_at = 0
for _name, _n in (("ident", P), ("upto", P), ("after", P), ("causal", 3 * P), ("cmp_mask", 2 * N_CMP), ("has_cmp", 2)):
    CONST_AT[_name] = (_at, _at + _n)
    _at += _n
N_CONST = _at


def shape_constants():
    import numpy as np

    s = np.arange(P)[:, None]
    t = np.arange(P)[None, :]
    same = (s // CHUNK) == (t // CHUNK)
    c = np.zeros((P, N_CONST), np.float32)

    def put(name, a):
        c[:, slice(*CONST_AT[name])] = a

    put("ident", s == t)
    put("upto", (s <= t) & same)
    put("after", (s > t) & same)
    tri = np.where(t <= s, 0.0, NEG)
    put("causal", np.concatenate([tri, np.zeros((P, P)), tri], 1))
    token = np.arange(SEQ).reshape(TT, P).T
    ends = np.arange(N_CMP) * CMP_STRIDE + CMP_BLOCK - 1
    put("cmp_mask", np.where(ends[None, None, :] <= token[:, :, None], 0.0, NEG).reshape(P, -1))
    put("has_cmp", token >= CMP_BLOCK - 1)

    pool = np.zeros((SEQ, len(POOL_WINDOWS), SEQ), np.float64)
    for g, width in enumerate(POOL_WINDOWS):
        for target in range(SEQ):
            lo = max(0, target - width + 1)
            pool[lo:target + 1, g, target] = 1.0 / (target + 1 - lo)
            pool[target, g, target] -= 1.0
    pool = np.concatenate([pool[:P], pool[P:, :, P:]], 2).reshape(P, -1)

    levels = np.zeros((P, LEVELS, P), np.float32)
    for v in range(LEVELS):
        b = 1 << v
        levels[:, v, :] = (s // (2 * b) == t // (2 * b)) & (s // b % 2 == 1) & (t // b % 2 == 0)
    heads = ((np.arange(P) // 32)[:, None] == (np.arange(256) // 64)[None, :])

    inv = ROPE_THETA ** (-np.arange(0, ROT, 2, dtype=np.float32) / ROT)
    angle = np.arange(SEQ, dtype=np.float32)[:, None] * inv.astype(np.float32)[None, :]
    rope = np.stack([np.cos(angle), np.sin(angle)], 1).reshape(TT, P, 2 * (ROT // 2)).transpose(1, 0, 2)
    hidden = np.where(t // CHUNK <= s // CHUNK, 0.0, NEG)
    return {
        "const_main": c,
        "const_pool": pool.astype(np.float32),
        "const_levels": levels.reshape(P, -1),
        "const_heads": heads.astype(np.float32),
        "const_rope": np.ascontiguousarray(rope.reshape(P, -1), np.float32),
        "const_tri": (s <= t).astype(np.float32),
        "const_chunks": np.concatenate([hidden, np.zeros((P, P)), hidden], 1).astype(np.float32),
    }


def two_block_model(nc, w, out):
    plan, start = weight_plan(w)
    n_chunks = len(plan)
    landed, total = [], [0] * RAW
    for n, pieces in enumerate(plan):
        total[n % RAW] += 16 * len(pieces)
        landed.append(total[n % RAW])

    ctx = ExitStack()
    ctx.enter_context(nc.allow_non_contiguous_dma(reason="small transposed parameters"))

    def sb(name, shape, dt=F32):
        return ctx.enter_context(nc.sbuf_tensor(name, shape, dt))

    def signal(name, per):
        return Signal(ctx, nc, name, per)

    def semaphore(name):
        return ctx.enter_context(nc.semaphore(name))

    raw = sb("raw", [P, RAW, KT * CW])
    w_hi = sb("w_hi", [P, SPLIT, KT * CW], F32R)
    w_lo = sb("w_lo", [P, SPLIT, KT * CW], F32R)
    x = sb("x", [P, TT, D])
    aT_hi = sb("aT_hi", [P, KT, SEQ], F32R)
    aT_lo = sb("aT_lo", [P, KT, SEQ], F32R)
    h_hi = sb("h_hi", [P, 3, 512], F32R)
    h_lo = sb("h_lo", [P, 3, 512], F32R)
    gb = sb("gb", [P, 2, D])
    NW = 10
    ws = [sb(f"ws{k}", [P, 2048]) for k in range(NW)]
    consts = sb("consts", [P, N_CONST])
    zrow = sb("zrow", [1, 512], BF16)
    ones = sb("ones", [P, 1])
    small = sb("small", [P, 640])
    ps = ctx.enter_context(nc.psum_tensor("ps", [P, 8, 512], F32))

    c_at = {name: slice(a, b) for name, (a, b) in CONST_AT.items()}
    ident = consts[:, c_at["ident"]]

    raw_landed = [semaphore(f"raw_landed{s}") for s in range(RAW)]
    hi_ready = semaphore("hi_ready")
    lo_ready = semaphore("lo_ready")
    weights_used = semaphore("weights_used")
    x_landed = semaphore("x_landed")
    consts_landed = semaphore("consts_landed")
    zrow_set = semaphore("zrow_set")
    opened = semaphore("accumulators_opened")
    out_stored = semaphore("out_stored")
    gain_landed = semaphore("gain_landed")
    gate_act = semaphore("gate_activated")
    hid_made = semaphore("hidden_made")
    hid_hi = semaphore("hidden_hi_ready")
    hid_lo = semaphore("hidden_lo_ready")
    ln_var = signal("ln_variance", TT)
    ln_rstd = signal("ln_rstd", TT)
    y_bank = signal("y_bank_summed", 3)
    ln_done = signal("ln_done", TT)
    turned = signal("turned_by_pe", 2 * TT)
    aT_hi_set = signal("aT_hi_set", 2 * TT)
    aT_lo_set = signal("aT_lo_set", 2 * TT)
    act_chain = semaphore("act_chain")
    dve_chain = semaphore("dve_chain")
    pool_chain = semaphore("pool_chain")

    hid_before, seen = {}, 0
    for l in range(DEPTH):
        for j in range(2):
            hid_before["ffn", l, j] = seen
            seen += FF_STEPS
    for i in range(DEPTH_2):
        hid_before["mlp", i] = seen
        seen += MLP_STEPS

    PER_TURN = 16 * BODY // RAW


    def slot_view(t, n, piece):
        kind, at, size = piece[:3]
        if kind == "cols":
            return t[:, n % RAW, :].rearrange("p (k c) -> p k c", c=CW)[:, :, at:at + size]
        return t[:, n % RAW, :].rearrange("p (r c) -> p r c", c=D)

    def used_part(t, n):
        pieces = plan[n]
        if pieces[0][0] != "cols":
            return t[:, n % RAW, :]
        width = sum(p[2] for p in pieces)
        if width == CW:
            return t[:, n % RAW, :]
        return t[:, n % RAW, :].rearrange("p (k c) -> p k c", c=CW)[:, :, 0:width]

    def load_chunk(sp, n):
        if n >= RAW:
            sp.wait_ge(lo_ready, n - RAW + 1)
        for piece in plan[n]:
            if piece[0] == "half":
                _, g, r, src = piece
                dst = raw[64 * g:64 * g + 64, n % RAW, r * D:(r + 1) * D]
            else:
                dst, src = slot_view(raw, n, piece), piece[3]
            sp.dma_start(dst, src).then_inc(raw_landed[n % RAW], 16)

    def split_high(act, n, turn=0):
        if n >= n_chunks:
            return
        act.wait_ge(raw_landed[n % RAW], landed[n] + PER_TURN * turn)
        if n >= SPLIT:
            act.wait_ge(weights_used, n - SPLIT + 1 + BODY * turn)
        nc.scalar.copy(used_part(w_hi, n), used_part(raw, n)).then_inc(hi_ready, 1)

    def split_low(dve, n, turn=0):
        if n >= n_chunks:
            return
        dve.wait_ge(hi_ready, n + 1 + BODY * turn)
        nc.vector.tensor_tensor(used_part(w_lo, n), used_part(raw, n), used_part(w_hi, n).bitcast(F32),
                                ALU.subtract).then_inc(lo_ready, 1)

    def product(pe, dst, l_hi, l_lo, r_hi, r_lo, start, stop):
        nc.tensor.matmul(dst, l_hi, r_hi, start=start, stop=False)
        nc.tensor.matmul(dst, l_hi, r_lo, start=False, stop=False)
        return nc.tensor.matmul(dst, l_lo, r_hi, start=False, stop=stop)

    def cols_slot(t, n):
        return t[:, n % SPLIT, :].rearrange("p (k c) -> p k c", c=CW)

    def features_product(pe, n, bank, turn=0, tiles=2, xpass=None):
        pe.wait_ge(lo_ready, n + 1 + BODY * turn)
        hi, lo = cols_slot(w_hi, n), cols_slot(w_lo, n)
        for ft in range(tiles):
            for k in range(KT):
                if xpass is not None and ft == 0 and k % 4 == 0:
                    pe.wait_ge(aT_lo_set.sem, aT_lo_set.count(xpass, 2 + k // 4))
                last = product(pe, ps[:, bank, ft * SEQ:(ft + 1) * SEQ], hi[:, k, ft * P:(ft + 1) * P],
                               lo[:, k, ft * P:(ft + 1) * P], aT_hi[:, k, :], aT_lo[:, k, :], k == 0, k == KT - 1)
        last.then_inc(weights_used, 1)

    def tokens_product(pe, n, bank, width=CW):
        pe.wait_ge(lo_ready, n + 1)
        hi, lo = cols_slot(w_hi, n), cols_slot(w_lo, n)
        for t in range(TT):
            for k in range(KT):
                last = product(pe, ps[:, bank, t * CW:t * CW + width], aT_hi[:, k, t * P:(t + 1) * P],
                               aT_lo[:, k, t * P:(t + 1) * P], hi[:, k, 0:width], lo[:, k, 0:width], k == 0, k == KT - 1)
        last.then_inc(weights_used, 1)

    def open_accumulators(pe):
        for b in range(4):
            last = nc.tensor.matmul(ps[:, b, :], zrow[0:1, 0:P], zrow[0:1, :], start=True, stop=False)
        return last

    def last_rows(pe, chunks, turn):
        for b in range(4):
            t, c = b // 2, slice(b % 2 * 512, b % 2 * 512 + 512)
            for q, (n, l_hi, l_lo, wait) in enumerate(chunks):
                if b == 0:
                    wait()
                    pe.wait_ge(lo_ready, n + 1)
                hi = w_hi[:, n % SPLIT, :].rearrange("p (r c) -> p r c", c=D)
                lo = w_lo[:, n % SPLIT, :].rearrange("p (r c) -> p r c", c=D)
                for r in range(2):
                    s = slice(r * SEQ + t * P, r * SEQ + (t + 1) * P)
                    last = product(pe, ps[:, b, :], l_hi[:, s], l_lo[:, s], hi[:, r, c], lo[:, r, c], False, q == 1 and r == 1)
                if b == 3:
                    last.then_inc(weights_used, 1)
            if b < 3:
                last.then_inc(y_bank.sem, 1)

    def wait_y(eng, turn, b, n_last):
        if b < 3:
            eng.wait_ge(y_bank.sem, y_bank.count(turn, b))
        else:
            eng.wait_ge(weights_used, n_last + 1)

    def rows_product(pe, n, l_hi, l_lo, turn=0):
        pe.wait_ge(lo_ready, n + 1 + BODY * turn)
        hi = w_hi[:, n % SPLIT, :].rearrange("p (r c) -> p r c", c=D)
        lo = w_lo[:, n % SPLIT, :].rearrange("p (r c) -> p r c", c=D)
        for t in range(TT):
            for half in range(2):
                c = slice(half * 512, half * 512 + 512)
                for r in range(2):
                    s = slice(r * SEQ + t * P, r * SEQ + (t + 1) * P)
                    last = product(pe, ps[:, 2 * t + half, :], l_hi[:, s], l_lo[:, s], hi[:, r, c], lo[:, r, c],
                                   False, False)
        last.then_inc(weights_used, 1)

    def y_tile(t):
        return ps[:, 2 * t:2 * t + 2, :].rearrange("p b c -> p (b c)")


    def ffn_tensor(pe, l, j, xpass):
        n0, hid0 = start["ffn", l, j], hid_before["ffn", l, j]
        open_accumulators(pe)
        features_product(pe, n0, 4, xpass=xpass)
        features_product(pe, n0 + 1, 5)

        def step(b, it, rows=True):
            n, i = n0 + 2 + 3 * b, 1 + b
            features_product(pe, n, 4 + 2 * (i % 2), turn=it)
            features_product(pe, n + 1, 5 + 2 * (i % 2), turn=it)
            if rows:
                pe.wait_ge(hid_lo, hid0 + i + 2 * it)
                rows_product(pe, n + 2, h_hi[:, (i - 1) % 2, :], h_lo[:, (i - 1) % 2, :], turn=it)

        turns = (FF_STEPS - 1) // 2 - 1
        with pe.Fori(0, turns) as it:
            step(0, it)
            step(1, it)
        step(2 * turns, 0)
        step(2 * turns + 1, 0, rows=False)
        last_rows(pe, [(n, h_hi[:, i % 2, :], h_lo[:, i % 2, :], lambda i=i: pe.wait_ge(hid_lo, hid0 + i + 1))
                       for n, i in ((n0 + 3 * FF_STEPS - 2, FF_STEPS - 2), (n0 + 3 * FF_STEPS - 1, FF_STEPS - 1))],
                  3 * l + 2 * j)

    def ffn_scalar(act, l, j):
        n0, hid0 = start["ffn", l, j], hid_before["ffn", l, j]
        gate = [ws[0][:, 0:512], ws[0][:, 512:1024]]

        def silu(n, i, turn=0, steps=0):
            act.wait_ge(weights_used, n + 1 + BODY * turn)
            if i + steps >= 2 or steps:
                act.wait_ge(hid_made, hid0 + i - 1 + 2 * turn)
            nc.scalar.activation(gate[i % 2], ps[:, 4 + 2 * (i % 2), :], ACT.Silu).then_inc(gate_act, 1)

        split_high(act, n0 + 3)
        silu(n0, 0)
        split_high(act, n0 + 4)

        def two_steps(n_first, i_first, turn=0, final=False):
            for b in range(2):
                n, i = n_first + 3 * b, i_first + b
                split_high(act, n + 3, turn)
                silu(n, i, turn, steps=1)
                split_high(act, n + 4, turn)
                if not (final and b == 1):
                    split_high(act, n + 5, turn)

        turns = (FF_STEPS - 1) // 2 - 1
        with act.Fori(0, turns) as it:
            two_steps(n0 + 2, 1, it)
        two_steps(n0 + 2 + BODY * turns, 1 + 2 * turns, final=True)

    def hidden_vector(dve, n, hid, buf, bank, gate, turn=0, step=0, war=True):
        dve.wait_ge(gate_act, hid + 1 + step * turn)
        if n is not None:
            dve.wait_ge(weights_used, n + 1 + BODY * turn)
        up = ps[:, bank, :] if bank is not None else gate
        h = ws[1][:, 512 * buf:512 * buf + 512]
        nc.vector.tensor_tensor(h, gate, up, ALU.mult).then_inc(hid_made, 1)
        dve.wait_ge(hid_made, hid + 1 + step * turn)
        nc.vector.tensor_copy(h_hi[:, buf, :], h).then_inc(hid_hi, 1)
        dve.wait_ge(hid_hi, hid + 1 + step * turn)
        nc.vector.tensor_tensor(h_lo[:, buf, :], h, h_hi[:, buf, :].bitcast(F32), ALU.subtract).then_inc(hid_lo, 1)

    def ffn_vector(dve, l, j):
        n0, hid0 = start["ffn", l, j], hid_before["ffn", l, j]
        gate = [ws[0][:, 0:512], ws[0][:, 512:1024]]
        split_low(dve, n0 + 3)
        hidden_vector(dve, n0 + 1, hid0, 0, 5, gate[0])
        split_low(dve, n0 + 4)

        def two_steps(n_first, i_first, turn=0, final=False):
            for b in range(2):
                n, i = n_first + 3 * b, i_first + b
                split_low(dve, n + 3, turn)
                hidden_vector(dve, n + 1, hid0 + i, i % 2, 5 + 2 * (i % 2), gate[i % 2], turn, step=2)
                split_low(dve, n + 4, turn)
                if not (final and b == 1):
                    split_low(dve, n + 5, turn)

        turns = (FF_STEPS - 1) // 2 - 1
        with dve.Fori(0, turns) as it:
            two_steps(n0 + 2, 1, it)
        two_steps(n0 + 2 + BODY * turns, 1 + 2 * turns, final=True)

    def ffn_sync(sp, l, j):
        n0 = start["ffn", l, j]
        wg, wu, wd = w["ffn_wg"][l, j], w["ffn_wu"][l, j], w["ffn_wd"][l, j]
        wdr = wd.rearrange("(s r p) c -> p s r c", p=P, r=2)
        load_chunk(sp, n0)
        load_chunk(sp, n0 + 1)
        with sp.Fori(0, (FF_STEPS - 1) // 2) as it:
            for b in range(2):
                n = n0 + 2 + 3 * b
                for q, m in ((0, wg), (1, wu)):
                    wait_slot(sp, n + q, it)
                    src = m[:, bass.ds((1 + b) * CW + it * (2 * CW), CW)].rearrange("(k p) c -> p k c", p=P)
                    sp.dma_start(slot_view(raw, n + q, plan[n + q][0]), src).then_inc(raw_landed[(n + q) % RAW], 16)
                wait_slot(sp, n + 2, it)
                src = wd[bass.ds(b * CW + it * (2 * CW), CW), :].rearrange("(r p) c -> p r c", p=P)
                sp.dma_start(slot_view(raw, n + 2, plan[n + 2][0]), src).then_inc(raw_landed[(n + 2) % RAW], 16)
        load_chunk(sp, n0 + 3 * FF_STEPS - 1)

    def wait_slot(sp, n, turn):
        sp.wait_ge(lo_ready, n - RAW + 1 + BODY * turn)


    def mlp_tensor(pe, i, xpass):
        n0, hid0 = start["mlp", i], hid_before["mlp", i]
        open_accumulators(pe)
        features_product(pe, n0, 4, xpass=xpass)

        def step(b, it, rows=True):
            n, s = n0 + 1 + 2 * b, 1 + b
            features_product(pe, n, 4 + s % 3, turn=it)
            if rows:
                pe.wait_ge(hid_lo, hid0 + s + 3 * it)
                rows_product(pe, n + 1, h_hi[:, (s - 1) % 3, :], h_lo[:, (s - 1) % 3, :], turn=it)

        turns = (MLP_STEPS - 1) // 3 - 1
        with pe.Fori(0, turns) as it:
            for b in range(3):
                step(b, it)
        for b in range(3):
            step(3 * turns + b, 0, rows=b < 2)
        last_rows(pe, [(n, h_hi[:, s % 3, :], h_lo[:, s % 3, :], lambda s=s: pe.wait_ge(hid_lo, hid0 + s + 1))
                       for n, s in ((n0 + 2 * MLP_STEPS - 2, MLP_STEPS - 2), (n0 + 2 * MLP_STEPS - 1, MLP_STEPS - 1))],
                  3 * DEPTH + 2 * i + 1)

    def mlp_scalar(act, i):
        n0, hid0 = start["mlp", i], hid_before["mlp", i]
        gate = [ws[0][:, 512 * k:512 * k + 512] for k in range(3)]

        def relu(n, s, turn=0, loop=False):
            act.wait_ge(weights_used, n + 1 + BODY * turn)
            if loop:
                act.wait_ge(hid_made, hid0 + s - 2 + 3 * turn if s >= 2 else hid0 + 3 * turn)
            nc.scalar.activation(gate[s % 3], ps[:, 4 + s % 3, :], ACT.Relu).then_inc(gate_act, 1)

        split_high(act, n0 + 3)
        relu(n0, 0)

        def three_steps(n_first, s_first, turn=0, final=False):
            for b in range(3):
                n, s = n_first + 2 * b, s_first + b
                split_high(act, n + 3, turn)
                relu(n, s, turn, loop=True)
                if not (final and b == 2):
                    split_high(act, n + 4, turn)

        turns = (MLP_STEPS - 1) // 3 - 1
        with act.Fori(0, turns) as it:
            three_steps(n0 + 1, 1, it)
        three_steps(n0 + 1 + BODY * turns, 1 + 3 * turns, final=True)

    def mlp_vector(dve, i):
        n0, hid0 = start["mlp", i], hid_before["mlp", i]
        gate = [ws[0][:, 512 * k:512 * k + 512] for k in range(3)]
        split_low(dve, n0 + 3)
        hidden_vector(dve, None, hid0, 0, None, gate[0])

        def three_steps(n_first, s_first, turn=0, final=False):
            for b in range(3):
                n, s = n_first + 2 * b, s_first + b
                split_low(dve, n + 3, turn)
                hidden_vector(dve, None, hid0 + s, s % 3, None, gate[s % 3], turn, step=3)
                if not (final and b == 2):
                    split_low(dve, n + 4, turn)

        turns = (MLP_STEPS - 1) // 3 - 1
        with dve.Fori(0, turns) as it:
            three_steps(n0 + 1, 1, it)
        three_steps(n0 + 1 + BODY * turns, 1 + 3 * turns, final=True)

    def mlp_sync(sp, i):
        n0 = start["mlp", i]
        w1, w2 = w["mlp_w1_2"][i], w["mlp_w2_2"][i]
        load_chunk(sp, n0)
        with sp.Fori(0, (MLP_STEPS - 1) // 3) as it:
            for b in range(3):
                n = n0 + 1 + 2 * b
                wait_slot(sp, n, it)
                src = w1[:, bass.ds((1 + b) * CW + it * (3 * CW), CW)].rearrange("(k p) c -> p k c", p=P)
                sp.dma_start(slot_view(raw, n, plan[n][0]), src).then_inc(raw_landed[n % RAW], 16)
                wait_slot(sp, n + 1, it)
                src = w2[bass.ds(b * CW + it * (3 * CW), CW), :].rearrange("(r p) c -> p r c", p=P)
                sp.dma_start(slot_view(raw, n + 1, plan[n + 1][0]), src).then_inc(raw_landed[(n + 1) % RAW], 16)
        load_chunk(sp, n0 + 2 * MLP_STEPS - 1)


    def turn_tensor(pe, xpass, src, ready, scaled=False):
        for t in range(TT):
            ready(pe, t)
            for half in range(2):
                turn_bank(pe, src, t, half, scaled)

    def turn_bank(pe, src, t, half, scaled=False):
        for q in range(4):
            k = 4 * half + q
            o, tile = ps[:, 4 + 2 * t + half, q * P:(q + 1) * P], src[:, t, k * P:(k + 1) * P]
            if scaled:
                last = nc.tensor.matmul(o, tile, diag[:, t, :], start=True, stop=True)
            else:
                last = nc.tensor.transpose(o, tile, ident)
        last.then_inc(turned.sem, 1)

    BY_TILE = [(t, half) for t in range(TT) for half in range(2)]

    def turn_scalar(act, xpass, order=BY_TILE):
        for e, (t, half) in enumerate(order):
            act.wait_ge(turned.sem, turned.count(xpass, e))
            nc.scalar.copy(aT_hi[:, 4 * half:4 * half + 4, t * P:(t + 1) * P],
                           ps[:, 4 + 2 * t + half, :].rearrange("p (q c) -> p q c", c=P)).then_inc(aT_hi_set.sem, 1)

    def turn_vector(dve, xpass, order=BY_TILE):
        for e, (t, half) in enumerate(order):
            dve.wait_ge(aT_hi_set.sem, aT_hi_set.count(xpass, e))
            s = (slice(None), slice(4 * half, 4 * half + 4), slice(t * P, (t + 1) * P))
            nc.vector.tensor_tensor(aT_lo[s], ps[:, 4 + 2 * t + half, :].rearrange("p (q c) -> p q c", c=P),
                                    aT_hi[s].bitcast(F32), ALU.subtract).then_inc(aT_lo_set.sem, 1)

    def wait_turned(pe, xpass):
        pe.wait_ge(aT_lo_set.sem, aT_lo_set.count(xpass, 2 * TT - 1))


    Z = ws[2].rearrange("p (t c) -> p t c", c=D)
    stats = small[:, 0:24].rearrange("p (t a b) -> p t a b", a=2, b=6)
    mv = small[:, 24:28].rearrange("p (t a) -> p t a", a=2)
    ve = small[:, 28:30]
    rstd = small[:, 30:32]
    mhalf = small[:, 34:66]
    eps_d = small[:, 32:33]

    def norm_vector(dve, q, scale, n_last):
        ch = Chain(dve, dve_chain)
        ch.n = dve_steps[0]
        for t in range(TT):
            for a in range(2):
                c = slice(512 * a, 512 * a + 512)
                wait_y(dve, q, 2 * t + a, n_last)
                ch.link(nc.vector.scalar_tensor_tensor(out=Z[:, t, c], in0=ps[:, 2 * t + a, :], scalar=scale / ALPHA, in1=x[:, t, c],
                                                       op0=ALU.mult, op1=ALU.add))
                m = ch.mark(nc.vector.bn_stats(stats[:, t, a, :], Z[:, t, 512 * a:512 * a + 512]))
            ch.wait(m)
            ch.link(nc.vector.bn_aggr(mv[:, t, :], stats[:, t, :, :].rearrange("p a b -> p (a b)")))
            nc.vector.tensor_scalar(ve[:, t:t + 1], mv[:, t, 1:2], LN_EPS / ALPHA ** 2, None, ALU.add).then_inc(ln_var.sem, 1)
            if t == 0:
                dve.wait_ge(gain_landed, gain_count("ln", q))
            ch.link(nc.vector.scalar_tensor_tensor(out=Z[:, t, :], in0=Z[:, t, :], scalar=mv[:, t, 0:1], in1=gb[:, 0, :],
                                                   op0=ALU.subtract, op1=ALU.mult))
            dve.wait_ge(ln_rstd.sem, ln_rstd.count(q, t))
            nc.vector.scalar_tensor_tensor(out=x[:, t, :], in0=Z[:, t, :], scalar=rstd[:, t:t + 1], in1=gb[:, 1, :],
                                           op0=ALU.mult, op1=ALU.add).then_inc(ln_done.sem, 1)
        dve_steps[0] = ch.n

    def norm_pool(pool, q):
        l, j = q // 3, q % 3
        if q:
            pool.wait_ge(ln_done.sem, ln_done.count(q - 1, TT - 1))
        else:
            pool.wait_ge(hi_ready, 3)
        if q == 3 * DEPTH - 1:
            load_pre_gain(pool, 0)
        pool.dma_start(gb[:, 0, :], w["ln_g"][l, j:j + 1, :].to_broadcast([P, D])).then_inc(gain_landed, 16)
        pool.dma_start(gb[:, 1, :], w["ln_b"][l, j:j + 1, :].to_broadcast([P, D])).then_inc(gain_landed, 16)
        for t in range(TT):
            pool.wait_ge(ln_var.sem, ln_var.count(q, t))
            nc.gpsimd.tensor_tensor(rstd[:, t:t + 1], ve[:, t:t + 1], mhalf[:, 0:1], ALU.pow).then_inc(ln_rstd.sem, 1)

    def gain_count(kind, q):
        return 32 * (q + 1) if kind == "ln" else 32 * 3 * DEPTH + 16 * (q + 1)

    def norm_done(q):
        return lambda pe, t: pe.wait_ge(ln_done.sem, ln_done.count(q, t))


    def cols(k, a, b, rows=slice(0, P)):
        return ws[k][rows, a:b]

    qT = cols(0, 0, 1024).rearrange("p (f s) -> p f s", s=SEQ)
    k_win = cols(0, 1024, 1280)
    k_sel = cols(3, 1680, 1680 + N_CMP + SEQ)
    gqT, gkT = cols(0, 1536, 1792), cols(0, 1792, 2048)
    pooledT = cols(1, 0, 512)
    pool_y = cols(1, 512, 1024)
    v_tok = cols(1, 1024, 1536).rearrange("p (t c) -> p t c", c=256)
    u_tok = cols(1, 1536, 2048).rearrange("p (t c) -> p t c", c=256)
    gka = cols(2, 0, 512).rearrange("p (t c) -> p t c", c=256)
    gv = cols(2, 512, 1024).rearrange("p (t c) -> p t c", c=256)
    gr = cols(2, 1536, 2048)
    pool_m = cols(3, 0, 1536).rearrange("p (g s) -> p g s", s=3 * P)
    pool_wt = cols(3, 1536, 1664).rearrange("p (g d) -> p g d", d=64)
    pool_sc = cols(3, 1664, 1666)
    cmp_w1 = cols(4, 0, 2048).rearrange("p (v j o) -> p v j o", v=2, o=64)
    cmp_pe = cols(5, 0, 32).rearrange("p (v j) -> p v j", v=2)
    cmp_w2 = cols(5, 32, 160, slice(0, 64)).rearrange("p (v o) -> p v o", v=2)
    wa2 = cols(5, 160, 288, slice(0, 17))
    gla_g = cols(5, 288, 544)
    head_mask = cols(5, 544, 800)
    blocks = cols(5, 800, 1760).rearrange("p (v j n) -> p v j n", v=2, n=2 * N_CMP)
    gelu_T = cols(5, 1760, 1820, slice(0, 64))
    kcT = k_sel[:, 0:N_CMP]
    vc = cols(5, 1840, 1968, slice(0, N_CMP)).rearrange("p (g d) -> p g d", d=64)
    E1, E2, E3 = cols(8, 0, 256), cols(8, 256, 512), cols(8, 512, 768)
    qtT, ktT = cols(8, 768, 1024), cols(8, 1024, 1280)
    k3 = cols(8, 1280, 1536).rearrange("p (t c) -> p t c", c=P)
    o_gla = cols(8, 1536, 2048)
    att = cols(9, 0, 1024).rearrange("p (t c) -> p t c", c=512)
    S_gla = cols(9, 1024, 2048).rearrange("p (c v) -> p c v", v=256)
    ga_T = cols(6, 0, 256, slice(0, 17))
    absz, la = cols(6, 256, 512), cols(6, 512, 768)
    q_heads = cols(7, 0, 1024).rearrange("p (t c) -> p t c", c=512)
    sq = cols(6, 768, 1280)
    gate = small[:, 66:114].rearrange("p (h b t) -> p h b t", b=3, t=2)
    tanh_g = small[:, 114:162].rearrange("p (t c) -> p t c", c=24)
    ss_gla, rs_gla = small[:, 162:170], small[:, 170:178]
    stat = small[:, 178:226].rearrange("p (r c) -> p r c", c=24)

    MIX_LOADS = 13
    mix_landed = signal("mix_weights_landed", MIX_LOADS)
    mix_set = signal("mix_cleared", 2)
    mix_act = signal("mix_projected_by_act", 6)
    mix_dve = signal("mix_projected_by_dve", 7)
    cmp_pre = signal("compress_hidden", 1)
    cmp_act = signal("compress_gelu", 1)
    cmp_out = signal("compressed", 1)
    cmp_set = signal("compressed_copied", 2)
    ga_turned = signal("decay_input_turned", 1)
    ga_set = signal("decay_input_set", 1)
    la_pre = signal("log_decay_product", 1)
    la_ln = signal("log_decay_logs", 1)
    la_set = signal("log_decay_set", 1)
    b_sum = signal("decay_sums", 1)
    b_exp = signal("decay_exps", 3)
    qk_set = signal("gla_q_k_set", 4)
    gate_tanh = signal("gate_tanh", 1)
    at_done = signal("gla_scores", 2)
    at_set = signal("gla_scores_masked", 2)
    ds_done = signal("gla_state_products", 3)
    s_set = signal("gla_state_set", 3)
    inter = signal("gla_inter_done", 1)
    intra = signal("gla_intra_done", 1)
    inter_set = signal("gla_inter_copied", 1)
    gla_ss = signal("gla_square_sums", 1)
    gla_rs = signal("gla_rms", 1)
    gla_o = signal("gla_output", 1)
    gla_turned = signal("gla_output_turned", 1)
    pool_done = signal("pool_means", 1)
    pool_set = signal("pool_means_set", 1)
    pool_out = signal("pool_output", 1)
    pool_scaled = signal("pool_scaled", 4)
    mixT_hi = signal("mix_hi_set", 4)
    mixT_lo = signal("mix_lo_set", 4)
    scored = signal("nsa_scored", 8)
    peaked = signal("nsa_maxima", 8)
    exped = signal("nsa_exps", 8)
    weighed = signal("nsa_weights", 8)
    p_turned = signal("nsa_weights_turned", 8)
    pT_act = signal("nsa_turned_by_act", 8)
    pT_dve = signal("nsa_turned_by_dve", 8)
    summed = signal("nsa_values_summed", 8)
    HEADS = [f + 4 * g for f in range(4) for g in range(2)]

    def mix_pool(pool, l):
        if l:
            pool.wait_ge(ln_done.sem, ln_done.count(3 * l - 2, TT - 1))
        def load(dst, src):
            pool.dma_start(dst, src).then_inc(mix_landed.sem, 1 * 16)
        load(pool_m[:], w["const_pool"].rearrange("p (g s) -> p g s", s=3 * P))
        load(head_mask, w["const_heads"])
        load(cmp_w1[:, 0, :, :], w["cmp_w1"][l, 0].rearrange("(j p) o -> p j o", p=P))
        load(cmp_w1[:, 1, :, :], w["cmp_w1"][l, 1].rearrange("(j p) o -> p j o", p=P))
        for v in range(2):
            load(cmp_pe[:, v, :], w["cmp_pe"][l, v].rearrange("(j r) d -> (r d) j", r=2))
        load(cmp_w2[:], w["cmp_w2"][l].rearrange("v i o -> i v o"))
        load(wa2[0:16, :], w["gla_wa2"][l])
        load(wa2[16:17, :], w["gla_ba"][l:l + 1, :])
        load(gla_g, w["gla_norm_g"][l:l + 1, :].to_broadcast([P, 256]))
        for r in range(2):
            load(pool_wt[64 * r:64 * r + 64, :, :], w["pool_w"][l].rearrange("(g r) c d -> r c g d", r=2)[r])
        load(pool_sc, w["pool_scale"][l].rearrange("(g p) -> p g", p=P))
        nc.gpsimd.memset(S_gla[:, 0, :], 0.0).then_inc(mix_set.sem, 1)
        nc.gpsimd.memset(ga_T, 1.0).then_inc(mix_set.sem, 1)
        pool.wait_ge(gla_ss.sem, gla_ss.count(l, 0))
        nc.gpsimd.tensor_tensor(rs_gla, ss_gla, mhalf[:, 0:8], ALU.pow).then_inc(gla_rs.sem, 1)

    def mix_tensor(pe, l, xpass):
        n0 = start["mix", l]
        wait_turned(pe, xpass)
        for m in range(11):
            if m == 8:
                pe.wait_ge(mix_act.sem, mix_act.count(l, 0))
            if m == 9:
                pe.wait_ge(mix_act.sem, mix_act.count(l, 1))
            if m == 10:
                pe.wait_ge(mix_dve.sem, mix_dve.count(l, 1))
            if m in (0, 1, 2, 3, 4, 7):
                features_product(pe, n0 + m, m % 8)
            else:
                tokens_product(pe, n0 + m, m % 8, 168 if m == 8 else CW)
        pe.wait_ge(mix_act.sem, mix_act.count(l, 5))
        pe.wait_ge(mix_dve.sem, mix_dve.count(l, 6))
        pe.wait_ge(mix_landed.sem, 16 * MIX_LOADS * (l + 1))
        pe.wait_ge(mix_set.sem, mix_set.count(l, 1))
        for t in range(TT):
            last = nc.tensor.transpose(ps[0:16, 1, t * P:(t + 1) * P], gka[:, t, 152:168], ident)
        last.then_inc(ga_turned.sem, 1)
        for v in range(2):
            for j in range(16):
                last = nc.tensor.matmul(ps[0:64, 0, 64 * v:64 * v + 30], cmp_w1[:, v, j, :], blocks[:, v, j, :],
                                        start=(j == 0), stop=(j == 15))
        last.then_inc(cmp_pre.sem, 1)
        for g in range(4):
            o = ps[64 * (g % 2):64 * (g % 2) + 64, 2, (g // 2) * SEQ:(g // 2 + 1) * SEQ]
            nc.tensor.matmul(o, u_tok[:, 0, 64 * g:64 * g + 64], pool_m[:, g, 0:SEQ], start=True, stop=False)
            last = nc.tensor.matmul(o[:, P:SEQ], u_tok[:, 1, 64 * g:64 * g + 64], pool_m[:, g, SEQ:3 * P], start=False, stop=True)
        last.then_inc(pool_done.sem, 1)
        pe.wait_ge(ga_set.sem, ga_set.count(l, 0))
        for t in range(TT):
            last = nc.tensor.matmul(ps[:, 3, t * P:(t + 1) * P], ga_T[:, t * P:(t + 1) * P], wa2, start=True, stop=True)
        last.then_inc(la_pre.sem, 1)
        pe.wait_ge(cmp_act.sem, cmp_act.count(l, 0))
        for g in range(2):
            nc.tensor.matmul(ps[64 * g:64 * g + 64, 0, 0:N_CMP], cmp_w2[:, 0, :], gelu_T[:, N_CMP * g:N_CMP * (g + 1)],
                             start=True, stop=True)
        for g in range(2):
            last = nc.tensor.matmul(ps[0:N_CMP, 1, 64 * g:64 * g + 64],
                                    gelu_T[:, 30 + N_CMP * g:30 + N_CMP * (g + 1)], cmp_w2[:, 1, :], start=True, stop=True)
        last.then_inc(cmp_out.sem, 1)
        pe.wait_ge(pool_set.sem, pool_set.count(l, 0))
        for g in range(4):
            r = slice(64 * (g % 2), 64 * (g % 2) + 64)
            last = nc.tensor.matmul(ps[r, 6 + g % 2, (g // 2) * SEQ:(g // 2 + 1) * SEQ], pool_wt[r, g // 2, :],
                                    pooledT[r, (g // 2) * SEQ:(g // 2 + 1) * SEQ], start=True, stop=True)
        last.then_inc(pool_out.sem, 1)
        pe.wait_ge(la_set.sem, la_set.count(l, 0))
        for t in range(TT):
            s = slice(t * P, (t + 1) * P)
            nc.tensor.matmul(ps[:, 4, s], la[:, s], consts[:, c_at["upto"]], start=True, stop=True)
            last = nc.tensor.matmul(ps[:, 4, SEQ + t * P:SEQ + (t + 1) * P], consts[:, c_at["after"]], la[:, s],
                                    start=True, stop=True)
        last.then_inc(b_sum.sem, 1)
        for t in range(TT):
            pe.wait_ge(qk_set.sem, qk_set.count(l, 3))
            nc.tensor.matmul(ps[:, 2 + t, :], ktT[:, t * P:(t + 1) * P], q_heads[:, t, :], start=True, stop=True).then_inc(at_done.sem, 1)
        pe.wait_ge(pool_scaled.sem, pool_scaled.count(l, 3))
        for c in range(4):
            if c:
                pe.wait_ge(s_set.sem, s_set.count(l, c - 1))
            r = slice(64 * (c % 2), 64 * (c % 2) + 64)
            last = nc.tensor.matmul(ps[r, 6, (c // 2) * 256:(c // 2 + 1) * 256], qtT[:, 64 * c:64 * c + 64], S_gla[:, c, :],
                                    start=True, stop=True)
            if c < 3:
                nc.tensor.matmul(ps[:, c % 2, 0:256], k3[r, c // 2, :], gv[r, c // 2, :], start=True,
                                 stop=True).then_inc(ds_done.sem, 1)
        last.then_inc(inter.sem, 1)
        for t in range(TT):
            pe.wait_ge(at_set.sem, at_set.count(l, t))
            for h in range(4):
                last = nc.tensor.matmul(ps[:, 7, t * 256 + 64 * h:t * 256 + 64 * h + 64], att[:, t, h * P:(h + 1) * P],
                                        gv[:, t, 64 * h:64 * h + 64], start=True, stop=True)
        last.then_inc(intra.sem, 1)
        def scores(e):
            h = HEADS[e]
            f, g = h % 4, h // 4
            r = slice(64 * g, 64 * g + 64)
            if e >= 2:
                pe.wait_ge(peaked.sem, peaked.count(l, e - 2))
            for bank, keys, more in ((2 * (e % 2), k_sel, N_CMP), (2 * (e % 2) + 1, k_win, 0)):
                nc.tensor.matmul(ps[:, bank, 0:more + P], qT[r, f, 0:P], keys[r, 0:more + P], start=True, stop=True)
                last = nc.tensor.matmul(ps[:, bank, more + P:2 * more + 3 * P], qT[r, f, P:SEQ], keys[r, :], start=True, stop=True)
            last.then_inc(scored.sem, 1)

        pe.wait_ge(cmp_set.sem, cmp_set.count(l, 1))
        pe.wait_ge(s_set.sem, s_set.count(l, 2))
        scores(0)
        scores(1)
        pe.wait_ge(gla_o.sem, gla_o.count(l, 0))
        for f in range(2):
            for t in range(TT):
                last = nc.tensor.transpose(ps[:, 4, f * SEQ + t * P:f * SEQ + (t + 1) * P],
                                           o_gla[:, t * 256 + f * P:t * 256 + (f + 1) * P], ident)
        last.then_inc(gla_turned.sem, 1)

        pe.wait_ge(mixT_lo.sem, mixT_lo.count(l, 1))

        def turned_over(e):
            E = probs(e)
            pe.wait_ge(weighed.sem, weighed.count(l, e))
            if e:
                pe.wait_ge(pT_act.sem, pT_act.count(l, e - 1))
                pe.wait_ge(pT_dve.sem, pT_dve.count(l, e - 1))
            for b in range(2):
                for q in range(3):
                    nc.tensor.transpose(ps[:, 4 + b, q * P:(q + 1) * P], E[:, 384 * b + q * P:384 * b + (q + 1) * P], ident)
                last = nc.tensor.transpose(ps[0:N_CMP, 4 + b, 384:512], E[:, 768 + N_CMP * b:768 + N_CMP * (b + 1)], ident)
            last.then_inc(p_turned.sem, 1)

        def values(e):
            h = HEADS[e]
            f, g = h % 4, h // 4
            pe.wait_ge(pT_act.sem, pT_act.count(l, e))
            pe.wait_ge(pT_dve.sem, pT_dve.count(l, e))
            T = turned_probs(e)
            o = ps[64 * g:64 * g + 64, 6 + f // 2, (f % 2) * SEQ:(f % 2 + 1) * SEQ]
            for b in range(2):
                nc.tensor.matmul(o, v_tok[:, 0, P * b + 64 * g:P * b + 64 * g + 64], T[:, 384 * b:384 * b + SEQ],
                                 start=(b == 0), stop=False)
                nc.tensor.matmul(o[:, P:SEQ], v_tok[:, 1, P * b + 64 * g:P * b + 64 * g + 64],
                                 T[:, 384 * b + SEQ:384 * b + 384], start=False, stop=False)
            nc.tensor.matmul(o, vc[:, g, :], T[0:N_CMP, 768:768 + SEQ], start=False, stop=True).then_inc(summed.sem, 1)

        for e in range(10):
            if 1 <= e < 7:
                scores(e + 1)
            if 1 <= e <= 8:
                turned_over(e - 1)
            if e >= 2:
                values(e - 2)
        n1 = start["mix_out", l]
        open_accumulators(pe)
        pair = lambda t, r: t[:, 2 * r:2 * r + 2, :].rearrange("p k s -> p (k s)")
        for r in range(2):
            pe.wait_ge(mixT_lo.sem, mixT_lo.count(l, 2 + r))
            rows_product(pe, n1 + r, pair(aT_hi, r), pair(aT_lo, r))
        last_rows(pe, [(n1 + r, pair(aT_hi, r), pair(aT_lo, r), lambda: pe.wait_ge(mixT_lo.sem, mixT_lo.count(l, 1)))
                       for r in (2, 3)], 3 * l + 1)

    def probs(e):
        return cols(6, 1024 * (e % 2), 1024 * (e % 2) + 800)

    def turned_probs(e):
        return cols(7, 1024 * (e % 2), 1024 * (e % 2) + 1024)

    def mix_scalar(act, l):
        n0 = start["mix", l]
        dst = {0: cols(0, 0, 512), 1: cols(0, 512, 1024), 6: cols(1, 1536, 2048),
               7: cols(0, 1536, 2048)}
        for m in range(11):
            if m < 10:
                split_high(act, n0 + m + 3)
            if m in dst or m in (4, 10):
                act.wait_ge(weights_used, n0 + m + 1)
            if m == 4:
                nc.scalar.copy(k_sel[:, N_CMP:], ps[:, m, 0:SEQ])
                nc.scalar.copy(k_win, ps[:, m, SEQ:512]).then_inc(mix_act.sem, 1)
            if m in dst:
                nc.scalar.copy(dst[m], ps[:, m % 8, :]).then_inc(mix_act.sem, 1)
        nc.scalar.activation(gr, ps[:, 2, :], ACT.Silu).then_inc(mix_act.sem, 1)
        act.wait_ge(mix_dve.sem, mix_dve.count(l, 5))
        nc.scalar.activation(tanh_g, gka[:, :, 128:152], ACT.Tanh, scale=0.5).then_inc(gate_tanh.sem, 1)
        act.wait_ge(ga_turned.sem, ga_turned.count(l, 0))
        act.wait_ge(mix_set.sem, mix_set.count(l, 1))
        nc.scalar.copy(ga_T[0:16, :], ps[0:16, 1, 0:SEQ]).then_inc(ga_set.sem, 1)
        act.wait_ge(cmp_pre.sem, cmp_pre.count(l, 0))
        nc.scalar.activation(gelu_T.rearrange("p (v n) -> p v n", v=2),
                             ps[0:64, 0, 0:128].rearrange("p (v n) -> p v n", v=2)[:, :, 0:30],
                             ACT.Gelu_apprx_tanh).then_inc(cmp_act.sem, 1)
        act.wait_ge(pool_done.sem, pool_done.count(l, 0))
        nc.scalar.copy(pooledT, ps[:, 2, :]).then_inc(pool_set.sem, 1)
        ch = Chain(act, act_chain)
        ch.n = act_steps[0]
        act.wait_ge(la_pre.sem, la_pre.count(l, 0))
        ch.link(nc.scalar.activation(absz, ps[:, 3, 0:SEQ], ACT.Abs))
        ch.link(nc.scalar.activation(absz, absz, ACT.Exp, scale=-1.0))
        nc.scalar.activation(absz, absz, ACT.Ln, bias=1.0).then_inc(la_ln.sem, 1)
        act_steps[0] = ch.n
        act.wait_ge(b_sum.sem, b_sum.count(l, 0))
        nc.scalar.activation(E1, ps[:, 4, 0:SEQ], ACT.Exp, scale=1.0 / 16).then_inc(b_exp.sem, 1)
        nc.scalar.activation(E2, ps[:, 4, 0:SEQ], ACT.Exp, scale=-1.0 / 16).then_inc(b_exp.sem, 1)
        nc.scalar.activation(E3, ps[:, 4, SEQ:512], ACT.Exp, scale=1.0 / 16).then_inc(b_exp.sem, 1)
        act.wait_ge(pool_scaled.sem, pool_scaled.count(l, 3))
        nc.scalar.copy(aT_hi[:, 4:6, :], pool_y.rearrange("p (k s) -> p k s", s=SEQ)).then_inc(mixT_hi.sem, 1)
        act.wait_ge(inter.sem, inter.count(l, 0))
        nc.scalar.copy(o_gla, ps[:, 6, :]).then_inc(inter_set.sem, 1)
        act.wait_ge(gla_turned.sem, gla_turned.count(l, 0))
        nc.scalar.copy(aT_hi[:, 6:8, :], ps[:, 4, :].rearrange("p (k s) -> p k s", s=SEQ)).then_inc(mixT_hi.sem, 1)

        def exps(e):
            E, st = probs(e), stat[:, e % 2, :]
            act.wait_ge(peaked.sem, peaked.count(l, e))
            for k, s in enumerate(PART):
                last = nc.scalar.activation(E[:, s], E[:, s], ACT.Exp, bias=st[:, 6 + k:7 + k], scale=0.125,
                                            accum_out=st[:, 12 + k:13 + k])
            last.then_inc(exped.sem, 1)

        def copies(e):
            T = turned_probs(e)
            act.wait_ge(p_turned.sem, p_turned.count(l, e))
            if e >= 2:
                act.wait_ge(summed.sem, summed.count(l, e - 2))
            nc.scalar.copy(T[:, 0:768].rearrange("p (b s) -> p b s", b=2), ps[:, 4:6, 0:384]).then_inc(pT_act.sem, 1)

        for e in range(10):
            if e < 8:
                exps(e)
            if e == 1:
                split_high(act, n0 + 13)
            if 1 <= e <= 8:
                copies(e - 1)
            if e in (5, 9):
                act.wait_ge(summed.sem, summed.count(l, e - 2))
                a = 0 if e == 5 else 2
                nc.scalar.copy(aT_hi[:, a:a + 2, :], ps[:, 6 + a // 2, :].rearrange("p (k s) -> p k s", s=SEQ)).then_inc(mixT_hi.sem, 1)
        for r in range(2):
            split_high(act, start["mix_out", l] + r + 3)

    PART = [slice(0, P), slice(P, 384), slice(384, 384 + P), slice(384 + P, 768),
            slice(768, 768 + N_CMP), slice(768 + N_CMP, 768 + 2 * N_CMP)]

    def mix_vector(dve, l):
        n0 = start["mix", l]
        ch = Chain(dve, dve_chain)
        ch.n = dve_steps[0]
        for m in range(11):
            if m < 10:
                split_low(dve, n0 + m + 3)
            if m in (2, 3, 5, 8, 9):
                dve.wait_ge(weights_used, n0 + m + 1)
            if m in (2, 3):
                v = m - 2
                if v == 0:
                    dve.wait_ge(mix_landed.sem, 16 * MIX_LOADS * (l + 1))
                for r in range(2):
                    rows = slice(64 * r, 64 * r + 64)
                    src = window_view(ps[rows, m, :], r)
                    nc.vector.tensor_tensor(
                        blocks[rows, v, :, :].rearrange("p j (g n) -> p j g n", g=2), src,
                        cmp_pe[rows, v, :].unsqueeze(2).unsqueeze(3).to_broadcast([64, 16, 2, N_CMP]),
                        ALU.add).then_inc(mix_dve.sem, 1)
            elif m == 5:
                nc.vector.tensor_copy(cols(1, 1024, 1536), ps[:, 5, :]).then_inc(mix_dve.sem, 1)
            elif m == 8:
                nc.vector.tensor_copy(gka[:, :, 0:168], ps[:, 0, :].rearrange("p (t c) -> p t c", t=2)[:, :, 0:168]).then_inc(mix_dve.sem, 1)
            elif m == 9:
                nc.vector.tensor_copy(cols(2, 512, 1024), ps[:, 1, :]).then_inc(mix_dve.sem, 1)
        dve.wait_ge(gate_tanh.sem, gate_tanh.count(l, 0))
        tg = tanh_g.rearrange("p t (h b) -> p h b t", b=3)
        for k, b in enumerate((1, 2, 0)):
            m = ch.mark(nc.vector.tensor_scalar(gate[:, :, k, :], tg[:, :, b, :], 0.5, 0.5, ALU.mult, ALU.add))
        ch.wait(m)
        ch.link(nc.vector.tensor_tensor(gate[:, :, 2, :], gate[:, :, 2, :],
                                        consts[:, c_at["has_cmp"]].unsqueeze(1).to_broadcast([P, 8, 2]), ALU.mult))
        dve.wait_ge(la_ln.sem, la_ln.count(l, 0))
        nc.vector.scalar_tensor_tensor(out=la, in0=ps[:, 3, 0:SEQ], scalar=0.0, in1=absz, op0=ALU.min,
                                       op1=ALU.subtract).then_inc(la_set.sem, 1)
        dve.wait_ge(cmp_out.sem, cmp_out.count(l, 0))
        nc.vector.tensor_copy(kcT, ps[:, 0, 0:N_CMP]).then_inc(cmp_set.sem, 1)
        nc.vector.tensor_copy(vc.rearrange("p g d -> p (g d)"), ps[0:N_CMP, 1, 0:P]).then_inc(cmp_set.sem, 1)
        dve.wait_ge(pool_out.sem, pool_out.count(l, 0))
        for g in range(4):
            r = slice(64 * (g % 2), 64 * (g % 2) + 64)
            c = slice((g // 2) * SEQ, (g // 2 + 1) * SEQ)
            nc.vector.tensor_scalar(pool_y[r, c], ps[r, 6 + g % 2, c], pool_sc[r, g // 2:g // 2 + 1], None,
                                    ALU.mult).then_inc(pool_scaled.sem, 1)
        dve.wait_ge(b_exp.sem, b_exp.count(l, 0))
        nc.vector.scalar_tensor_tensor(out=qtT, in0=gqT, scalar=32.0 ** -0.5, in1=E1, op0=ALU.mult,
                                       op1=ALU.mult).then_inc(qk_set.sem, 1)
        dve.wait_ge(qk_set.sem, qk_set.count(l, 0))
        for t in range(TT):
            m = ch.mark(nc.vector.tensor_tensor(
                q_heads[:, t, :].rearrange("p (h s) -> p h s", h=4),
                qtT[:, t * P:(t + 1) * P].unsqueeze(1).to_broadcast([P, 4, P]),
                head_mask.rearrange("p (h v) -> p h v", h=4)[:, :, 0:1].to_broadcast([P, 4, P]), ALU.mult))
        dve.wait_ge(b_exp.sem, b_exp.count(l, 1))
        nc.vector.tensor_tensor(ktT, gkT, E2, ALU.mult).then_inc(qk_set.sem, 1)
        dve.wait_ge(b_exp.sem, b_exp.count(l, 2))
        nc.vector.tensor_tensor(k3[:], gka[:, :, 0:P], E3.rearrange("p (t c) -> p t c", c=P), ALU.mult).then_inc(qk_set.sem, 1)
        ch.wait(m)
        dve.wait_ge(mixT_hi.sem, mixT_hi.count(l, 0))
        nc.vector.tensor_tensor(aT_lo[:, 4:6, :], pool_y.rearrange("p (k s) -> p k s", s=SEQ),
                                aT_hi[:, 4:6, :].bitcast(F32), ALU.subtract).then_inc(mixT_lo.sem, 1)
        nc.vector.memset(stat[:, 0, 18:24], 0.0).then_inc(qk_set.sem, 1)
        for t in range(TT):
            dve.wait_ge(at_done.sem, at_done.count(l, t))
            nc.vector.tensor_tensor(att[:, t, :].rearrange("p (h s) -> p h s", h=4),
                                    ps[:, 2 + t, :].rearrange("p (h s) -> p h s", h=4),
                                    consts[:, c_at["upto"]].unsqueeze(1).to_broadcast([P, 4, P]),
                                    ALU.mult).then_inc(at_set.sem, 1)
        for c in range(3):
            dve.wait_ge(ds_done.sem, ds_done.count(l, c))
            ch.link(nc.vector.tensor_tensor(sq[:, 0:256], ps[:, c % 2, 0:256], head_mask, ALU.mult))
            if c:
                dve.wait_ge(s_set.sem, s_set.count(l, c - 1))
            else:
                dve.wait_ge(mix_set.sem, mix_set.count(l, 0))
            nc.vector.scalar_tensor_tensor(out=S_gla[:, c + 1, :], in0=S_gla[:, c, :], scalar=E1[:, 64 * c + 63:64 * c + 64],
                                           in1=sq[:, 0:256], op0=ALU.mult, op1=ALU.add).then_inc(s_set.sem, 1)
        dve.wait_ge(s_set.sem, s_set.count(l, 2))
        dve.wait_ge(inter_set.sem, inter_set.count(l, 0))
        dve.wait_ge(intra.sem, intra.count(l, 0))
        ch.link(nc.vector.tensor_tensor(o_gla, o_gla, ps[:, 7, :], ALU.add))
        ch.link(nc.vector.tensor_tensor(sq, o_gla, o_gla, ALU.mult))
        ch.link(nc.vector.tensor_reduce(ss_gla, sq.rearrange("p (h v) -> p h v", v=64), AX.X, ALU.add))
        nc.vector.tensor_scalar(ss_gla, ss_gla, 1.0 / 64, RMS_EPS, ALU.mult, ALU.add).then_inc(gla_ss.sem, 1)
        ch.link(nc.vector.tensor_tensor(o_gla.rearrange("p (t c) -> p t c", t=2), o_gla.rearrange("p (t c) -> p t c", t=2),
                                        gla_g.unsqueeze(1).to_broadcast([P, 2, 256]), ALU.mult))
        ch.link(nc.vector.tensor_tensor(o_gla, o_gla, gr, ALU.mult))
        dve.wait_ge(gla_rs.sem, gla_rs.count(l, 0))
        oh = o_gla.rearrange("p (h v) -> p h v", v=64)
        nc.vector.tensor_tensor(oh, oh, rs_gla.unsqueeze(2).to_broadcast([P, 8, 64]), ALU.mult).then_inc(gla_o.sem, 1)
        dve.wait_ge(mixT_hi.sem, mixT_hi.count(l, 1))
        nc.vector.tensor_tensor(aT_lo[:, 6:8, :], ps[:, 4, :].rearrange("p (k s) -> p k s", s=SEQ),
                                aT_hi[:, 6:8, :].bitcast(F32), ALU.subtract).then_inc(mixT_lo.sem, 1)

        causal, cmpm = consts[:, c_at["causal"]], consts[:, c_at["cmp_mask"]]

        def peaks(e):
            E, st = probs(e), stat[:, e % 2, :]
            b0 = 2 * (e % 2)
            dve.wait_ge(scored.sem, scored.count(l, e))
            if e >= 2:
                dve.wait_ge(p_turned.sem, p_turned.count(l, e - 2))
            second = N_CMP + P
            src = [ps[:, b0, N_CMP:second], ps[:, b0, second + N_CMP:second + N_CMP + SEQ],
                   ps[:, b0 + 1, 0:P], ps[:, b0 + 1, P:384],
                   ps[:, b0, 0:N_CMP], ps[:, b0, second:second + N_CMP]]
            mask = [causal[:, 0:P], causal[:, P:384]] * 2 + [cmpm[:, 0:N_CMP], cmpm[:, N_CMP:2 * N_CMP]]
            for k in range(6):
                m = ch.mark(nc.vector.tensor_tensor_reduce(out=E[:, PART[k]], in0=src[k], in1=mask[k], scale=1.0,
                                                           scalar=-3.0e38, op0=ALU.add, op1=ALU.max,
                                                           accum_out=st[:, k:k + 1]))
            ch.wait(m)
            nc.vector.tensor_scalar(st[:, 6:12], st[:, 0:6], -0.125, None, ALU.mult).then_inc(peaked.sem, 1)

        def weights(e):
            E, st, h = probs(e), stat[:, e % 2, :], HEADS[e]
            dve.wait_ge(exped.sem, exped.count(l, e))
            ch.link(nc.vector.reciprocal(st[:, 18:24], st[:, 12:18]))
            ch.link(nc.vector.tensor_tensor(st[:, 18:24], st[:, 18:24], gate[:, h, :, :].rearrange("p b t -> p (b t)"), ALU.mult))
            for k, s in enumerate(PART):
                last = nc.vector.tensor_scalar(E[:, s], E[:, s], st[:, 18 + k:19 + k], None, ALU.mult)
                if k < 5:
                    ch.mark(last)
            last.then_inc(weighed.sem, 1)

        def copies(e):
            T = turned_probs(e)
            dve.wait_ge(pT_act.sem, pT_act.count(l, e))
            nc.vector.tensor_copy(T[0:N_CMP, 768:1024].rearrange("p (b s) -> p b s", b=2), ps[0:N_CMP, 4:6, 384:512]).then_inc(pT_dve.sem, 1)

        peaks(0)
        for e in range(10):
            if e < 7:
                peaks(e + 1)
            if 1 <= e <= 8:
                copies(e - 1)
            if e < 8:
                weights(e)
            if e == 1:
                split_low(dve, n0 + 13)
            if e in (5, 9):
                a = 0 if e == 5 else 2
                dve.wait_ge(mixT_hi.sem, mixT_hi.count(l, 2 + a // 2))
                nc.vector.tensor_tensor(aT_lo[:, a:a + 2, :], ps[:, 6 + a // 2, :].rearrange("p (k s) -> p k s", s=SEQ),
                                        aT_hi[:, a:a + 2, :].bitcast(F32), ALU.subtract).then_inc(mixT_lo.sem, 1)
        dve_steps[0] = ch.n
        for r in range(2):
            split_low(dve, start["mix_out", l] + r + 3)

    def window_view(bank, r):
        base = bank[:, r:r + 1]
        return bass.AP(base.tensor, base.offset, [base.ap[0], [2, 16], [SEQ, 2], [CMP_STRIDE, N_CMP]])


    H = Z
    M = ws[9].rearrange("p (t c) -> p t c", c=D)
    junk = ws[1].rearrange("p (t c) -> p t c", c=D)
    pre_g = ws[7][:, 0:D]
    diag = ws[7][:, D:D + 2 * P].rearrange("p (t s) -> p t s", t=TT)
    ss2, ve2, rs2 = small[:, 226:228], small[:, 228:230], small[:, 230:232]
    ss3, ve3, rs3 = small[:, 232:236], small[:, 236:238], small[:, 238:240]
    ROOT_D = 32.0
    assert ROOT_D ** 2 == D

    pre_gain = signal("prenorm_gain_landed", 1)
    pre_sq = signal("prenorm_squares", TT)
    pre_rs = signal("prenorm_rsqrt", TT)
    pre_done = signal("prenorm_done", TT)
    add_gain = signal("addnorm_gain_landed", 1)
    add_sq = signal("addnorm_squares", 4)
    add_var = signal("addnorm_mean_square", TT)
    add_rs = signal("addnorm_rsqrt", TT)
    add_done = signal("addnorm_done", TT)

    def wait_x(eng, q, t):
        if q:
            eng.wait_ge(add_done.sem, add_done.count(q - 1, t))
        else:
            eng.wait_ge(ln_done.sem, ln_done.count(3 * DEPTH - 1, t))

    def x_squares(act, q, t):
        wait_x(act, q, t)
        nc.scalar.activation(junk[:, t, :], x[:, t, :], ACT.Square, accum_out=ss2[:, t:t + 1]).then_inc(pre_sq.sem, 1)

    def prenorm_scalar(act, q):
        for t in range(1 if q else 0, TT):
            x_squares(act, q, t)

    def scaled_x(dve, q, t):
        wait_x(dve, q, t)
        if t == 0:
            dve.wait_ge(pre_gain.sem, 16 * (q + 1))
        nc.vector.scalar_tensor_tensor(out=H[:, t, :], in0=x[:, t, :], scalar=ROOT_D, in1=pre_g, op0=ALU.mult, op1=ALU.mult)

    def token_factors(dve, q, t):
        dve.wait_ge(pre_rs.sem, pre_rs.count(q, t))
        nc.vector.tensor_scalar(diag[:, t, :], ident, rs2[:, t:t + 1], None, ALU.mult).then_inc(pre_done.sem, 1)

    def load_pre_gain(pool, q):
        if q % 2:
            pool.wait_ge(out_set.sem, out_set.count(q // 2, 1))
        elif q:
            pool.wait_ge(pre_done.sem, pre_done.count(q - 1, TT - 1))
        pool.dma_start(pre_g, w["norm_g_2"][q // 2, 2 * (q % 2):2 * (q % 2) + 1, :].to_broadcast([P, D])).then_inc(pre_gain.sem, 16)

    def x_rsqrt(pool, q, t):
        pool.wait_ge(pre_sq.sem, pre_sq.count(q, t))
        nc.gpsimd.tensor_tensor(ve2[:, t:t + 1], ss2[:, t:t + 1], eps_d, ALU.add).then_inc(pool_chain, 1)
        pool_steps[0] += 1
        pool.wait_ge(pool_chain, pool_steps[0])
        nc.gpsimd.tensor_tensor(rs2[:, t:t + 1], ve2[:, t:t + 1], mhalf[:, 0:1], ALU.pow).then_inc(pre_rs.sem, 1)

    def prenorm_pool(pool, q):
        for t in range(1 if q else 0, TT):
            x_rsqrt(pool, q, t)

    def prenorm_is_done(q):
        return lambda pe, t: pe.wait_ge(pre_done.sem, pre_done.count(q, t))

    def addnorm_scalar(act, a):
        for b in range(4):
            wait_y(act, 3 * DEPTH + a, b, add_last[a])
            nc.scalar.activation(junk[:, b // 2, b % 2 * 512:b % 2 * 512 + 512], ps[:, b, :], ACT.Square,
                                 accum_out=ss3[:, b:b + 1]).then_inc(add_sq.sem, 1)
            if b == 2 and a + 1 < 2 * DEPTH_2:
                x_squares(act, a + 1, 0)

    def addnorm_vector(dve, a):
        ch = Chain(dve, dve_chain)
        ch.n = dve_steps[0]
        following = a + 1 < 2 * DEPTH_2
        dve.wait_ge(add_gain.sem, 16 * (a + 1))
        for t in range(TT):
            for half in range(2):
                b, c = 2 * t + half, slice(512 * half, 512 * half + 512)
                if b == 3 and following:
                    token_factors(dve, a + 1, 0)
                dve.wait_ge(add_sq.sem, add_sq.count(a, b))
                if half:
                    nc.vector.scalar_tensor_tensor(out=ve3[:, t:t + 1], in0=ss3[:, b - 1:b], scalar=D * RMS_EPS, in1=ss3[:, b:b + 1],
                                                   op0=ALU.add, op1=ALU.add).then_inc(add_var.sem, 1)
                m = ch.mark(nc.vector.scalar_tensor_tensor(out=Z[:, t, c], in0=ps[:, b, :], scalar=ROOT_D, in1=gb[:, 1, c],
                                                           op0=ALU.mult, op1=ALU.mult))
            ch.wait(m)
            dve.wait_ge(add_rs.sem, add_rs.count(a, t))
            nc.vector.scalar_tensor_tensor(out=x[:, t, :], in0=Z[:, t, :], scalar=rs3[:, t:t + 1], in1=x[:, t, :],
                                           op0=ALU.mult, op1=ALU.add).then_inc(add_done.sem, 1)
            if following:
                scaled_x(dve, a + 1, t)
                if t:
                    token_factors(dve, a + 1, 1)
        dve_steps[0] = ch.n

    def prenorm_vector(dve, q):
        if q == 0:
            for t in range(TT):
                scaled_x(dve, q, t)
            for t in range(TT):
                token_factors(dve, q, t)

    def addnorm_pool(pool, a):
        if a:
            pool.wait_ge(add_done.sem, add_done.count(a - 1, TT - 1))
        pool.dma_start(gb[:, 1, :], w["norm_g_2"][a // 2, 1 + 2 * (a % 2):2 + 2 * (a % 2), :].to_broadcast([P, D])).then_inc(add_gain.sem, 16)
        if a + 1 < 2 * DEPTH_2:
            load_pre_gain(pool, a + 1)
        for t in range(TT):
            pool.wait_ge(add_var.sem, add_var.count(a, t))
            nc.gpsimd.tensor_tensor(rs3[:, t:t + 1], ve3[:, t:t + 1], mhalf[:, 0:1], ALU.pow).then_inc(add_rs.sem, 1)
            if t == 0 and a + 1 < 2 * DEPTH_2:
                x_rsqrt(pool, a + 1, 0)

    add_last = []
    for i in range(DEPTH_2):
        add_last += [start["out", i] + 3, start["mlp", i] + 2 * MLP_STEPS - 1]


    HN = 8
    param = gb[:, 0, :]
    m_landed = semaphore("mixer_parameters_landed")
    out_sq = signal("mixer_output_squares", 2)
    out_ss = signal("mixer_head_squares", 2)
    out_rs = signal("mixer_head_rsqrt", 2)
    out_set = signal("mixer_output_set", 2)
    M4 = ws[9].rearrange("p (t h v) -> p t h v", t=TT, v=P)
    head_ss, head_rs = (small[:, c:c + 16].rearrange("p (g c) -> p g c", g=2) for c in (240, 256))

    def output_group(i, g):
        if i % 3 == 0:
            return M4[:, g, :, :].unsqueeze(1), *(s.rearrange("p (t h v) -> p t h v", t=1, v=P)
                                                  for s in (ws[4][:, 0:D], ws[2][:, D:2 * D]))
        return M4[:, :, 4 * g:4 * g + 4, :], *(s.rearrange("p (t h v) -> p t h v", t=TT, v=P)
                                               for s in (ws[8][:, 0:D], ws[8][:, D:2 * D]))

    def head_norm_scalar(act, i, g):
        part, squares, _ = output_group(i, g)
        nc.scalar.activation(squares, part, ACT.Square).then_inc(out_sq.sem, 1)

    def head_squares_vector(dve, i, ch, g, factor, scale=None):
        part, squares, product = output_group(i, g)
        ss = head_ss[:, g, :]
        ch.mark(nc.vector.tensor_tensor(product, part, factor, ALU.mult))
        dve.wait_ge(out_sq.sem, out_sq.count(i, g))
        ch.link(nc.vector.tensor_reduce(ss.rearrange("p (t h) -> p t h", t=part.shape[1]), squares, AX.X, ALU.add))
        if scale is not None:
            ch.link(nc.vector.tensor_tensor(ss, ss, scale, ALU.mult))
        nc.vector.tensor_scalar(ss, ss, 1.0 / P, RMS_EPS, ALU.mult, ALU.add).then_inc(out_ss.sem, 1)

    def head_norm_vector(dve, i, ch, g):
        part, _, product = output_group(i, g)
        dve.wait_ge(out_rs.sem, out_rs.count(i, g))
        rs = head_rs[:, g, :].rearrange("p (t h) -> p t h", t=part.shape[1])
        nc.vector.tensor_tensor(part, product, rs.unsqueeze(3).to_broadcast(list(part.shape)), ALU.mult).then_inc(out_set.sem, 1)

    def head_norm_pool(pool, i):
        for g in range(2):
            pool.wait_ge(out_ss.sem, out_ss.count(i, g))
            nc.gpsimd.tensor_tensor(head_rs[:, g, :], head_ss[:, g, :], mhalf[:, 0:8], ALU.pow).then_inc(out_rs.sem, 1)

    def out_order(i):
        return [(t, half) for t in range(TT) for half in range(2)] if i % 3 == 0 else [(t, half) for half in range(2) for t in range(TT)]

    def out_tensor(pe, i, xpass):
        by_tile = i % 3 == 0
        for e, (t, half) in enumerate(out_order(i)):
            if e % 2 == 0:
                pe.wait_ge(out_set.sem, out_set.count(i, e // 2))
            if e == 1 and not by_tile:
                pe.wait_ge(taken.sem, taken.count(i - 1, HN - 1))
            turn_bank(pe, M, t, half)
        open_accumulators(pe)
        pair = lambda t, r: t[:, 2 * r:2 * r + 2, :].rearrange("p k s -> p (k s)")
        first, second = (lambda k=k: pe.wait_ge(aT_lo_set.sem, aT_lo_set.count(xpass, k)) for k in ((2 if by_tile else 1), 3))
        first()
        for r in range(2):
            rows_product(pe, start["out", i] + r, pair(aT_hi, r), pair(aT_lo, r))
        last_rows(pe, [(start["out", i] + r, pair(aT_hi, r), pair(aT_lo, r), second) for r in (2, 3)], 3 * DEPTH + 2 * i)

    def out_scalar(act, i, xpass):
        turn_scalar(act, xpass, out_order(i))
        for r in range(2):
            split_high(act, start["out", i] + r + 3)

    def out_vector(dve, i, xpass):
        turn_vector(dve, xpass, out_order(i))
        for r in range(2):
            split_low(dve, start["out", i] + r + 3)

    
    loads_upto = [5, 8, 12, 17]

    def wait_params(eng, i):
        eng.wait_ge(m_landed, 16 * loads_upto[i])

    def mixer_sync(sp, i):
        def load(dst, src):
            sp.dma_start(dst, src).then_inc(m_landed, 16)

        for n in range(start["in", i], start["out", i] + 4):
            load_chunk(sp, n)
            if n == start["in", i] + 1:
                if i:
                    sp.wait_ge(out_set.sem, out_set.count(i - 1, 1))
                else:
                    sp.wait_ge(ln_done.sem, ln_done.count(3 * DEPTH - 1, TT - 1))
                (gdn_parameters, mlstm_parameters, diff_parameters)[i % 3](load, i)

    def mixer_pool(pool, i):
        if i % 3 == 0:
            gdn_pool(pool, i)
        head_norm_pool(pool, i)

    def mixer_tensor(pe, i, xpass, xpass_out):
        wait_turned(pe, xpass)
        (gdn_tensor, mlstm_tensor, diff_tensor)[i % 3](pe, i)
        out_tensor(pe, i, xpass_out)

    def mixer_scalar(act, i, xpass_out):
        ch = Chain(act, act_chain)
        ch.n = act_steps[0]
        (gdn_scalar, mlstm_scalar, diff_scalar)[i % 3](act, i, ch)
        act_steps[0] = ch.n
        out_scalar(act, i, xpass_out)

    def mixer_vector(dve, i, xpass_out):
        ch = Chain(dve, dve_chain)
        ch.n = dve_steps[0]
        (gdn_vector, mlstm_vector, diff_vector)[i % 3](dve, i, ch)
        dve_steps[0] = ch.n
        out_vector(dve, i, xpass_out)


    def gated(n0, m):
        return n0 + (m if m > 1 else 0)

    qT4 = cols(0, 0, 1024).rearrange("p (f s) -> p f s", s=SEQ)
    kT4 = cols(0, 1024, 2048).rearrange("p (f s) -> p f s", s=SEQ)
    v8 = ws[4].rearrange("p (t c) -> p t c", c=D)
    og = ws[5].rearrange("p (t c) -> p t c", c=D)
    tri = param[:, 0:P]
    gate_b = param[:, P:P + 16]
    ml_gain = ws[3][:, 0:D]
    raw_g = small[:, 272:304].rearrange("p (t c) -> p t c", c=16)
    lnf = small[:, 304:320].rearrange("p (t h) -> p t h", h=HN)
    absf = small[:, 320:336].rearrange("p (t h) -> p t h", h=HN)
    Bsum = small[:, 336:352].rearrange("p (t h) -> p t h", h=HN)
    cgate = small[:, 352:368].rearrange("p (t h) -> p t h", h=HN)
    ml_st = small[:, 368:400].rearrange("p (r c) -> p r c", c=16)

    ml_pre = signal("mlstm_gate_biased", 1)
    ml_tanh = signal("mlstm_gate_tanh", 1)
    ml_cap = signal("mlstm_gate_capped", 1)
    ml_ln = signal("mlstm_log_set", 1)
    ml_lf = signal("mlstm_log_forget", 1)
    ml_B = signal("mlstm_running_sum", 1)
    ml_c = signal("mlstm_key_bias", 1)
    ml_act = signal("mlstm_projected_by_act", 8)
    ml_dve = signal("mlstm_projected_by_dve", 4)
    taken = signal("values_taken", HN)

    def mlstm_parameters(load, i):
        load(tri, w["const_tri"])
        load(gate_b, w["mlstm_gate_b_2"].rearrange("n a h -> n (a h)").to_broadcast([P, 16]))
        load(ml_gain, w["mlstm_norm_g_2"].to_broadcast([P, D]))

    def running_sums(pe, i):
        wait_params(pe, i)
        pe.wait_ge(ml_lf.sem, 1)
        for t in range(TT):
            o = ps[:, 6, HN * t:HN * (t + 1)]
            if t:
                nc.tensor.matmul(o, tri[:, P - 1:P].to_broadcast([P, P]), lnf[:, 0, :], start=True, stop=False)
            last = nc.tensor.matmul(o, tri, lnf[:, t, :], start=(t == 0), stop=True)
        last.then_inc(ml_B.sem, 1)

    def mlstm_tensor(pe, i):
        n0 = start["in", i]
        for m in range(1, 13):
            if m == 2:
                tokens_product(pe, n0 + 1, 7, 16)
            if m == 7:
                running_sums(pe, i)
            if m > 4:
                e = m - 4
                if e <= 4:
                    pe.wait_ge(ml_act.sem, ml_act.count(0, e - 1))
                else:
                    pe.wait_ge(ml_dve.sem, ml_dve.count(0, e - 5))
            if m <= 4:
                features_product(pe, gated(n0, m), (m - 1) % 4)
            else:
                tokens_product(pe, gated(n0, m), (m - 1) % 4)
        pe.wait_ge(ml_c.sem, 1)

        def scores(h):
            r = slice(64 * (h % 2), 64 * (h % 2) + 64)
            if h < 2:
                pe.wait_ge(ml_act.sem, ml_act.count(0, 6 + h))
            if h >= 2:
                pe.wait_ge(weighed.sem, weighed.count(2, h - 2))
            b = h % 2
            nc.tensor.matmul(ps[:, b, 0:P], qT4[r, h // 2, 0:P], kT4[r, h // 2, 0:P], start=True, stop=True)
            nc.tensor.matmul(ps[:, b, P:384], qT4[r, h // 2, P:SEQ], kT4[r, h // 2, :], start=True, stop=True)
            for t in range(TT):
                last = nc.tensor.matmul(ps[:, 2 + b, t * P:(t + 1) * P], cgate[:, t, h:h + 1].to_broadcast([P, P]),
                                        ident, start=True, stop=True)
            last.then_inc(scored.sem, 1)

        scores(0)
        for h in range(HN + 2):
            if h < HN - 1:
                scores(h + 1)
            if 1 <= h <= HN:
                pe.wait_ge(weighed.sem, weighed.count(2, h - 1))
                weights_over(pe, h - 1, 0)
            if h >= 2:
                weighted_values(pe, h - 2, 0)

    def weights_over(pe, h, turn):
        b = h % 2
        E = head_probs(h)
        if h >= 2:
            pe.wait_ge(pT_act.sem, pT_act.count(DEPTH + turn, h - 2))
        for q in range(3):
            last = nc.tensor.transpose(ps[:, 4 + b, q * P:(q + 1) * P], E[:, q * P:(q + 1) * P], ident)
        last.then_inc(p_turned.sem, 1)

    def weighted_values(pe, h, turn):
        b = h % 2
        T = head_turned(h)
        pe.wait_ge(pT_act.sem, pT_act.count(DEPTH + turn, h))
        if h >= 2:
            pe.wait_ge(taken.sem, taken.count(turn, h - 2))
        v = slice(h * P, (h + 1) * P)
        nc.tensor.matmul(ps[:, 6 + b, 0:P], T[:, 0:P], v8[:, 0, v], start=True, stop=True)
        nc.tensor.matmul(ps[:, 6 + b, P:SEQ], T[:, P:SEQ], v8[:, 0, v], start=True, stop=False)
        nc.tensor.matmul(ps[:, 6 + b, P:SEQ], T[:, SEQ:384], v8[:, 1, v], start=False, stop=True).then_inc(summed.sem, 1)

    def head_probs(h):
        return cols(6, 1024 * (h % 2), 1024 * (h % 2) + 768)

    def head_turned(h):
        return cols(7, 512 * (h % 2), 512 * (h % 2) + 384)

    def mlstm_scalar(act, i, ch):
        n0 = start["in", i]
        for m in range(1, 13):
            if m < 12:
                split_high(act, gated(n0, m) + 3)
            b = (m - 1) % 4
            if m <= 4:
                act.wait_ge(weights_used, gated(n0, m) + 1)
                dst = cols(0, 512 * (m - 1), 512 * m)
                nc.scalar.copy(dst, ps[:, b, :]).then_inc(ml_act.sem, 1)
            elif m >= 9:
                act.wait_ge(weights_used, gated(n0, m) + 1)
                c = slice(CW * (m - 9), CW * (m - 8))
                nc.scalar.activation(og[:, :, c], ps[:, b, :].rearrange("p (t c) -> p t c", t=TT), ACT.Tanh, scale=0.5).then_inc(ml_act.sem, 1)
            if m == 1:
                split_high(act, n0 + 4)
                act.wait_ge(ml_pre.sem, 1)
                nc.scalar.activation(raw_g[:], raw_g[:], ACT.Tanh, scale=1.0 / 15).then_inc(ml_tanh.sem, 1)
            if m == 3:
                act.wait_ge(ml_cap.sem, 1)
                ch.link(nc.scalar.activation(absf[:], raw_g[:, :, 8:16], ACT.Abs))
                ch.link(nc.scalar.activation(absf[:], absf[:], ACT.Exp, scale=-1.0))
                nc.scalar.activation(absf[:], absf[:], ACT.Ln, bias=1.0).then_inc(ml_ln.sem, 1)

        def copies(h):
            act.wait_ge(p_turned.sem, p_turned.count(2, h))
            if h >= 2:
                act.wait_ge(summed.sem, summed.count(2, h - 2))
            nc.scalar.copy(head_turned(h), ps[:, 4 + h % 2, 0:384]).then_inc(pT_act.sem, 1)

        for h in range(HN + 2):
            if h < HN:
                st, E = ml_st[:, h % 2, :], cols(6, 1024 * (h % 2) + 512, 1024 * (h % 2) + 896)
                act.wait_ge(peaked.sem, peaked.count(2, h))
                nc.scalar.activation(E[:, 0:P], E[:, 0:P], ACT.Exp, bias=st[:, 2:3])
                nc.scalar.activation(E[:, P:384], E[:, P:384], ACT.Exp, bias=st[:, 3:4])
                nc.scalar.activation(st[:, 4:6], st[:, 4:6], ACT.Exp).then_inc(exped.sem, 1)
            if h == 1:
                split_high(act, n0 + 15)
            if 1 <= h <= HN:
                copies(h - 1)
            if h in (5, 9):
                act.wait_ge(taken.sem, taken.count(0, h - 2))
                head_norm_scalar(act, i, h // 9)

    def output_gate_vector(dve, ch, e):
        c = slice(CW * e, CW * (e + 1))
        dve.wait_ge(ml_act.sem, ml_act.count(0, 4 + e))
        ch.link(nc.vector.tensor_scalar(og[:, :, c], og[:, :, c], 0.5, 0.5, ALU.mult, ALU.add))
        ch.mark(nc.vector.tensor_tensor(og[:, :, c], og[:, :, c], ml_gain[:, c].unsqueeze(1).to_broadcast([P, TT, CW]), ALU.mult))

    def mlstm_vector(dve, i, ch):
        n0 = start["in", i]
        wait_params(dve, i)
        for m in range(1, 13):
            if m < 12:
                split_low(dve, gated(n0, m) + 3)
            if 5 <= m <= 8:
                dve.wait_ge(weights_used, n0 + m + 1)
                c = slice(CW * (m - 5), CW * (m - 4))
                nc.vector.tensor_copy(v8[:, :, c], ps[:, (m - 1) % 4, :].rearrange("p (t c) -> p t c", t=TT)).then_inc(ml_dve.sem, 1)
            if m == 1:
                split_low(dve, n0 + 4)
                dve.wait_ge(weights_used, n0 + 2)
                nc.vector.tensor_tensor(raw_g[:], ps[:, 7, :].rearrange("p (t c) -> p t c", t=TT)[:, :, 0:16],
                                        gate_b.unsqueeze(1).to_broadcast([P, TT, 16]), ALU.add).then_inc(ml_pre.sem, 1)
            if m == 2:
                dve.wait_ge(ml_tanh.sem, 1)
                nc.vector.tensor_scalar(raw_g[:], raw_g[:], 15.0, None, ALU.mult).then_inc(ml_cap.sem, 1)
            if m == 4:
                dve.wait_ge(ml_ln.sem, 1)
                dve.wait_ge(ml_cap.sem, 1)
                nc.vector.scalar_tensor_tensor(out=lnf[:], in0=raw_g[:, :, 8:16], scalar=0.0, in1=absf[:], op0=ALU.min,
                                               op1=ALU.subtract).then_inc(ml_lf.sem, 1)
            if m == 8:
                dve.wait_ge(ml_B.sem, 1)
                ch.mark(nc.vector.tensor_copy(Bsum[:], ps[:, 6, 0:16].rearrange("p (t h) -> p t h", h=HN)))
                nc.vector.tensor_tensor(cgate[:], raw_g[:, :, 0:8], ps[:, 6, 0:16].rearrange("p (t h) -> p t h", h=HN),
                                        ALU.subtract).then_inc(ml_c.sem, 1)
            if m >= 10:
                output_gate_vector(dve, ch, m - 10)
        output_gate_vector(dve, ch, 3)
        ch.wait()
        causal = consts[:, c_at["causal"]]

        def peaks(h):
            st, b = ml_st[:, h % 2, :], h % 2
            E = cols(6, 1024 * b + 512, 1024 * b + 896)
            dve.wait_ge(scored.sem, scored.count(2, h))
            ch.mark(nc.vector.tensor_tensor_reduce(out=E[:, 0:P], in0=ps[:, 2 + b, 0:P], in1=causal[:, 0:P], scale=1.0,
                                                   scalar=-3.0e38, op0=ALU.add, op1=ALU.max, accum_out=st[:, 0:1]))
            ch.link(nc.vector.tensor_tensor_reduce(out=E[:, P:384], in0=ps[:, 2 + b, 0:SEQ], in1=causal[:, P:384], scale=1.0,
                                                   scalar=-3.0e38, op0=ALU.add, op1=ALU.max, accum_out=st[:, 1:2]))
            ch.link(nc.vector.tensor_scalar(st[:, 2:4], st[:, 0:2], 0.0, -1.0, ALU.max, ALU.mult))
            nc.vector.tensor_tensor(st[:, 4:6], st[:, 2:4], Bsum[:, :, h], ALU.subtract).then_inc(peaked.sem, 1)

        def weights(h):
            st, b = ml_st[:, h % 2, :], h % 2
            E, Pw = cols(6, 1024 * b + 512, 1024 * b + 896), head_probs(h)
            dve.wait_ge(exped.sem, exped.count(2, h))
            if h >= 2:
                dve.wait_ge(p_turned.sem, p_turned.count(2, h - 2))
            ch.mark(nc.vector.tensor_tensor_reduce(out=Pw[:, 0:P], in0=ps[:, b, 0:P], in1=E[:, 0:P], scale=0.125, scalar=0.0,
                                                   op0=ALU.mult, op1=ALU.add, accum_out=st[:, 6:7]))
            nc.vector.tensor_tensor_reduce(out=Pw[:, P:384], in0=ps[:, b, P:384], in1=E[:, P:384], scale=0.125, scalar=0.0,
                                           op0=ALU.mult, op1=ALU.add, accum_out=st[:, 7:8]).then_inc(weighed.sem, 1)
            dve.wait_ge(weighed.sem, weighed.count(2, h))
            ch.link(nc.vector.scalar_tensor_tensor(out=st[:, 8:10], in0=st[:, 6:8], scalar=-1.0, in1=st[:, 6:8],
                                                   op0=ALU.mult, op1=ALU.max))
            ch.link(nc.vector.tensor_tensor(st[:, 8:10], st[:, 8:10], st[:, 4:6], ALU.max))
            ch.link(nc.vector.reciprocal(st[:, 10:12], st[:, 8:10]))

        def scaled(h):
            st, b = ml_st[:, h % 2, :], h % 2
            dve.wait_ge(summed.sem, summed.count(2, h))
            ch.mark(nc.vector.tensor_scalar(M4[:, 0, h, :], ps[:, 6 + b, 0:P], st[:, 10:11], None, ALU.mult))
            nc.vector.tensor_scalar(M4[:, 1, h, :], ps[:, 6 + b, P:SEQ], st[:, 11:12], None, ALU.mult).then_inc(taken.sem, 1)

        peaks(0)
        for h in range(HN + 2):
            if h < HN - 1:
                peaks(h + 1)
            if h >= 2:
                scaled(h - 2)
            if h < HN:
                weights(h)
            if h == 1:
                split_low(dve, n0 + 15)
            if h in (5, 9):
                g = h // 9
                dve.wait_ge(taken.sem, taken.count(0, 4 * g + 3))
                head_squares_vector(dve, i, ch, g, og.rearrange("p t (h v) -> p t h v", v=P)[:, :, 4 * g:4 * g + 4, :])
            if h in (6, 9):
                head_norm_vector(dve, i, ch, h // 9)


    q_tok = ws[1].rearrange("p (t h c) -> p t h c", t=TT, c=64)
    k_tok = ws[3].rearrange("p (t h c) -> p t h c", t=TT, c=64)
    qT8 = ws[0].rearrange("p (f s) -> p f s", s=SEQ)
    kT8 = ws[2].rearrange("p (f s) -> p f s", s=SEQ)
    rope = param[:, 0:2 * ROT].rearrange("p (t a c) -> p t a c", t=TT, a=2)
    lam_p = param[:, 32:288]
    df_gain = param[:, 288:416]
    chunk_mask = param[:, 416:800]
    rt = ws[8].rearrange("p (k t h c) -> p k t h c", k=8, t=TT, c=8)
    df_st = small[:, 400:480].rearrange("p (r c) -> p r c", c=40)
    lam = small[:, 480:488]
    LAMBDA_INIT = 0.8 - 0.6 * math.exp(-0.3 * 2)

    df_act = signal("diff_projected_by_act", 12)
    df_rot = signal("diff_rotated", 2)
    df_turned = signal("diff_qk_turned", 8)
    df_tcopy = signal("diff_qk_turned_copied", 8)
    df_lam = signal("diff_lambda_sums", 1)
    df_lexp = signal("diff_lambda_exps", 1)

    def diff_parameters(load, i):
        load(param[:, 0:2 * ROT], w["const_rope"])
        load(lam_p, w["diff_lambda_2"].rearrange("n a d -> n (a d)").to_broadcast([P, 256]))
        load(chunk_mask, w["const_chunks"])
        load(df_gain, w["diff_norm_g_2"].to_broadcast([P, P]))

    def diff_tensor(pe, i):
        n0 = start["in", i]
        for m in range(12):
            if m >= 4:
                pe.wait_ge(df_act.sem, df_act.count(0, m - 4))
            if m in (8, 11):
                v, src = (0, ws[1]) if m == 8 else (1, ws[3])
                pe.wait_ge(df_rot.sem, df_rot.count(0, v))
                for b in range(4):
                    if v:
                        pe.wait_ge(df_tcopy.sem, df_tcopy.count(0, b))
                    for a in range(2):
                        for t in range(TT):
                            f = 2 * b + a
                            last = nc.tensor.transpose(ps[:, 4 + b, a * SEQ + t * P:a * SEQ + (t + 1) * P],
                                                       src[:, t * D + f * P:t * D + (f + 1) * P], ident)
                    last.then_inc(df_turned.sem, 1)
            tokens_product(pe, n0 + m, m % 4)
        pe.wait_ge(df_tcopy.sem, df_tcopy.count(0, 7))
        pe.wait_ge(df_act.sem, df_act.count(0, 11))

        def scores(h):
            if h >= 2:
                pe.wait_ge(peaked.sem, peaked.count(3, h - 2))
            for c in range(2):
                r, b = slice(64 * c, 64 * c + 64), 2 * (h % 2) + c
                nc.tensor.matmul(ps[:, b, 0:P], qT8[r, h, 0:P], kT8[r, h, 0:P], start=True, stop=True)
                last = nc.tensor.matmul(ps[:, b, P:384], qT8[r, h, P:SEQ], kT8[r, h, :], start=True, stop=True)
            last.then_inc(scored.sem, 1)

        scores(0)
        for h in range(HN + 2):
            if h < HN - 1:
                scores(h + 1)
            if 1 <= h <= HN:
                pe.wait_ge(weighed.sem, weighed.count(3, h - 1))
                weights_over(pe, h - 1, 1)
            if h >= 2:
                weighted_values(pe, h - 2, 1)

    def diff_scalar(act, i, ch):
        n0 = start["in", i]
        dst = [ws[1], ws[3], ws[4]]

        def turned_copies(v):
            for b in range(4 * v, 4 * v + 4):
                act.wait_ge(df_turned.sem, df_turned.count(0, b))
                nc.scalar.copy((qT8, kT8)[v][:, 2 * (b % 4):2 * (b % 4) + 2, :],
                               ps[:, 4 + b % 4, :].rearrange("p (a s) -> p a s", a=2)).then_inc(df_tcopy.sem, 1)

        for m in range(12):
            if m < 11:
                split_high(act, n0 + m + 3)
            if m == 11:
                turned_copies(1)
            act.wait_ge(weights_used, n0 + m + 1)
            c = slice(CW * (m % 4), CW * (m % 4 + 1))
            nc.scalar.copy(dst[m // 4].rearrange("p (t c) -> p t c", c=D)[:, :, c],
                           ps[:, m % 4, :].rearrange("p (t c) -> p t c", t=TT)).then_inc(df_act.sem, 1)
            if m == 8:
                turned_copies(0)
        act.wait_ge(df_lam.sem, 1)
        nc.scalar.activation(lam[:, 2:4], lam[:, 0:2], ACT.Exp).then_inc(df_lexp.sem, 1)
        for h in range(HN + 2):
            if h < HN:
                st, E = df_st[:, h % 2, :], head_probs(h)
                act.wait_ge(peaked.sem, peaked.count(3, h))
                for k, s in enumerate(DIFF_PART):
                    last = nc.scalar.activation(E[:, s], E[:, s], ACT.Exp, bias=st[:, 4 + k:5 + k], scale=0.125,
                                                accum_out=st[:, 8 + k:9 + k])
                last.then_inc(exped.sem, 1)
            if h == 1:
                split_high(act, n0 + 14)
            if 1 <= h <= HN:
                act.wait_ge(p_turned.sem, p_turned.count(3, h - 1))
                if h >= 3:
                    act.wait_ge(summed.sem, summed.count(3, h - 3))
                nc.scalar.copy(head_turned(h - 1), ps[:, 4 + (h - 1) % 2, 0:384]).then_inc(pT_act.sem, 1)
            if h >= 2:
                act.wait_ge(summed.sem, summed.count(3, h - 2))
                nc.scalar.copy(M4[:, :, h - 2, :], ps[:, 6 + h % 2, 0:SEQ].rearrange("p (t v) -> p t v", t=TT)).then_inc(taken.sem, 1)
            if h in (5, 9):
                act.wait_ge(taken.sem, taken.count(1, h - 2))
                head_norm_scalar(act, i, h // 9)

    DIFF_PART = [slice(0, P), slice(P, 384), slice(384, 512), slice(512, 768)]

    def diff_vector(dve, i, ch):
        n0 = start["in", i]
        wait_params(dve, i)
        ch.link(nc.vector.tensor_tensor_reduce(out=rt[:, 7, 0, :, :].rearrange("p h c -> p (h c)")[:, 0:64], in0=lam_p[:, 0:64],
                                               in1=lam_p[:, 64:128], scale=1.0, scalar=0.0, op0=ALU.mult, op1=ALU.add,
                                               accum_out=lam[:, 0:1]))
        nc.vector.tensor_tensor_reduce(out=rt[:, 7, 1, :, :].rearrange("p h c -> p (h c)")[:, 0:64], in0=lam_p[:, 128:192],
                                       in1=lam_p[:, 192:256], scale=1.0, scalar=0.0, op0=ALU.mult, op1=ALU.add,
                                       accum_out=lam[:, 1:2]).then_inc(df_lam.sem, 1)

        def rotate(v, tok):
            x1, x2 = tok[:, :, :, 0:8], tok[:, :, :, 8:16]
            cs = [rope[:, :, a, :].unsqueeze(2).to_broadcast([P, TT, 16, 8]) for a in range(2)]
            k0 = 0
            marks = []
            for k, (a, b) in enumerate(((x1, cs[0]), (x2, cs[1]), (x1, cs[1]), (x2, cs[0]))):
                for t in range(TT):
                    marks.append(ch.mark(nc.vector.tensor_tensor(rt[:, k0 + k, t, :, :], a[:, t], b[:, t], ALU.mult)))
            ch.wait()
            for t in range(TT):
                ch.mark(nc.vector.tensor_tensor(x1[:, t], rt[:, k0, t], rt[:, k0 + 1, t], ALU.subtract))
                last = nc.vector.tensor_tensor(x2[:, t], rt[:, k0 + 2, t], rt[:, k0 + 3, t], ALU.add)
                if t == 0:
                    ch.mark(last)
            last.then_inc(df_rot.sem, 1)
            dve.wait_ge(df_rot.sem, df_rot.count(0, v))

        for m in range(12):
            if m < 11:
                split_low(dve, n0 + m + 3)
            if m in (5, 9):
                dve.wait_ge(df_act.sem, df_act.count(0, m - 2))
                rotate(m // 8, (q_tok, k_tok)[m // 8])
        dve.wait_ge(df_lexp.sem, 1)
        ch.link(nc.vector.tensor_tensor(lam[:, 4:5], lam[:, 3:4], lam[:, 2:3], ALU.subtract))
        ch.link(nc.vector.tensor_scalar(lam[:, 5:6], lam[:, 4:5], LAMBDA_INIT, None, ALU.subtract))

        def peaks(h):
            E, st, b0 = head_probs(h), df_st[:, h % 2, :], 2 * (h % 2)
            dve.wait_ge(scored.sem, scored.count(3, h))
            if h >= 2:
                dve.wait_ge(p_turned.sem, p_turned.count(3, h - 2))
            for k, s in enumerate(DIFF_PART):
                c = (slice(0, P), slice(P, 384))[k % 2]
                ch.mark(nc.vector.tensor_tensor_reduce(out=E[:, s], in0=ps[:, b0 + k // 2, c], in1=chunk_mask[:, c], scale=1.0,
                                                       scalar=-3.0e38, op0=ALU.add, op1=ALU.max, accum_out=st[:, k:k + 1]))
            ch.wait()
            nc.vector.tensor_scalar(st[:, 4:8], st[:, 0:4], -0.125, None, ALU.mult).then_inc(peaked.sem, 1)

        def weights(h):
            E, st = head_probs(h), df_st[:, h % 2, :]
            dve.wait_ge(exped.sem, exped.count(3, h))
            ch.link(nc.vector.reciprocal(st[:, 12:16], st[:, 8:12]))
            ch.link(nc.vector.tensor_scalar(st[:, 14:16], st[:, 14:16], lam[:, 5:6], None, ALU.mult))
            for t in range(TT):
                ch.mark(nc.vector.tensor_scalar(E[:, DIFF_PART[2 + t]], E[:, DIFF_PART[2 + t]], st[:, 14 + t:15 + t], None, ALU.mult))
            ch.wait()
            for t in range(TT):
                last = nc.vector.scalar_tensor_tensor(out=E[:, DIFF_PART[t]], in0=E[:, DIFF_PART[t]], scalar=st[:, 12 + t:13 + t],
                                                      in1=E[:, DIFF_PART[2 + t]], op0=ALU.mult, op1=ALU.add)
                if t == 0:
                    ch.mark(last)
            last.then_inc(weighed.sem, 1)

        ch.link(nc.vector.tensor_scalar(df_gain, df_gain, 1.0 - LAMBDA_INIT, None, ALU.mult))
        peaks(0)
        for h in range(HN):
            if h < HN - 1:
                peaks(h + 1)
            weights(h)
            if h == 1:
                split_low(dve, n0 + 14)
            if h in (5, 7):
                g = h // 7
                dve.wait_ge(taken.sem, taken.count(1, 4 * g + 3))
                head_squares_vector(dve, i, ch, g, df_gain.unsqueeze(1).unsqueeze(1).to_broadcast([P, TT, 4, P]))
            if h in (6, 7):
                head_norm_vector(dve, i, ch, h - 6)


    g_qT = ws[0].rearrange("p (f s) -> p f s", s=SEQ)
    g_kT = ws[1].rearrange("p (f s) -> p f s", s=SEQ)
    g_vT = ws[9].rearrange("p (f s) -> p f s", s=SEQ)
    g_kbT = ws[8].rearrange("p (f s) -> p f s", s=SEQ)

    def by_head(k):
        return ws[k].rearrange("p (t h v) -> p t h v", t=TT, v=P)

    g_kb, g_k, g_v, g_z, g_dec, g_A, g_Y, g_T, g_TT = (by_head(k) for k in (2, 3, 4, 5, 6, 7, 1, 8, 9))
    g_value, g_kcdT, g_S2 = by_head(1), by_head(7), ws[8].rearrange("p (r c) -> p r c", r=2)
    g_Sd = ws[2][:, 0:D]
    levels = param[:, 0:LEVELS * P].rearrange("p (v s) -> p v s", s=P)
    g_gain = param[:, 768:896]
    conv_rows = param[0:96, 896:1024]
    conv_w = small[:, 488:584].rearrange("p (j f) -> p j f", j=4)
    a_log, dt_b = small[:, 584:592], small[:, 592:600]
    th = lambda k: small[:, 272 + 16 * k:288 + 16 * k].rearrange("p (t h) -> p t h", h=HN)
    g_g, g_ln, g_beta, g_gc, g_eg, g_es, g_brk, g_rkes = (th(k) for k in range(8))
    g_el = small[:, 400:432].rearrange("p (c h) -> p c h", h=HN)
    g_r = small[:, 432:464].rearrange("p (a t h) -> p a t h", a=2, h=HN)
    g_ea = small[:, 464:472]
    g_rq2 = small[:, 472:488].rearrange("p (t h) -> p t h", h=HN)

    gp = lambda name, per: signal("gdn_" + name, per)
    gd_cwT, gd_cw = gp("taps_turned", 1), gp("taps_set", 1)
    gd_u, gd_lnset, gd_tb, gd_g = gp("decay_input", 1), gp("decay_logs", 1), gp("beta_tanh", 1), gp("log_decay", 1)
    gd_tap0, gd_conv, gd_silu = gp("first_tap", 12), gp("convolved", 12), gp("activated", 12)
    gd_z = gp("output_gate", 4)
    gd_sums, gd_sexp, gd_rows, gd_D, gd_Dexp, gd_dec = (gp("chunk_sums", 1), gp("chunk_exps", 3), gp("sum_rows", 4),
                                                        gp("differences", 4), gp("decays", 4), gp("decays_masked", 4))
    gd_sq, gd_ss, gd_ssx, gd_r = gp("squares", 2), gp("square_sums", 2), gp("square_sums_set", 2), gp("norms", 2)
    gd_kt, gd_kc, gd_vt, gd_vc = gp("k_turned", 4), gp("k_copied", 4), gp("v_turned", 4), gp("v_scaled", 4)
    gd_kb, gd_kbt, gd_kbc = gp("beta_k", 4), gp("beta_k_turned", 4), gp("beta_k_copied", 4)
    gd_a, gd_as, gd_at, gd_ats = gp("a_product", 4), gp("a_set", 4), gp("attn_product", 4), gp("attn_set", 4)
    gd_kbe, gd_kst = gp("beta_k_decayed", 4), gp("state_keys", 4)
    inv_y, inv_ys, inv_z, inv_t = (gp("inverse_right", 4 * LEVELS), gp("inverse_right_set", 4 * LEVELS),
                                   gp("inverse_both", 4 * LEVELS), gp("inverse_set", 4 * LEVELS))
    gd_val, gd_vals, gd_kcd, gd_kcds = gp("values", 4), gp("values_set", 4), gp("state_reads", 4), gp("state_reads_set", 4)
    gd_p1, gd_vn, gd_p2, gd_S = gp("read_of_state", 3), gp("new_values", 3), gp("state_gain", 3), gp("state", 3)
    gd_o1, gd_o1t, gd_o2, gd_o2t = gp("state_output", 3), gp("state_output_taken", 3), gp("chunk_output", 2), gp("chunk_output_taken", 2)

    UNITS = [(t, half) for t in range(TT) for half in range(2)]

    def gdn_parameters(load, i):
        j = i // 3
        load(levels[:], w["const_levels"].rearrange("p (v s) -> p v s", s=P))
        load(conv_rows, w["gdn_conv_2"][j].rearrange("j (f c) -> (j f) c", c=P))
        load(g_gain, w["gdn_norm_g_2"][j:j + 1, :].to_broadcast([P, P]))
        load(a_log, w["gdn_a_log_2"][j:j + 1, :].to_broadcast([P, HN]))
        load(dt_b, w["gdn_dt_bias_2"][j:j + 1, :].to_broadcast([P, HN]))

    def gdn_pool(pool, i):
        j = i // 3
        for a in range(2):
            pool.wait_ge(gd_ssx.sem, gd_ssx.count(j, a))
            flat = small[:, 432 + 16 * a:448 + 16 * a]
            nc.gpsimd.tensor_tensor(flat, flat, mhalf[:, 0:16], ALU.pow).then_inc(gd_r.sem, 1)

    def gdn_tensor(pe, i):
        j, n0 = i // 3, start["in", i]
        wait_params(pe, i)
        nc.tensor.transpose(ps[:, 7, 0:96], conv_rows, ident[0:96, 0:96]).then_inc(gd_cwT.sem, 1)
        upto, after = consts[:, c_at["upto"]], consts[:, c_at["after"]]
        for m in range(1, 17):
            if m >= 4:
                s, e = (gd_conv, m - 4) if m - 3 <= 12 else (gd_z, m - 16)
                pe.wait_ge(s.sem, s.count(j, e))
            if m == 2:
                tokens_product(pe, n0 + 1, 3, GDN_AB)
            if m in (9, 12):
                a, sqT = (0, g_kbT) if m == 9 else (1, ws[7].rearrange("p (f s) -> p f s", s=SEQ))
                pe.wait_ge(gd_sq.sem, gd_sq.count(j, a))
                pe.wait_ge(gd_D.sem, gd_D.count(j, 3))
                if a:
                    pe.wait_ge(gd_ssx.sem, gd_ssx.count(j, 0))
                for t in range(TT):
                    for h in range(HN):
                        e = 64 + 16 * a + 8 * t + h
                        last = nc.tensor.matmul(ps[:, 3, e:e + 1], sqT[:, h, t * P:(t + 1) * P], ones[:], start=True, stop=True)
                last.then_inc(gd_ss.sem, 1)
            if m == 12:
                for u, (t, half) in enumerate(UNITS):
                    for q in range(4):
                        last = nc.tensor.transpose(ps[:, 4 + u, q * P:(q + 1) * P], g_kT[:, 4 * half + q, t * P:(t + 1) * P], ident)
                    last.then_inc(gd_kt.sem, 1)
            if m == 15:
                pe.wait_ge(gd_silu.sem, gd_silu.count(j, 11))
                for u, (t, half) in enumerate(UNITS):
                    pe.wait_ge(gd_kc.sem, gd_kc.count(j, u))
                    for q in range(4):
                        last = nc.tensor.transpose(ps[:, 4 + u, q * P:(q + 1) * P], g_vT[:, 4 * half + q, t * P:(t + 1) * P], ident)
                    last.then_inc(gd_vt.sem, 1)
            if m == 16:
                pe.wait_ge(gd_kb.sem, gd_kb.count(j, 3))
                pe.wait_ge(gd_vc.sem, gd_vc.count(j, 3))
                for b in range(4):
                    for a in range(2):
                        for t in range(TT):
                            last = nc.tensor.transpose(ps[:, 4 + b, a * SEQ + t * P:a * SEQ + (t + 1) * P], g_kb[:, t, 2 * b + a, :], ident)
                    last.then_inc(gd_kbt.sem, 1)
            if m <= 12:
                features_product(pe, gated(n0, m), (m - 1) % 3)
            else:
                tokens_product(pe, n0 + m, (m - 1) % 3)
            if m == 3:
                pe.wait_ge(gd_g.sem, gd_g.count(j, 0))
                pe.wait_ge(gd_tb.sem, gd_tb.count(j, 0))
                for t in range(TT):
                    nc.tensor.matmul(ps[:, 3, 8 * t:8 * t + 8], upto, g_g[:, t, :], start=True, stop=True)
                    nc.tensor.matmul(ps[:, 3, 16 + 8 * t:24 + 8 * t], after, g_g[:, t, :], start=True, stop=True)
                    for c in range(2):
                        e = 32 + 8 * (2 * t + c)
                        last = nc.tensor.matmul(ps[:, 3, e:e + 8], upto[:, 64 * c + 63:64 * c + 64].to_broadcast([P, P]),
                                                g_g[:, t, :], start=True, stop=True)
                last.then_inc(gd_sums.sem, 1)
                pe.wait_ge(gd_cw.sem, gd_cw.count(j, 0))
                for u, (t, half) in enumerate(UNITS):
                    for q in range(4):
                        h = 4 * half + q
                        last = nc.tensor.matmul(ps[:, 4 + u, q * P:(q + 1) * P], g_g[:, t, h:h + 1].to_broadcast([P, P]), upto,
                                                start=True, stop=True)
                    last.then_inc(gd_rows.sem, 1)
        pe.wait_ge(gd_kbc.sem, gd_kbc.count(j, 3))
        for u, (t, half) in enumerate(UNITS):
            s = slice(t * P, (t + 1) * P)
            for q in range(4):
                h = 4 * half + q
                last = nc.tensor.matmul(ps[:, 4 + u, q * P:(q + 1) * P], g_kT[:, h, s], g_kbT[:, h, s], start=True, stop=True)
            last.then_inc(gd_a.sem, 1)
        pe.wait_ge(gd_z.sem, gd_z.count(j, 3))
        for u, (t, half) in enumerate(UNITS):
            s = slice(t * P, (t + 1) * P)
            for q in range(4):
                h = 4 * half + q
                last = nc.tensor.matmul(ps[:, u, q * P:(q + 1) * P], g_kT[:, h, s], g_qT[:, h, s], start=True, stop=True)
            last.then_inc(gd_at.sem, 1)
        for v in range(LEVELS):
            for u, (t, half) in enumerate(UNITS):
                if v:
                    pe.wait_ge(inv_t.sem, inv_t.count(j, 4 * (v - 1) + u))
                else:
                    pe.wait_ge(gd_ats.sem, gd_ats.count(j, u))
                for q in range(4):
                    h = 4 * half + q
                    last = nc.tensor.matmul(ps[:, u, q * P:(q + 1) * P], g_A[:, t, h, :], g_T[:, t, h, :] if v else ident,
                                            start=True, stop=True)
                last.then_inc(inv_y.sem, 1)
            for u, (t, half) in enumerate(UNITS):
                pe.wait_ge(inv_ys.sem, inv_ys.count(j, 4 * v + u))
                for q in range(4):
                    h = 4 * half + q
                    if 0 < v < LEVELS - 1:
                        nc.tensor.matmul(ps[:, u, q * P:(q + 1) * P], g_TT[:, t, h, :], g_Y[:, t, h, :], start=True, stop=True)
                    last = nc.tensor.matmul(ps[:, 4 + u, q * P:(q + 1) * P], g_Y[:, t, h, :], g_TT[:, t, h, :] if v else ident,
                                            start=True, stop=True)
                last.then_inc(inv_z.sem, 1)
        for u, (t, half) in enumerate(UNITS):
            pe.wait_ge(inv_t.sem, inv_t.count(j, 4 * (LEVELS - 1) + u))
            pe.wait_ge(gd_kbe.sem, gd_kbe.count(j, 3))
            for q in range(4):
                h = 4 * half + q
                last = nc.tensor.matmul(ps[:, u, q * P:(q + 1) * P], g_TT[:, t, h, :], g_v[:, t, h, :], start=True, stop=True)
            last.then_inc(gd_val.sem, 1)
            for q in range(4):
                h = 4 * half + q
                last = nc.tensor.matmul(ps[:, 4 + u, q * P:(q + 1) * P], g_kb[:, t, h, :], g_TT[:, t, h, :], start=True, stop=True)
            last.then_inc(gd_kcd.sem, 1)
        pe.wait_ge(gd_vals.sem, gd_vals.count(j, 3))
        pe.wait_ge(gd_kcds.sem, gd_kcds.count(j, 3))
        pe.wait_ge(gd_kst.sem, gd_kst.count(j, 3))

        def bank_of(b, h):
            return ps[:, b + h // 4, (h % 4) * P:(h % 4 + 1) * P]

        for c in range(4):
            t, r, s = c // 2, slice(64 * (c % 2), 64 * (c % 2) + 64), slice(64 * c, 64 * c + 64)
            if c:
                S = g_S2[:, c % 2, :]
                pe.wait_ge(gd_S.sem, gd_S.count(j, c - 1))
                for h in range(HN):
                    last = nc.tensor.matmul(bank_of(0, h)[r, :], g_kcdT[:, t, h, r], S[:, h * P:(h + 1) * P], start=True, stop=True)
                last.then_inc(gd_p1.sem, 1)
                if c > 1:
                    pe.wait_ge(gd_o1t.sem, gd_o1t.count(j, c - 2))
                for h in range(HN):
                    last = nc.tensor.matmul(bank_of(2, h)[r, :], g_qT[:, h, s], S[:, h * P:(h + 1) * P], start=True, stop=True)
                last.then_inc(gd_o1.sem, 1)
                pe.wait_ge(gd_vn.sem, gd_vn.count(j, c - 1))
            if c < 3:
                for h in range(HN):
                    last = nc.tensor.matmul(bank_of(4, h), g_k[r, t, h, :], g_value[r, t, h, :], start=True, stop=True)
                last.then_inc(gd_p2.sem, 1)
            if c % 2:
                if t:
                    pe.wait_ge(gd_o2t.sem, gd_o2t.count(j, 0))
                for h in range(HN):
                    last = nc.tensor.matmul(bank_of(6, h), g_dec[:, t, h, :], g_value[:, t, h, :], start=True, stop=True)
                last.then_inc(gd_o2.sem, 1)

    def conv_dst(m):
        buf = (g_qT, g_kT, g_vT)[(m - 1) // 4]
        f = 2 * ((m - 1) % 4)
        return buf[:, f:f + 2, :]

    def gdn_scalar(act, i, ch):
        j, n0 = i // 3, start["in", i]
        wait_params(act, i)

        activated_at = {6: (1, 2), 7: (3, 4), 8: (5, 6), 9: (7, 8), 10: (9,), 11: (10,), 12: (11,), 13: (12,)}

        def activate(m):
            act.wait_ge(gd_conv.sem, gd_conv.count(j, m - 1))
            nc.scalar.activation(conv_dst(m), conv_dst(m), ACT.Silu).then_inc(gd_silu.sem, 1)

        act.wait_ge(gd_cw.sem, gd_cw.count(j, 0))
        for m in range(1, 17):
            split_high(act, gated(n0, m) + 3)
            act.wait_ge(weights_used, gated(n0, m) + 1)
            b = (m - 1) % 3
            if m <= 12:
                for a in range(2):
                    f = 2 * (m - 1) + a
                    last = nc.scalar.activation(conv_dst(m)[:, a, :], ps[:, b, a * SEQ:(a + 1) * SEQ], ACT.Copy,
                                                scale=conv_w[:, 3, f:f + 1])
                last.then_inc(gd_tap0.sem, 1)
            else:
                c = slice(2 * (m - 13), 2 * (m - 12))
                nc.scalar.activation(g_z[:, :, c, :], ps[:, b, :].rearrange("p (t h v) -> p t h v", t=TT, v=P), ACT.Silu).then_inc(gd_z.sem, 1)
            if m == 1:
                split_high(act, n0 + 4)
                act.wait_ge(gd_u.sem, gd_u.count(j, 0))
                nc.scalar.activation(g_beta[:], ps[:, 3, :].rearrange("p (t c) -> p t c", t=TT)[:, :, 8:16], ACT.Tanh, scale=0.5).then_inc(gd_tb.sem, 1)
                ch.link(nc.scalar.activation(g_ea, a_log, ACT.Exp))
                ch.link(nc.scalar.activation(g_ln[:], g_g[:], ACT.Abs))
                ch.link(nc.scalar.activation(g_ln[:], g_ln[:], ACT.Exp, scale=-1.0))
                nc.scalar.activation(g_ln[:], g_ln[:], ACT.Ln, bias=1.0).then_inc(gd_lnset.sem, 1)
            if m == 3:
                act.wait_ge(gd_sums.sem, gd_sums.count(j, 0))
                for k, (dst, c) in enumerate(((g_eg, 0), (g_es, 16))):
                    nc.scalar.activation(dst[:], ps[:, 3, c:c + 16].rearrange("p (t h) -> p t h", h=HN), ACT.Exp).then_inc(gd_sexp.sem, 1)
                nc.scalar.activation(g_el[:], ps[:, 3, 32:64].rearrange("p (c h) -> p c h", h=HN), ACT.Exp).then_inc(gd_sexp.sem, 1)
            if m == 6:
                for u, (t, half) in enumerate(UNITS):
                    act.wait_ge(gd_D.sem, gd_D.count(j, u))
                    d = g_dec[:, t, 4 * half:4 * half + 4, :]
                    nc.scalar.activation(d, d, ACT.Exp).then_inc(gd_Dexp.sem, 1)
            for f in activated_at.get(m, ()):
                activate(f)
            if m in (7, 10):
                src, dst = ((ws[0], ws[8]), (ws[1], ws[7]))[m == 10]
                act.wait_ge(gd_silu.sem, gd_silu.count(j, 3 if m == 7 else 7))
                nc.scalar.activation(dst[:], src[:], ACT.Square).then_inc(gd_sq.sem, 1)
            if m == 12:
                for u, (t, half) in enumerate(UNITS):
                    act.wait_ge(gd_kt.sem, gd_kt.count(j, u))
                    nc.scalar.copy(g_k[:, t, 4 * half:4 * half + 4, :], ps[:, 4 + u, :].rearrange("p (h v) -> p h v", v=P)).then_inc(gd_kc.sem, 1)
            if m == 15:
                for b in range(4):
                    act.wait_ge(gd_kbt.sem, gd_kbt.count(j, b))
                    nc.scalar.copy(g_kbT[:, 2 * b:2 * b + 2, :], ps[:, 4 + b, :].rearrange("p (a s) -> p a s", a=2)).then_inc(gd_kbc.sem, 1)
        for u, (t, half) in enumerate(UNITS):
            act.wait_ge(gd_val.sem, gd_val.count(j, u))
            nc.scalar.copy(g_value[:, t, 4 * half:4 * half + 4, :], ps[:, u, :].rearrange("p (h v) -> p h v", v=P)).then_inc(gd_vals.sem, 1)
        for t in range(TT):
            act.wait_ge(gd_o2t.sem, gd_o2t.count(j, t))
            head_norm_scalar(act, i, t)

    def gdn_vector(dve, i, ch):
        j, n0 = i // 3, start["in", i]
        upto = consts[:, c_at["upto"]]
        four = lambda s: s.unsqueeze(2).to_broadcast([P, 4, P])
        eight = lambda s, n=P: s.unsqueeze(2).to_broadcast([n, HN, P])
        rq, rk = g_r[:, 0, :, :], g_r[:, 1, :, :]
        wait_params(dve, i)
        dve.wait_ge(gd_cwT.sem, gd_cwT.count(j, 0))
        nc.vector.tensor_copy(conv_w[:], ps[:, 7, 0:96].rearrange("p (j f) -> p j f", j=4)).then_inc(gd_cw.sem, 1)
        dve.wait_ge(gd_cw.sem, gd_cw.count(j, 0))
        for m in range(1, 17):
            split_low(dve, gated(n0, m) + 3)
            b = (m - 1) % 3
            if m <= 12:
                dve.wait_ge(gd_tap0.sem, gd_tap0.count(j, m - 1))
                for s in range(1, 4):
                    for a in range(2):
                        f, d = 2 * (m - 1) + a, conv_dst(m)[:, a, s:SEQ]
                        last = nc.vector.scalar_tensor_tensor(out=d, in0=ps[:, b, a * SEQ:(a + 1) * SEQ - s],
                                                              scalar=conv_w[:, 3 - s, f:f + 1], in1=d, op0=ALU.mult, op1=ALU.add)
                        if not (s == 3 and a == 1):
                            ch.mark(last)
                    if s < 3:
                        ch.wait()
                last.then_inc(gd_conv.sem, 1)
            if m == 1:
                split_low(dve, n0 + 4)
                dve.wait_ge(weights_used, n0 + 2)
                nc.vector.tensor_tensor(g_g[:], ps[:, 3, :].rearrange("p (t c) -> p t c", t=TT)[:, :, 0:8],
                                        dt_b.unsqueeze(1).to_broadcast([P, TT, HN]), ALU.add).then_inc(gd_u.sem, 1)
                dve.wait_ge(gd_lnset.sem, gd_lnset.count(j, 0))
                ch.link(nc.vector.scalar_tensor_tensor(out=g_g[:], in0=g_g[:], scalar=0.0, in1=g_ln[:], op0=ALU.max, op1=ALU.add))
                nc.vector.scalar_tensor_tensor(out=g_g[:], in0=g_g[:], scalar=-1.0, in1=g_ea.unsqueeze(1).to_broadcast([P, TT, HN]),
                                               op0=ALU.mult, op1=ALU.mult).then_inc(gd_g.sem, 1)
                dve.wait_ge(gd_tb.sem, gd_tb.count(j, 0))
                ch.link(nc.vector.tensor_scalar(g_beta[:], g_beta[:], 0.5, 0.5, ALU.mult, ALU.add))
            if m == 4:
                dve.wait_ge(gd_sexp.sem, gd_sexp.count(j, 2))
                ch.link(nc.vector.tensor_copy(g_gc[:], ps[:, 3, 0:16].rearrange("p (t h) -> p t h", h=HN)))
            if m in (4, 5):
                for u, (t, half) in list(enumerate(UNITS))[2 * m - 8:2 * m - 6]:
                    dve.wait_ge(gd_rows.sem, gd_rows.count(j, u))
                    for q in range(4):
                        h = 4 * half + q
                        last = nc.vector.tensor_scalar(g_dec[:, t, h, :], ps[:, 4 + u, q * P:(q + 1) * P], g_gc[:, t, h:h + 1],
                                                       0.0, ALU.subtract, ALU.min)
                    last.then_inc(gd_D.sem, 1)
            if m in (9, 12):
                a = m // 12
                dve.wait_ge(gd_ss.sem, gd_ss.count(j, a))
                nc.vector.tensor_scalar(small[:, 432 + 16 * a:448 + 16 * a], ps[:, 3, 64 + 16 * a:80 + 16 * a], RMS_EPS, None,
                                        ALU.add).then_inc(gd_ssx.sem, 1)
            if m == 13:
                dve.wait_ge(gd_r.sem, gd_r.count(j, 1))
                ch.mark(nc.vector.tensor_scalar(rq, rq, float(P) ** -0.5, None, ALU.mult))
                ch.mark(nc.vector.tensor_tensor(g_brk[:], g_beta[:], rk, ALU.mult))
                ch.mark(nc.vector.tensor_tensor(g_rkes[:], g_es[:], rk, ALU.mult))
                ch.wait()
                for u, (t, half) in enumerate(UNITS):
                    hs = slice(4 * half, 4 * half + 4)
                    dve.wait_ge(gd_kc.sem, gd_kc.count(j, u))
                    nc.vector.tensor_tensor(g_kb[:, t, hs, :], g_k[:, t, hs, :], four(g_brk[:, t, hs]), ALU.mult).then_inc(gd_kb.sem, 1)
            if m == 14:
                for u, (t, half) in enumerate(UNITS):
                    hs = slice(4 * half, 4 * half + 4)
                    dve.wait_ge(gd_vt.sem, gd_vt.count(j, u))
                    nc.vector.tensor_tensor(g_v[:, t, hs, :], ps[:, 4 + u, :].rearrange("p (h v) -> p h v", v=P), four(g_beta[:, t, hs]),
                                            ALU.mult).then_inc(gd_vc.sem, 1)
            if m == 15:
                for u, (t, half) in enumerate(UNITS):
                    dve.wait_ge(gd_Dexp.sem, gd_Dexp.count(j, u))
                    for q in range(4):
                        h = 4 * half + q
                        last = nc.vector.scalar_tensor_tensor(out=g_dec[:, t, h, :], in0=g_dec[:, t, h, :], scalar=rk[:, t, h:h + 1],
                                                              in1=upto, op0=ALU.mult, op1=ALU.mult)
                    last.then_inc(gd_dec.sem, 1)
        for u, (t, half) in enumerate(UNITS):
            hs = slice(4 * half, 4 * half + 4)
            dve.wait_ge(gd_dec.sem, gd_dec.count(j, u))
            dve.wait_ge(gd_a.sem, gd_a.count(j, u))
            nc.vector.tensor_tensor(g_A[:, t, hs, :], ps[:, 4 + u, :].rearrange("p (h v) -> p h v", v=P), g_dec[:, t, hs, :],
                                    ALU.mult).then_inc(gd_as.sem, 1)
        for u, (t, half) in enumerate(UNITS):
            hs = slice(4 * half, 4 * half + 4)
            dve.wait_ge(gd_at.sem, gd_at.count(j, u))
            if u == 0:
                dve.wait_ge(gd_as.sem, gd_as.count(j, 3))
            nc.vector.tensor_tensor(g_dec[:, t, hs, :], ps[:, u, :].rearrange("p (h v) -> p h v", v=P), g_dec[:, t, hs, :],
                                    ALU.mult).then_inc(gd_ats.sem, 1)
        bc = lambda m: m.unsqueeze(1).to_broadcast([P, 4, P])
        for v in range(LEVELS):
            for u, (t, half) in enumerate(UNITS):
                hs = slice(4 * half, 4 * half + 4)
                dve.wait_ge(inv_y.sem, inv_y.count(j, 4 * v + u))
                nc.vector.tensor_tensor(g_Y[:, t, hs, :], ps[:, u, :].rearrange("p (h v) -> p h v", v=P), bc(levels[:, v, :]),
                                        ALU.mult).then_inc(inv_ys.sem, 1)
                if v == 0:
                    nc.vector.tensor_tensor(g_kb[:, t, hs, :], g_kb[:, t, hs, :], four(g_eg[:, t, hs]), ALU.mult).then_inc(gd_kbe.sem, 1)
                    nc.vector.tensor_tensor(g_k[:, t, hs, :], g_k[:, t, hs, :], four(g_rkes[:, t, hs]), ALU.mult).then_inc(gd_kst.sem, 1)
            for u, (t, half) in enumerate(UNITS):
                hs = slice(4 * half, 4 * half + 4)
                if v == 0:
                    dve.wait_ge(inv_ys.sem, inv_ys.count(j, u))
                    ch.mark(nc.vector.tensor_tensor(g_T[:, t, hs, :], bc(ident), g_Y[:, t, hs, :], ALU.subtract))
                dve.wait_ge(inv_z.sem, inv_z.count(j, 4 * v + u))
                if 0 < v < LEVELS - 1:
                    ch.mark(nc.vector.tensor_tensor(g_T[:, t, hs, :], g_T[:, t, hs, :], ps[:, u, :].rearrange("p (h v) -> p h v", v=P),
                                                    ALU.subtract))
                nc.vector.tensor_tensor(g_TT[:, t, hs, :], g_TT[:, t, hs, :] if v else bc(ident),
                                        ps[:, 4 + u, :].rearrange("p (h v) -> p h v", v=P), ALU.subtract).then_inc(inv_t.sem, 1)
                if v < LEVELS - 1:
                    dve.wait_ge(inv_t.sem, inv_t.count(j, 4 * v + u))
            if 1 <= v <= 4:
                t, f = (v - 1) % 2, g_z[:, (v - 1) % 2, :, :]
                if v == 1:
                    dve.wait_ge(gd_z.sem, gd_z.count(j, 3))
                if v == 3:
                    ch.wait()
                nc.vector.tensor_tensor(f, f, g_gain.unsqueeze(1).to_broadcast([P, HN, P]) if v < 3 else eight(rq[:, t, :]),
                                        ALU.mult).then_inc(dve_chain, 1)
                ch.n += 1
        for u, (t, half) in enumerate(UNITS):
            hs = slice(4 * half, 4 * half + 4)
            dve.wait_ge(gd_kcd.sem, gd_kcd.count(j, u))
            nc.vector.tensor_copy(g_kcdT[:, t, hs, :], ps[:, 4 + u, :].rearrange("p (h v) -> p h v", v=P)).then_inc(gd_kcds.sem, 1)
        dve.wait_ge(gd_kcds.sem, gd_kcds.count(j, 3))
        ch.mark(nc.vector.memset(M[0:64, 0, :], 0.0))
        pair = lambda b, r=slice(0, P): ps[r, b:b + 2, :].rearrange("p b c -> p (b c)")
        dve.wait_ge(gd_sexp.sem, gd_sexp.count(j, 2))
        for c in range(4):
            t, r = c // 2, slice(64 * (c % 2), 64 * (c % 2) + 64)
            val = g_value[r, t, :, :].rearrange("p h v -> p (h v)")
            if c:
                dve.wait_ge(gd_p1.sem, gd_p1.count(j, c - 1))
                if c == 1:
                    dve.wait_ge(gd_vals.sem, gd_vals.count(j, 3))
                nc.vector.tensor_tensor(val, val, pair(0, r), ALU.subtract).then_inc(gd_vn.sem, 1)
                if c < 3:
                    m = ch.mark(nc.vector.tensor_tensor(g_Sd.rearrange("p (h v) -> p h v", v=P),
                                                        g_S2[:, c % 2, :].rearrange("p (h v) -> p h v", v=P),
                                                        eight(g_el[:, c, :]), ALU.mult))
            if c < 3:
                dve.wait_ge(gd_p2.sem, gd_p2.count(j, c))
                if c:
                    ch.wait(m)
                    nc.vector.tensor_tensor(g_S2[:, (c + 1) % 2, :], g_Sd, pair(4), ALU.add).then_inc(gd_S.sem, 1)
                else:
                    nc.vector.tensor_copy(g_S2[:, 1, :], pair(4)).then_inc(gd_S.sem, 1)
                dve.wait_ge(gd_S.sem, gd_S.count(j, c))
            if c:
                dve.wait_ge(gd_o1.sem, gd_o1.count(j, c - 1))
                nc.vector.tensor_tensor(M4[r, t, :, :], pair(2, r).rearrange("p (h v) -> p h v", v=P),
                                        eight(g_eg[r, t, :], 64), ALU.mult).then_inc(gd_o1t.sem, 1)
            if c % 2:
                dve.wait_ge(gd_o2.sem, gd_o2.count(j, t))
                dve.wait_ge(gd_o1t.sem, gd_o1t.count(j, c - 1))
                nc.vector.tensor_tensor(M[:, t, :], M[:, t, :], pair(6), ALU.add).then_inc(gd_o2t.sem, 1)
                dve.wait_ge(gd_o2t.sem, gd_o2t.count(j, t))
                ch.mark(nc.vector.tensor_tensor(g_rq2[:, t, :], rq[:, t, :], rq[:, t, :], ALU.mult))
                head_squares_vector(dve, i, ch, t, g_z[:, t, :, :], g_rq2[:, t, :])
            if c >= 2:
                head_norm_vector(dve, i, ch, c - 2)

    def order_of_stages():
        st, xp, q = [], 0, 0
        for l in range(DEPTH):
            for j in range(2):
                if j == 1:
                    st.append(("mix", l, xp))
                    xp += 0
                    st.append(("norm", q, xp + 1, (1.0, start["mix_out", l] + 3)))
                    q, xp = q + 1, xp + 1
                st.append(("ffn", l, j, xp))
                n_last = start["ffn", l, j] + 3 * FF_STEPS - 1
                final = l == DEPTH - 1 and j == 1
                st.append(("norm", q, None if final else xp + 1, (0.5, n_last)))
                q, xp = q + 1, xp + (0 if final else 1)
        q, a = 0, 0
        n_last = start["ffn", DEPTH - 1, 1] + 3 * FF_STEPS - 1
        for i in range(DEPTH_2):
            st.append(("prenorm", q, xp + 1, n_last))
            q, xp = q + 1, xp + 1
            st.append(("mixer", i, xp, xp + 1))
            xp += 1
            n_last = start["out", i] + 3
            st.append(("addnorm", a))
            a += 1
            st.append(("prenorm", q, xp + 1, n_last))
            q, xp = q + 1, xp + 1
            st.append(("mlp", i, xp))
            n_last = start["mlp", i] + 2 * MLP_STEPS - 1
            st.append(("addnorm", a))
            a += 1
        return st


    dve_steps, act_steps, pool_steps = [0], [0], [0]
    ST = order_of_stages()

    def split_two(split, eng, n_last):
        for n in (n_last + 2, n_last + 3):
            split(eng, n)

    block = ctx.enter_context(nc.Block())

    @block.sync
    def _(sp):
        sp.dma_start(x[:], w["x"][0].rearrange("(t p) d -> p t d", p=P)).then_inc(x_landed, 16)
        sp.dma_start(consts[:], w["const_main"]).then_inc(consts_landed, 16)
        for st in ST:
            if st[0] == "ffn":
                ffn_sync(sp, st[1], st[2])
            elif st[0] == "mlp":
                mlp_sync(sp, st[1])
            elif st[0] == "mix":
                for n in range(start["mix", st[1]], start["mix_out", st[1]] + 4):
                    load_chunk(sp, n)
            elif st[0] == "mixer":
                mixer_sync(sp, st[1])
        sp.wait_ge(add_done.sem, add_done.count(2 * DEPTH_2 - 1, TT - 1))
        sp.dma_start(out[0].rearrange("(t p) d -> p t d", p=P), x[:]).then_inc(out_stored, 16)
        sp.wait_ge(out_stored, 16)

    @block.gpsimd
    def _(pool):
        nc.gpsimd.memset(mhalf, -0.5).then_inc(pool_chain, 1)
        nc.gpsimd.memset(eps_d, D * RMS_EPS).then_inc(pool_chain, 1)
        pool.wait_ge(pool_chain, 2)
        pool_steps[0] = 2
        for st in ST:
            if st[0] == "norm":
                norm_pool(pool, st[1])
            elif st[0] == "mix":
                mix_pool(pool, st[1])
            elif st[0] == "prenorm":
                prenorm_pool(pool, st[1])
            elif st[0] == "addnorm":
                addnorm_pool(pool, st[1])
            elif st[0] == "mixer":
                mixer_pool(pool, st[1])

    @block.scalar
    def _(act):
        turn_scalar(act, 0)
        for n in range(SPLIT):
            split_high(act, n)
        for st in ST:
            if st[0] == "ffn":
                ffn_scalar(act, st[1], st[2])
            elif st[0] == "norm":
                if st[2] is not None:
                    turn_scalar(act, st[2])
                    split_two(split_high, act, st[3][1])
            elif st[0] == "mix":
                mix_scalar(act, st[1])
            elif st[0] == "prenorm":
                prenorm_scalar(act, st[1])
                turn_scalar(act, st[2])
                split_two(split_high, act, st[3])
            elif st[0] == "addnorm":
                addnorm_scalar(act, st[1])
            elif st[0] == "mlp":
                mlp_scalar(act, st[1])
            elif st[0] == "mixer":
                mixer_scalar(act, st[1], st[3])

    @block.vector
    def _(dve):
        nc.vector.memset(ones[:], 1.0)
        nc.vector.memset(zrow[:], 0.0).then_inc(zrow_set, 1)
        turn_vector(dve, 0)
        for n in range(SPLIT):
            split_low(dve, n)
        for st in ST:
            if st[0] == "ffn":
                ffn_vector(dve, st[1], st[2])
            elif st[0] == "norm":
                scale, n_last = st[3]
                norm_vector(dve, st[1], scale, n_last)
                if st[2] is not None:
                    turn_vector(dve, st[2])
                    split_two(split_low, dve, n_last)
            elif st[0] == "mix":
                mix_vector(dve, st[1])
            elif st[0] == "prenorm":
                prenorm_vector(dve, st[1])
                turn_vector(dve, st[2])
                split_two(split_low, dve, st[3])
            elif st[0] == "addnorm":
                addnorm_vector(dve, st[1])
            elif st[0] == "mlp":
                mlp_vector(dve, st[1])
            elif st[0] == "mixer":
                mixer_vector(dve, st[1], st[3])

    @block.tensor
    def _(pe):
        pe.wait_ge(zrow_set, 1)
        pe.wait_ge(consts_landed, 16)
        pe.wait_ge(x_landed, 16)
        turn_tensor(pe, 0, x, lambda pe, t: None)
        for st in ST:
            if st[0] == "ffn":
                ffn_tensor(pe, st[1], st[2], st[3])
            elif st[0] == "norm":
                if st[2] is not None:
                    turn_tensor(pe, st[2], x, norm_done(st[1]))
            elif st[0] == "mix":
                mix_tensor(pe, st[1], st[2])
            elif st[0] == "prenorm":
                turn_tensor(pe, st[2], H, prenorm_is_done(st[1]), scaled=True)
            elif st[0] == "mlp":
                mlp_tensor(pe, st[1], st[2])
            elif st[0] == "mixer":
                mixer_tensor(pe, st[1], st[2], st[3])

    ctx.close()


_INS = [
    "x", "ln_g", "ln_b", "ffn_wg", "ffn_wu", "ffn_wd", "w_in", "w_out", "cmp_pe", "cmp_w1", "cmp_w2", "pool_w",
    "pool_scale", "gla_wa2", "gla_ba", "gla_norm_g", "norm_g_2", "mlp_w1_2", "mlp_w2_2", "gdn_w_in_2",
    "gdn_conv_2", "gdn_a_log_2", "gdn_dt_bias_2", "gdn_norm_g_2", "gdn_w_out_2", "mlstm_w_in_2",
    "mlstm_gate_b_2", "mlstm_norm_g_2", "mlstm_w_out_2", "diff_w_in_2", "diff_lambda_2", "diff_norm_g_2",
    "diff_w_out_2",
]


def kernel(**inputs):
    import numpy as _np
    import concourse.bacc as _bacc
    from concourse.bass_utils import run_bass_kernel_spmd as _run

    nc = _bacc.Bacc("TRN2", target_bir_lowering=False, num_devices=1)
    arrays, w = {}, {}
    for name in _INS:
        arrays[f"in_{name}"] = _np.ascontiguousarray(inputs[name])
    arrays.update(shape_constants())
    for name, a in arrays.items():
        w[name.removeprefix("in_")] = nc.dram_tensor(name, a.shape, F32, kind="ExternalInput").ap()
    out = nc.dram_tensor("out_0", (1, SEQ, D), F32, kind="ExternalOutput").ap()
    two_block_model(nc, w, out)
    r = _run(nc, [arrays], core_ids=[0])
    return r.results[0]["out_0"]
```
